# Optimizing a Trainium2 kernel written in Bass

```python
import jax, jax.numpy as jnp
from jax import lax
import numpy as np

D_MODEL = 1024
BATCH = 1
SEQ = 256
DEPTH = 2

CHUNK = 64
N_A_LAYERS = DEPTH // 2
N_B_LAYERS = DEPTH - N_A_LAYERS
A_HEADS = 8
A_HEAD_DIM = D_MODEL // A_HEADS
B_HEADS = 16
B_HEAD_DIM = D_MODEL // B_HEADS
LEFT_CHUNKS = 8
BAND = (LEFT_CHUNKS + 1) * CHUNK
REL_MIN = -(CHUNK - 1)
REL_MAX = 256
N_REL = REL_MAX - REL_MIN + 1
ATTN_SCALE = B_HEAD_DIM ** -0.5
N_GROUPS = 4
EXPERTS_PER_GROUP = 8
N_EXPERTS = N_GROUPS * EXPERTS_PER_GROUP
TOP_K = 2
D_EXPERT = 512
MOE_BLOCK = 256
D_PLE = 256
EPS = 1e-6
NEG_INF = -1e30

kernel_name = "yoco_hgrn2_chunkattn_hiermoe"

def rmsnorm(x, g):
    xf = x.astype(jnp.float32)
    y = xf * lax.rsqrt(jnp.mean(xf * xf, axis=-1, keepdims=True) + EPS)
    return (y * g.astype(jnp.float32)).astype(x.dtype)

def hgrn2_mixer(h, lb, w_in, out_norm):
    f32 = jnp.float32
    B_, S_, _ = h.shape
    n_c = S_ // CHUNK
    proj = h @ w_in
    q, f_logit, i_val, og = jnp.split(proj, 4, axis=-1)
    f = lb + (1.0 - lb) * jax.nn.sigmoid(f_logit.astype(f32))
    k = 1.0 - f

    def heads(t):
        return t.reshape(B_, n_c, CHUNK, A_HEADS, A_HEAD_DIM).transpose(1, 0, 3, 2, 4)

    qc, kc, vc = heads(q.astype(f32)), heads(k), heads(i_val.astype(f32))
    g = jnp.cumsum(heads(jnp.log(f)), axis=3)
    g_last = g[:, :, :, -1:, :]
    q_dec = qc * jnp.exp(g)
    k_inv = kc * jnp.exp(-g)
    k_tail = kc * jnp.exp(g_last - g)
    causal = jnp.tril(jnp.ones((CHUNK, CHUNK), dtype=bool))
    att = jnp.where(causal, jnp.einsum('nbhtd,nbhsd->nbhts', q_dec, k_inv), 0.0)
    o_intra = jnp.einsum('nbhts,nbhse->nbhte', att, vc)

    def step(state, xs):
        qd, kt, v, dl = xs
        o = jnp.einsum('bhtd,bhde->bhte', qd, state)
        state = state * dl[:, :, 0, :, None] + jnp.einsum('bhsd,bhse->bhde', kt, v)
        return state, o

    s0 = jnp.zeros((B_, A_HEADS, A_HEAD_DIM, A_HEAD_DIM), f32)
    _, o_inter = lax.scan(step, s0, (q_dec, k_tail, vc, jnp.exp(g_last)))
    o = o_intra + o_inter
    o = o * lax.rsqrt(jnp.mean(o * o, axis=-1, keepdims=True) + EPS)
    o = o.transpose(1, 0, 3, 2, 4).reshape(B_, S_, D_MODEL) * out_norm.astype(f32)
    o = o * jax.nn.silu(og.astype(f32))
    return o.astype(h.dtype)

def chunk_attention(h, w_q, rel_bias, k_pad, v_pad):
    B_, S_, _ = h.shape
    n_c = S_ // CHUNK
    q = (h @ w_q).reshape(B_, S_, B_HEADS, B_HEAD_DIM)
    q_pos = jnp.arange(CHUNK)[:, None]
    k_pos = jnp.arange(BAND)[None, :] - LEFT_CHUNKS * CHUNK
    rel = jnp.clip(q_pos - k_pos, REL_MIN, REL_MAX) - REL_MIN
    bias = rel_bias[:, rel].astype(jnp.float32)
    band_idx = jnp.arange(BAND)

    def one_chunk(c):
        start = c * CHUNK
        qc = lax.dynamic_slice_in_dim(q, start, CHUNK, axis=1)
        kb = lax.dynamic_slice_in_dim(k_pad, start, BAND, axis=1)
        vb = lax.dynamic_slice_in_dim(v_pad, start, BAND, axis=1)
        s = jnp.einsum('bqhd,bkhd->bhqk', qc, kb).astype(jnp.float32) * ATTN_SCALE + bias
        valid = (start - LEFT_CHUNKS * CHUNK + band_idx) >= 0
        s = jnp.where(valid, s, NEG_INF)
        w = jax.nn.softmax(s, axis=-1).astype(vb.dtype)
        return jnp.einsum('bhqk,bkhd->bqhd', w, vb)

    o = lax.map(one_chunk, jnp.arange(n_c))
    return o.transpose(1, 0, 2, 3, 4).reshape(B_, S_, D_MODEL)

def hier_moe(h, w_group, b_group, w_expert, b_expert, w_gate, w_up, w_down):
    f32 = jnp.float32
    B_, S_, D_ = h.shape
    t = h.reshape(-1, D_)
    T = t.shape[0]
    grp_prob = jax.nn.softmax((t @ w_group).astype(f32) + b_group.astype(f32), axis=-1)
    grp_w, grp_idx = lax.top_k(grp_prob, 1)
    e_logits = ((t @ w_expert).astype(f32) + b_expert.astype(f32)).reshape(T, N_GROUPS, EXPERTS_PER_GROUP)
    e_logits = jnp.take_along_axis(e_logits, grp_idx[:, :, None], axis=1)[:, 0]
    top_logit, top_i = lax.top_k(e_logits, TOP_K)
    gate = grp_w * jax.nn.softmax(top_logit, axis=-1)
    expert = grp_idx * EXPERTS_PER_GROUP + top_i

    n_slots = T * TOP_K
    flat_e = expert.reshape(-1)
    order = jnp.argsort(flat_e)
    e_sorted = flat_e[order]
    tok_sorted = (order // TOP_K).astype(jnp.int32)
    w_sorted = gate.reshape(-1)[order]
    counts = jnp.bincount(flat_e, length=N_EXPERTS)
    padded = (counts + MOE_BLOCK - 1) // MOE_BLOCK * MOE_BLOCK
    pad_end = jnp.cumsum(padded)
    pad_start = pad_end - padded
    seg_start = jnp.cumsum(counts) - counts
    dest = pad_start[e_sorted] + jnp.arange(n_slots) - seg_start[e_sorted]
    n_blocks = -(-n_slots // MOE_BLOCK) + N_EXPERTS
    n_pad = n_blocks * MOE_BLOCK
    buf_tok = jnp.zeros((n_pad,), jnp.int32).at[dest].set(tok_sorted)
    buf_w = jnp.zeros((n_pad,), f32).at[dest].set(w_sorted)
    block_e = jnp.minimum(
        jnp.searchsorted(pad_end, jnp.arange(n_blocks) * MOE_BLOCK, side='right'), N_EXPERTS - 1)

    def expert_block(args):
        tok, e = args
        xb = t[tok]
        hid = jax.nn.silu(xb @ w_gate[e]) * (xb @ w_up[e])
        return hid @ w_down[e]

    y = lax.map(expert_block, (buf_tok.reshape(n_blocks, MOE_BLOCK), block_e))
    y = y.reshape(n_pad, D_) * buf_w[:, None].astype(y.dtype)
    out = jnp.zeros_like(t).at[buf_tok].add(y)
    return out.reshape(B_, S_, D_)

def setup_inputs(seed: int = 0) -> dict:
    key = jax.random.key(seed)
    ks = jax.random.split(key, 24)
    f32 = jnp.float32
    D, F, E, G = D_MODEL, D_EXPERT, N_EXPERTS, N_GROUPS

    def nrm(k, shape, scale):
        return jax.random.normal(k, shape, f32) * scale

    def gain(k, shape):
        return 1.0 + 0.05 * jax.random.normal(k, shape, f32)

    return {
        "x": nrm(ks[0], (BATCH, SEQ, D), 1.0),
        "p": nrm(ks[1], (DEPTH, BATCH, SEQ, D_PLE), 1.0),
        "a_w_in": nrm(ks[2], (N_A_LAYERS, D, 4 * D), D ** -0.5),
        "a_lb_logits": nrm(ks[3], (N_A_LAYERS + 1, D), 0.1),
        "a_out_norm": gain(ks[4], (N_A_LAYERS, D)),
        "a_w_o": nrm(ks[5], (N_A_LAYERS, D, D), D ** -0.5),
        "kv_norm": gain(ks[6], (D,)),
        "w_kv": nrm(ks[7], (D, 2 * D), D ** -0.5),
        "b_w_q": nrm(ks[8], (N_B_LAYERS, D, D), D ** -0.5),
        "b_rel_bias": nrm(ks[9], (N_B_LAYERS, B_HEADS, N_REL), 0.5),
        "b_w_o": nrm(ks[10], (N_B_LAYERS, D, D), D ** -0.5),
        "norm_mix": gain(ks[11], (DEPTH, D)),
        "norm_ffn": gain(ks[12], (DEPTH, D)),
        "norm_ple": gain(ks[13], (DEPTH, D)),
        "moe_w_group": nrm(ks[14], (DEPTH, D, G), D ** -0.5),
        "moe_b_group": nrm(ks[15], (DEPTH, G), 0.01),
        "moe_w_expert": nrm(ks[16], (DEPTH, D, E), D ** -0.5),
        "moe_b_expert": nrm(ks[17], (DEPTH, E), 0.01),
        "moe_w_gate": nrm(ks[18], (DEPTH, E, D, F), D ** -0.5),
        "moe_w_up": nrm(ks[19], (DEPTH, E, D, F), D ** -0.5),
        "moe_w_down": nrm(ks[20], (DEPTH, E, F, D), F ** -0.5),
        "ple_w_proj": nrm(ks[21], (DEPTH, D_PLE, D), D_PLE ** -0.5),
        "ple_w_gate": nrm(ks[22], (DEPTH, D, D), D ** -0.5),
        "final_norm": gain(ks[23], (D,)),
    }

def reference(x, p, a_w_in, a_lb_logits, a_out_norm, a_w_o, kv_norm, w_kv, b_w_q,
              b_rel_bias, b_w_o, norm_mix, norm_ffn, norm_ple, moe_w_group, moe_b_group,
              moe_w_expert, moe_b_expert, moe_w_gate, moe_w_up, moe_w_down, ple_w_proj,
              ple_w_gate, final_norm):
    B_, S_, _ = x.shape
    lower_bounds = jnp.cumsum(jax.nn.softmax(a_lb_logits.astype(jnp.float32), axis=0), axis=0)
    k_pad = v_pad = None
    for i in range(DEPTH):
        if i == N_A_LAYERS:
            kv = rmsnorm(x, kv_norm) @ w_kv
            k_sh, v_sh = jnp.split(kv, 2, axis=-1)
            pad = ((0, 0), (LEFT_CHUNKS * CHUNK, 0), (0, 0), (0, 0))
            k_pad = jnp.pad(k_sh.reshape(B_, S_, B_HEADS, B_HEAD_DIM), pad)
            v_pad = jnp.pad(v_sh.reshape(B_, S_, B_HEADS, B_HEAD_DIM), pad)
        h = rmsnorm(x, norm_mix[i])
        if i < N_A_LAYERS:
            mix = hgrn2_mixer(h, lower_bounds[i], a_w_in[i], a_out_norm[i]) @ a_w_o[i]
        else:
            j = i - N_A_LAYERS
            mix = chunk_attention(h, b_w_q[j], b_rel_bias[j], k_pad, v_pad) @ b_w_o[j]
        x = x + mix
        x = x + hier_moe(rmsnorm(x, norm_ffn[i]), moe_w_group[i], moe_b_group[i],
                         moe_w_expert[i], moe_b_expert[i], moe_w_gate[i], moe_w_up[i],
                         moe_w_down[i])
        x = x + (p[i] @ ple_w_proj[i]) * jax.nn.sigmoid(rmsnorm(x, norm_ple[i]) @ ple_w_gate[i])
    return rmsnorm(x, final_norm)


_drawn_inputs = setup_inputs


def setup_inputs(seed=0):
    import zlib

    import numpy as np

    out = dict(_drawn_inputs(seed))
    spreads = {}
    factors = {'kv_norm': 3.638, 'norm_ple': 3.227, 'moe_b_group': 8.0, 'moe_b_expert': 5.076}
    for name, (base, spread) in spreads.items():
        noise = np.random.default_rng([zlib.crc32(name.encode()), seed]).standard_normal(out[name].shape)
        drawn = base * np.exp(spread * noise) if base else spread * noise
        out[name] = __import__('jax').numpy.asarray(drawn.astype(out[name].dtype))
    for name, factor in factors.items():
        out[name] = (out[name] * factor).astype(out[name].dtype)
    return out
```

```python
from contextlib import ExitStack

import concourse.bass as bass
from concourse import mybir

F32 = mybir.dt.float32
I32 = mybir.dt.int32
ALU = mybir.AluOpType
ACT = mybir.ActivationFunctionType
AX = mybir.AxisListType.X

P = 128
D = 1024
SEQ = 256
NT = SEQ // P
NC = D // P
CHUNK = 64
BANK = 512
A_HEADS = 8
HALF_A = A_HEADS // 2
B_HEADS = 16
B_DIM = D // B_HEADS
HALF_B = B_HEADS // 2
ATTN_SCALE = B_DIM ** -0.5
N_REL = 320
D_PLE = 256
GROUPS = 4
PER_GROUP = 8
EXPERTS = GROUPS * PER_GROUP
D_EXPERT = 512
ROUTES = GROUPS + EXPERTS
EPS = 1e-6
MASKED = -1e30
SLOTS = 32
BATCH_E = P // SLOTS
COLS = P // SLOTS
RING = 8
SLOT = NC * BANK
BODY_E = 8
BODY_BLOCKS = 3 * BODY_E
BODIES = EXPERTS // BODY_E
BATCHES = BODY_E // BATCH_E
MIX_A_BLOCKS, BLOCKS_B, BLOCKS_C = 10, 11, 3
MOE_AT = (MIX_A_BLOCKS % RING, (MIX_A_BLOCKS + BLOCKS_B) % RING)
(G_MIX0, G_FFN0, G_PLE0, G_KV, G_MIX1, G_FFN1, G_PLE1) = range(7)


class Count:

    def __init__(self, eng, sem, base=0):
        self.eng, self.sem, self.base, self.n = eng, sem, base, 0

    def link(self, ins):
        self.n += 1
        ins.then_inc(self.sem, 1)
        self.eng.wait_ge(self.sem, self.base + self.n)


def expert_slots(layer, e):
    s = (MOE_AT[layer] + 3 * e) % RING
    if s == RING - 1:
        return 0, 1, s
    return s, s + 1, (s + 2) % RING


def build(nc, x, p, a_w_in, a_lb_logits, a_out_norm, a_w_o, kv_norm, w_kv, b_w_q, b_rel_bias,
          b_w_o, norm_mix, norm_ffn, norm_ple, moe_w_group, moe_b_group, moe_w_expert,
          moe_b_expert, moe_w_gate, moe_w_up, moe_w_down, ple_w_proj, ple_w_gate, final_norm, out):
    ctx = ExitStack()
    with ctx:
        def sb(name, shape, dt=F32):
            return ctx.enter_context(nc.sbuf_tensor(name, shape, dt))

        def sem(name):
            return ctx.enter_context(nc.semaphore(name))

        def sems(name):
            return [sem(f"{name}{layer}") for layer in range(2)]

        ring = sb("ring", [P, RING, SLOT])
        xs = sb("xs", [P, NT, D])
        hn = sb("hn", [P, NT, NC, P])
        hT = sb("hT", [P, NC, SEQ])
        hT2 = sb("hT2", [P, NC, SEQ])
        ident = sb("ident", [P, P])
        flip = sb("flip", [P, P])
        before = sb("before", [P, P])
        ones = sb("ones", [P, P])
        causal = sb("causal", [P, P])
        iota_i = sb("iota_i", [P, SLOTS], I32)
        iota = sb("iota", [P, SLOTS])
        thresh_i = sb("thresh_i", [P, SEQ // SLOTS - 1], I32)
        thresh = sb("thresh", [P, SEQ // SLOTS - 1])
        w_route = sb("w_route", [P, 2, NC, ROUTES])
        b_route = sb("b_route", [P, 2, ROUTES])
        gains = sb("gains", [P, 7, NC])
        rows = sb("rows", [3 * A_HEADS, P])
        cols = sb("cols", [P, 3 * A_HEADS])
        lb = sb("lb", [P, 4, A_HEADS])
        ssq = sb("ssq", [P, NT])
        ms = sb("ms", [P, NT])
        root = sb("root", [P, NT])
        rstd = sb("rstd", [P, NT])
        rounds_i = sb("rounds_i", [P, 2], I32)
        more_i = sb("more_i", [P, 2], I32)
        work = sb("work", [P, 10300])

        def view(at, n):
            return work[:, at:at + n]

        q_dec = [view(1024 * h, 1024).rearrange("p (j t) -> p j t", j=HALF_A) for h in range(2)]
        k_inv = view(2048, 1024)
        k_tail = view(3072, 1536).rearrange("p (n j d) -> p n j d", n=3, j=HALF_A)
        v_tok = view(4608, 1024).rearrange("p (t e) -> p t e", t=NT)
        og_tok = view(5632, 1024).rearrange("p (t e) -> p t e", t=NT)
        att_m = view(6656, 1024).rearrange("p (t j s) -> p t j s", t=NT, j=HALF_A)
        states = view(7680, 1536).rearrange("p (n j e) -> p n j e", n=3, j=HALF_A)
        o_sq = view(9216, 1024)
        dl = view(10240, 16).rearrange("p (h n j) -> p h n j", h=2, n=2)
        o_small = view(10256, 24).rearrange("p (a m) -> p a m", a=3)
        xs_flat = xs[:].rearrange("p t d -> p (t d)")
        h2_flat = hT2[:].rearrange("p c t -> p (c t)")
        t_key, t_log = xs_flat[:, 0:1024], xs_flat[:, 1024:2048]
        t_cum, t_exp = h2_flat[:, 0:1024], h2_flat[:, 1024:2048]
        xg = view(4096, 1024).rearrange("p (c s) -> p c s", c=NC)
        pick = view(5120, 256).rearrange("p (t e s) -> p t e s", t=NT, e=BATCH_E)
        pick_g = view(5376, 256).rearrange("p (t e s) -> p t e s", t=NT, e=BATCH_E)
        pick_gT = view(5632, 256)
        silu = view(5888, 128)
        hid = view(6016, 128)
        hidT = view(6144, 128)
        y_sb = view(6272, 1024)
        rank = view(7296, 64).rearrange("p (t e) -> p t e", t=NT)
        gate = view(7360, 64).rearrange("p (t e) -> p t e", t=NT)
        rank8 = view(7424, 16).rearrange("p (t e) -> p t e", t=NT)
        gate8 = view(7440, 16).rearrange("p (t e) -> p t e", t=NT)

        def pair(at, m):
            return view(at, NT * m).rearrange("p (t m) -> p t m", t=NT)

        logit = pair(7456, ROUTES)
        g_max, g_sum, g_w, top1, top2, top_d, top_x, top_s, w_1, w_2 = (
            pair(7536 + 2 * n, 1) for n in range(10))
        g_dif, g_exp, g_eq, g_cum, g_hot, g_pen = (pair(7560 + 8 * n, GROUPS) for n in range(6))
        e_log, e_dif, e_eq, e_cum, hot1, hot2, chosen = (
            pair(7616 + 64 * n, EXPERTS) for n in range(7))
        most = view(8064, 1)
        over = view(8072, 7)
        n_over = view(8080, 1)
        p_tok = view(8192, 512).rearrange("p (t m) -> p t m", t=NT)
        pT = view(8704, 512).rearrange("p (k s) -> p k s", k=NT)
        sig = view(9216, 1024).rearrange("p (t n) -> p t n", t=NT)
        bias = view(0, 4096).rearrange("p (h j) -> p h j", h=B_HEADS)
        qT = [view(4096 + 1024 * h, 1024).rearrange("p (j t) -> p j t", j=4) for h in range(2)]
        kT = [view(6144 + 1024 * h, 1024).rearrange("p (j t) -> p j t", j=4) for h in range(2)]
        v_rev = view(8192, 1024).rearrange("p (t e) -> p t e", t=NT)
        probs = [view(9216 + 384 * h, 384) for h in range(2)]
        score = [xs_flat[:, 384 * h:384 * h + 384] for h in range(2)]
        probsT = [xs_flat[:, 768 + 384 * h:1152 + 384 * h] for h in range(2)]
        s_max = view(9984, 32).rearrange("p (h t) -> p h t", t=NT)
        s_neg = view(10016, 32).rearrange("p (h t) -> p h t", t=NT)
        s_sum = view(10048, 32).rearrange("p (h t) -> p h t", t=NT)
        s_rec = view(10080, 32).rearrange("p (h t) -> p h t", t=NT)
        fin_gain = h2_flat[:, 0:D]
        fin = hT[:].rearrange("p c t -> p (c t)").rearrange("p (t d) -> p t d", t=NT)

        acc = ctx.enter_context(nc.psum_tensor("acc", [P, NT, D], F32))
        pb = ctx.enter_context(nc.psum_tensor("pb", [P, 4, BANK], F32))

        x_in, small_in, route_in, late_in = sem("x_in"), sem("small_in"), sem("route_in"), sem("late_in")
        p_in = sem("p_in")
        landed = [sem(f"landed{s}") for s in range(RING)]
        moe_landed = [[sem(f"moe_landed{la}_{s}") for s in range(RING)] for la in range(2)]
        moe_freed = sems("moe_freed")
        out_done = sem("out_done")
        pool_step, const_ready, zeroed, bias_mask = (
            sem("pool_step"), sem("const_ready"), sem("zeroed"), sem("bias_mask"))
        cols_ps, lb_ready, lbe = sem("cols_ps"), sem("lb_ready"), sem("lbe")
        dve_step = sem("dve_step")
        sq_done, ms_ready, root_ready, hn_ready = (
            sem("sq_done"), sem("ms_ready"), sem("root_ready"), sem("hn_ready"))
        tr_ps, ht_ready = sem("tr_ps"), sem("ht_ready")
        pj_ps, sig_done, f_ready, ln_done, cum_ready, tail_ready = (
            sem(n) for n in ("pj_ps", "sig_done", "f_ready", "ln_done", "cum_ready", "tail_ready"))
        exp_done, kinv_ready, ktail_ready, qdec_ready, v_ready, og_ready = (
            sem(n) for n in ("exp_done", "kinv_ready", "ktail_ready", "qdec_ready", "v_ready", "og_ready"))
        kt_ps, kt_ready, at_ps, at_ready, kv_ps, st_ready = (
            sem(n) for n in ("kt_ps", "kt_ready", "at_ps", "at_ready", "kv_ps", "st_ready"))
        o_ps, osq_done, oms_ready, oroot_ready, o_ready = (
            sem(n) for n in ("o_ps", "osq_done", "oms_ready", "oroot_ready", "o_ready"))
        ot_ps, ot_ready, added = sem("ot_ps"), sem("ot_ready"), sem("added")
        pt_ps, pt_ready = sem("pt_ps"), sem("pt_ready")
        lg_ps, rk_ps, dif_ready, rexp_done, chosen_ready, rounds_ready = (
            sems(n) for n in ("lg_ps", "rk_ps", "dif_ready", "rexp_done", "chosen_ready", "rounds_ready"))
        pick_ready, pgt_ps, pgt_ready, xg_ps, xg_ready, h_ps = (
            sems(n) for n in ("pick_ready", "pgt_ps", "pgt_ready", "xg_ps", "xg_ready", "h_ps"))
        silu_done, hid_ready, hidT_ps, hidT_ready, y_ps, y_act, y_dve, scat_done, dve_loop = (
            sems(n) for n in ("silu_done", "hid_ready", "hidT_ps", "hidT_ready", "y_ps", "y_act",
                              "y_dve", "scat_done", "dve_loop"))
        gate_ps, proj_ps, sig_ready, xs_ready = (
            sem(n) for n in ("gate_ps", "proj_ps", "sig_ready", "xs_ready"))
        qkv_ps, qkv_ready, s_ps, s_ready, e_ready, pT_ps, pT_ready, oa_ps, oa_ready = (
            sem(n) for n in ("qkv_ps", "qkv_ready", "s_ps", "s_ready", "e_ready", "pT_ps",
                             "pT_ready", "oa_ps", "oa_ready"))
        fin_ready = sem("fin_ready")

        def over_d(w):
            return w.rearrange("(p c) n -> p c n", c=NC)

        def over_rows(w):
            return w.rearrange("(c p) n -> p c n", p=P)

        blocks_a = [over_d(a_w_in[0][:, s * D + h * 512:s * D + h * 512 + 512])
                    for h in range(2) for s in (1, 0, 2, 3)]
        blocks_a += [over_rows(a_w_o[0][512 * j:512 * j + 512, :]) for j in range(2)]

        def embedding(layer):
            gates = [over_d(ple_w_gate[layer][:, 512 * j:512 * j + 512]) for j in range(2)]
            return gates + [over_rows(ple_w_proj[layer])]

        blocks_b = embedding(0)
        for h in range(2):
            blocks_b += [over_d(w[:, a + 512 * h:a + 512 * h + 512])
                         for w, a in ((b_w_q[0], 0), (w_kv, 0), (w_kv, D))]
        blocks_b += [over_rows(b_w_o[0][512 * j:512 * j + 512, :]) for j in range(2)]
        blocks_c = embedding(1)
        assert (len(blocks_a), len(blocks_b), len(blocks_c)) == (MIX_A_BLOCKS, BLOCKS_B, BLOCKS_C)
        place, uses = {}, [0] * RING
        for n, key in enumerate([("a", j) for j in range(len(blocks_a))]
                                + [("b", j) for j in range(len(blocks_b))]
                                + [("c", j) for j in range(len(blocks_c))]):
            uses[n % RING] += 1
            place[key] = n % RING, 16 * uses[n % RING]

        def slot_of(key, src=None):
            s = place[key][0]
            if src is None:
                return ring[:, s]
            return ring[:, s, 0:src.shape[1] * src.shape[2]].rearrange("p (c n) -> p c n", n=src.shape[2])

        def arrived(eng, key):
            s, value = place[key]
            eng.wait_ge(landed[s], value)

        def wait_used(eng, phase, j):
            if j >= len(blocks_b if phase == "b" else blocks_a) - 2:
                eng.wait_ge(added, (3 if phase == "b" else 1) + (j + 2 - len(blocks_b if phase == "b" else blocks_a)))
            elif phase == "a":
                eng.wait_ge(pj_ps, 2 * j + 2)
            elif j < 2:
                eng.wait_ge(gate_ps, 2 * j + 2)
            elif j == 2:
                eng.wait_ge(proj_ps, 4)
            else:
                eng.wait_ge(qkv_ps, 2 * (j - 3) + 2)

        def bank3(b, m):
            return pb[:, b, :].rearrange("p (a n) -> p a n", n=m)

        def wide(ap, n):
            return ap.unsqueeze(len(ap.shape)).to_broadcast(list(ap.shape) + [n])

        block = ctx.enter_context(nc.Block())

        @block.sync
        def _(sp):
            def load(key, src):
                sp.dma_start(slot_of(key, src), src).then_inc(landed[place[key][0]], 16)

            def load_expert(layer, i, k):
                e = k // 3
                s = (MOE_AT[layer] + k) % RING
                kind = expert_slots(layer, e % BODY_E).index(s)
                if kind < 2:
                    w = (moe_w_gate, moe_w_up)[kind]
                    src = w[layer][i * BODY_E + e].rearrange("(p c) n -> p (c n)", c=NC)
                    dst = ring[:, s, :]
                else:
                    src = moe_w_down[layer][i * BODY_E + e].rearrange("(c p) n -> p c n", p=P)
                    dst = ring[:, s, :].rearrange("p (c n) -> p c n", c=4)
                sp.dma_start(dst, src).then_inc(moe_landed[layer][s], 16)

            def experts(layer, phase, blocks):
                rounds = sp.alloc_register(f"sp_rounds{layer}")
                sp.reg_mov(rounds, 1)
                with sp.Fori(0, rounds) as r:
                    sp.wait_ge(moe_freed[layer], r * EXPERTS + 1)
                    for k in range(RING):
                        wait_used(sp, phase, len(blocks) - RING + k)
                        load_expert(layer, 0, k)
                    with sp.Fori(0, BODIES - 1) as i:
                        it = r * BODIES + i
                        for k in range(BODY_BLOCKS):
                            sp.wait_ge(moe_freed[layer], it * BODY_E + (k // 3 + 2))
                            load_expert(layer, i, k + RING)
                    for k in range(BODY_BLOCKS - RING):
                        sp.wait_ge(moe_freed[layer], r * EXPERTS + (EXPERTS - BODY_E + k // 3 + 2))
                        load_expert(layer, BODIES - 1, k + RING)
                    sp.wait_ge(rounds_ready[layer], 1)
                    sp.reg_load(rounds, rounds_i[0:1, layer:layer + 1])

            def after_experts(layer, phase, blocks):
                more = sp.value_load(more_i[0:1, layer:layer + 1], min_val=0, max_val=7)
                for j, src in enumerate(blocks):
                    if j < RING:
                        done = EXPERTS - BODY_E + (BODY_BLOCKS - RING + j) // 3 + 2
                        sp.wait_ge(moe_freed[layer], more * EXPERTS + done)
                    else:
                        wait_used(sp, phase, j - RING)
                    load((phase, j), src)

            sp.dma_start(xs[:], x[0].rearrange("(t p) d -> p t d", p=P)).then_inc(x_in, 16)
            for j, src in enumerate(blocks_a):
                if j >= RING:
                    wait_used(sp, "a", j - RING)
                load(("a", j), src)
            experts(0, "a", blocks_a)
            after_experts(0, "b", blocks_b)
            experts(1, "b", blocks_b)
            after_experts(1, "c", blocks_c)
            for t in range(NT):
                sp.wait_ge(fin_ready, t + 1)
                sp.dma_start(out[0].rearrange("(t p) d -> p t d", p=P)[:, t], fin[:, t]).then_inc(out_done, 16)
            sp.wait_ge(out_done, 16 * NT)

        @block.gpsimd
        def _(pool):
            step = Count(pool, pool_step)
            for m, value in ((ident, 0.0), (flip, 0.0), (ones, 1.0), (before, 1.0)):
                pool.memset(m[:], value).then_inc(pool_step, 1)
            pool.iota(iota_i[:], pattern=[[1, SLOTS]], base=0, channel_multiplier=0).then_inc(pool_step, 1)
            pool.iota(thresh_i[:], pattern=[[SLOTS, SEQ // SLOTS - 1]], base=SLOTS,
                      channel_multiplier=0).then_inc(pool_step, 1)
            step.n = 6
            step.link(pool.memset(causal[:], 1.0))
            pool.affine_select(out=ident[:], in_=ident[:], compare_op=ALU.not_equal, fill=1.0, base=0,
                               pattern=[[-1, P]], channel_multiplier=1).then_inc(const_ready, 1)
            pool.affine_select(out=flip[:], in_=flip[:], compare_op=ALU.not_equal, fill=1.0, base=1 - P,
                               pattern=[[1, P]], channel_multiplier=1).then_inc(const_ready, 1)
            pool.affine_select(out=before[:], in_=before[:], compare_op=ALU.is_gt, fill=0.0, base=0,
                               pattern=[[1, P]], channel_multiplier=-1).then_inc(const_ready, 1)
            pool.tensor_copy(iota[:], iota_i[:]).then_inc(const_ready, 1)
            pool.tensor_copy(thresh[:], thresh_i[:]).then_inc(const_ready, 1)
            step.link(pool.affine_select(out=causal[:], in_=causal[:], compare_op=ALU.is_ge, fill=0.0,
                                         base=0, pattern=[[1, P]], channel_multiplier=-1))
            pool.affine_select(out=causal[:, CHUNK:], in_=causal[:, CHUNK:], compare_op=ALU.is_ge, fill=0.0,
                               base=-CHUNK, pattern=[[0, CHUNK]], channel_multiplier=1).then_inc(const_ready, 1)
            for la in range(2):
                pool.memset(more_i[:, la:la + 1], 0).then_inc(moe_freed[la], 1)
            pool.memset(view(3072, 1536), 0.0).then_inc(zeroed, 1)
            pool.memset(view(6656, 1024), 0.0).then_inc(zeroed, 1)
            pool.wait_ge(added, 2)
            pool.memset(bias[0:CHUNK, :, 0:CHUNK], MASKED).then_inc(bias_mask, 1)

        @block.scalar
        def _(act):
            gain_rows = [norm_mix[0], norm_ffn[0], norm_ple[0], kv_norm, norm_mix[1], norm_ffn[1], norm_ple[1]]
            for n, g in enumerate(gain_rows):
                act.dma_start(gains[:, n, :], g.rearrange("(p c) -> p c", c=NC)).then_inc(small_in, 16)
            act.dma_start(rows[0:2 * A_HEADS, :], a_lb_logits.rearrange("r (h p) -> (r h) p", p=P)).then_inc(small_in, 16)
            act.dma_start(rows[2 * A_HEADS:3 * A_HEADS, :], a_out_norm[0].rearrange("(h p) -> h p", p=P)).then_inc(small_in, 16)
            for la in range(2):
                act.dma_start(w_route[:, la, :, 0:GROUPS], over_d(moe_w_group[la])).then_inc(route_in, 16)
                act.dma_start(w_route[:, la, :, GROUPS:], over_d(moe_w_expert[la])).then_inc(route_in, 16)
                act.dma_start(b_route[:, la, 0:GROUPS], moe_b_group[la].partition_broadcast(P)).then_inc(route_in, 16)
                act.dma_start(b_route[:, la, GROUPS:], moe_b_expert[la].partition_broadcast(P)).then_inc(route_in, 16)

            def norm(n, src):
                for t in range(NT):
                    act.activation(hn[:, t].rearrange("p c q -> p (c q)"), src[:, t], ACT.Square,
                                   accum_out=ssq[:, t:t + 1]).then_inc(sq_done, 1)
                act.wait_ge(ms_ready, n + 1)
                act.activation(root[:], ms[:], ACT.Sqrt).then_inc(root_ready, 1)

            act.wait_ge(x_in, 16)
            norm(0, xs)
            act.wait_ge(lb_ready, 1)
            act.activation(lb[:, 2:4, :], lb[:, 2:4, :], ACT.Exp).then_inc(lbe, 1)

            def gates_f(h):
                for b in range(2):
                    act.wait_ge(pj_ps, 8 * h + b + 1)
                    act.activation(t_key[:, BANK * b:BANK * b + BANK], pb[:, b, :], ACT.Sigmoid).then_inc(sig_done, 1)
                act.wait_ge(f_ready, h + 1)
                act.activation(t_log, t_key, ACT.Ln).then_inc(ln_done, 1)
                act.wait_ge(cum_ready, h + 1)
                act.activation(t_exp, t_cum, ACT.Exp).then_inc(exp_done, 1)
                act.activation(k_inv, t_cum, ACT.Exp, scale=-1.0).then_inc(exp_done, 1)
                act.wait_ge(tail_ready, h + 1)
                act.activation(t_log, t_log, ACT.Exp).then_inc(exp_done, 1)

            def values(h):
                for t in range(NT):
                    act.wait_ge(pj_ps, 8 * h + 5 + t)
                    act.activation(v_tok[:, t], pb[:, 1 + t, :], ACT.Copy).then_inc(v_ready, 1)
                for t in range(NT):
                    act.wait_ge(pj_ps, 8 * h + 7 + t)
                    act.activation(og_tok[:, t], pb[:, (3, 0)[t], :], ACT.Silu).then_inc(og_ready, 1)

            def keys_tail(h):
                act.wait_ge(kt_ps, 2 * h + 1)
                if h == 0:
                    act.wait_ge(zeroed, 1)
                act.activation(k_tail[0:64, 0], bank3(0, P)[0:64], ACT.Copy).then_inc(kt_ready, 1)
                act.activation(k_tail[64:128, 1], bank3(0, P)[64:128], ACT.Copy).then_inc(kt_ready, 1)
                act.wait_ge(kt_ps, 2 * h + 2)
                act.activation(k_tail[0:64, 2], bank3(1, P)[0:64], ACT.Copy).then_inc(kt_ready, 1)

            def out_squares(h):
                for t in range(NT):
                    act.wait_ge(o_ps, 2 * h + t + 1)
                    act.activation(o_sq[:, BANK * t:BANK * t + BANK], pb[:, (3, 0)[t], :],
                                   ACT.Square).then_inc(osq_done, 1)
                act.wait_ge(oms_ready, h + 1)
                act.activation(o_small[:, 1], o_small[:, 0], ACT.Sqrt).then_inc(oroot_ready, 1)

            gates_f(0)
            values(0)
            keys_tail(0)
            gates_f(1)
            out_squares(0)
            values(1)
            keys_tail(1)
            out_squares(1)

            def moe(layer):
                act.wait_ge(added, 2 * layer + 2)
                act.dma_start(p_tok, p[layer, 0].rearrange("(t q) m -> q t m", q=P)).then_inc(p_in, 16)
                if layer == 0:
                    rel = b_rel_bias[0]
                    act.dma_start(bias[CHUNK:P], bass.AP(tensor=rel.tensor, offset=rel.offset,
                                  ap=[[1, CHUNK], [N_REL, B_HEADS], [1, SEQ]])).then_inc(late_in, 16)
                    act.dma_start(bias[0:CHUNK, :, CHUNK:], bass.AP(tensor=rel.tensor, offset=rel.offset,
                                  ap=[[1, CHUNK], [N_REL, B_HEADS], [1, SEQ - CHUNK]])).then_inc(late_in, 16)
                else:
                    act.dma_start(fin_gain, final_norm.partition_broadcast(P)).then_inc(late_in, 16)
                norm(1 + 3 * layer, acc)
                act.wait_ge(pt_ps, layer + 1)
                act.activation(pT.rearrange("p k s -> p (k s)"), pb[:, 0, :], ACT.Copy).then_inc(pt_ready, 1)
                act.wait_ge(dif_ready[layer], 1)
                act.activation(g_exp, g_dif, ACT.Exp).then_inc(rexp_done[layer], 1)
                act.wait_ge(dif_ready[layer], 2)
                act.activation(top_x, top_d, ACT.Exp).then_inc(rexp_done[layer], 1)
                act.wait_ge(rounds_ready[layer], 1)
                rounds = act.value_load(rounds_i[0:1, layer:layer + 1], min_val=1, max_val=8)
                with act.Fori(0, rounds) as r:
                    with act.Fori(0, BODIES) as i:
                        it = r * BODIES + i
                        for b in range(BATCHES):
                            act.wait_ge(pgt_ps[layer], it * BATCHES + (b + 1))
                            act.activation(pick_gT, pb[:, 3, 256:512], ACT.Copy).then_inc(pgt_ready[layer], 1)
                            for e in range(BATCH_E * b, BATCH_E * b + BATCH_E):
                                act.wait_ge(h_ps[layer], it * BODY_E + (e + 1))
                                act.activation(silu, pb[:, 2, 0:P], ACT.Silu).then_inc(silu_done[layer], 1)
                                act.wait_ge(hidT_ps[layer], it * BODY_E + (e + 1))
                                act.activation(hidT, pb[:, 2, 256:384], ACT.Copy).then_inc(hidT_ready[layer], 1)
                                at = SLOTS * (e % BATCH_E)
                                act.wait_ge(y_ps[layer], it * BODY_E + (e + 1))
                                for g, done in ((0, moe_freed), (1, y_act)):
                                    act.activation(y_sb[at:at + SLOTS, 256 * g:256 * g + 256],
                                                   pb[SLOTS * g:SLOTS * g + SLOTS, 3, 0:256],
                                                   ACT.Copy).then_inc(done[layer], 1)
                act.wait_ge(scat_done[layer], rounds * (BODIES * BATCHES))
                norm(2 + 3 * layer, acc)

            def embed(layer):
                for j in range(2):
                    for t in range(NT):
                        n = 4 * layer + 2 * j + t
                        act.wait_ge(gate_ps, n + 1)
                        if j:
                            act.wait_ge(xs_ready, n - 1)
                        act.activation(sig[:, t], pb[:, t, :], ACT.Sigmoid).then_inc(sig_ready, 1)
                act.wait_ge(xs_ready, 4 * layer + 4)
                norm(3 + 3 * layer, xs)

            moe(0)
            embed(0)

            def qkv(n):
                h, kind = divmod(n, 3)
                first = (0, 2, 0, 2, 0, 0)[n]
                for b in range(2):
                    dst = (qT[h], kT[h], v_rev)[kind]
                    dst = dst[:, b] if kind == 2 else dst[:, 2 * b:2 * b + 2].rearrange("p j t -> p (j t)")
                    act.wait_ge(qkv_ps, 2 * n + b + 1)
                    act.activation(dst, pb[:, first + b, :], ACT.Copy,
                                   scale=ATTN_SCALE if kind == 0 else 1.0).then_inc(qkv_ready, 1)

            def exps(n):
                act.wait_ge(s_ready, n + 1)
                if n >= 2:
                    act.wait_ge(pT_ps, n - 1)
                for t, (a, b) in ((1, (0, 256)), (0, (256, 384))):
                    last = act.activation(probs[n % 2][:, a:b], score[n % 2][:, a:b], ACT.Exp,
                                          bias=s_neg[:, n, t:t + 1], accum_out=s_sum[:, n, t:t + 1])
                last.then_inc(e_ready, 1)

            for n in range(5):
                qkv(n)
            for n in range(HALF_B):
                exps(n)
            qkv(5)
            for n in range(HALF_B, B_HEADS):
                exps(n)
            moe(1)
            embed(1)

        @block.vector
        def _(dve):
            step = Count(dve, dve_step)

            def norm(n, src, write=True):
                dve.wait_ge(sq_done, 2 * n + 2)
                dve.tensor_scalar(ms[:], ssq[:], 1.0 / D, EPS, ALU.mult, ALU.add).then_inc(ms_ready, 1)
                dve.wait_ge(root_ready, n + 1)
                step.link(dve.reciprocal(rstd[:], root[:]))
                for t in range(NT if write else 0):
                    dve.tensor_scalar(hn[:, t], src[:, t].rearrange("p (q c) -> p c q", c=NC),
                                      rstd[:, t:t + 1], None, ALU.mult).then_inc(hn_ready, 1)

            def transposed(stage, gain, dst, swap=False):
                for t in range(NT):
                    for j in range(2):
                        dve.wait_ge(tr_ps, 4 * stage + 2 * t + j + 1)
                        to = P * (NT - 1 - t if swap else t)
                        dve.tensor_tensor(dst[:, 4 * j:4 * j + 4, to:to + P], bank3(2 * t + j, P),
                                          wide(gains[:, gain, 4 * j:4 * j + 4], P), ALU.mult).then_inc(ht_ready, 1)

            dve.wait_ge(cols_ps, 1)
            step.link(dve.tensor_copy(cols[:], pb[:, 3, 0:3 * A_HEADS]))
            step.link(dve.tensor_tensor(lb[:, 0], cols[:, 0:A_HEADS], cols[:, A_HEADS:2 * A_HEADS], ALU.max))
            step.link(dve.tensor_tensor(lb[:, 2:4], cols[:, 0:2 * A_HEADS].rearrange("p (r h) -> p r h", r=2),
                                        lb[:, 0].unsqueeze(1).to_broadcast([P, 2, A_HEADS]), ALU.subtract))
            dve.tensor_copy(lb[:, 1], lb[:, 0]).then_inc(lb_ready, 1)
            norm(0, xs)
            dve.wait_ge(small_in, 16 * 9)
            transposed(0, G_MIX0, hT)
            dve.wait_ge(lbe, 1)
            step.link(dve.tensor_tensor(lb[:, 1], lb[:, 2], lb[:, 3], ALU.add))
            step.link(dve.reciprocal(lb[:, 0], lb[:, 1]))
            step.link(dve.tensor_tensor(lb[:, 0], lb[:, 0], lb[:, 2], ALU.mult))
            step.link(dve.tensor_scalar(lb[:, 1], lb[:, 0], -1.0, 1.0, ALU.mult, ALU.add))
            dve.wait_ge(const_ready, 6)

            def forget(h):
                dve.wait_ge(sig_done, 2 * h + 2)
                for j in range(HALF_A):
                    hd = HALF_A * h + j
                    part = t_key[:, SEQ * j:SEQ * j + SEQ]
                    last = dve.tensor_scalar(part, part, lb[:, 1, hd:hd + 1], lb[:, 0, hd:hd + 1], ALU.mult, ALU.add)
                last.then_inc(f_ready, 1)

            def decays(h):
                dve.wait_ge(ln_done, h + 1)
                for n in range(HALF_A * SEQ // CHUNK):
                    part = slice(CHUNK * n, CHUNK * n + CHUNK)
                    last = dve.tensor_tensor_scan(t_cum[:, part], ones[:, 0:CHUNK], t_log[:, part], 0.0,
                                                  ALU.mult, ALU.add)
                last.then_inc(cum_ready, 1)
                dve.wait_ge(cum_ready, h + 1)
                g3 = t_cum.rearrange("p (n s) -> p n s", s=CHUNK)
                dve.tensor_tensor(t_log.rearrange("p (n s) -> p n s", s=CHUNK), wide(g3[:, :, CHUNK - 1], CHUNK),
                                  g3, ALU.subtract).then_inc(tail_ready, 1)
                step.link(dve.tensor_scalar(t_key, t_key, -1.0, 1.0, ALU.mult, ALU.add))
                dve.wait_ge(exp_done, 3 * h + 2)
                dve.tensor_tensor(k_inv, k_inv, t_key, ALU.mult).then_inc(kinv_ready, 1)
                e4 = t_exp.rearrange("p (j n s) -> p n j s", j=HALF_A, s=CHUNK)
                step.link(dve.tensor_copy(dl[:, h], e4[:, 1:3, :, CHUNK - 1]))
                dve.wait_ge(exp_done, 3 * h + 3)
                dve.tensor_tensor(t_log, t_log, t_key, ALU.mult).then_inc(ktail_ready, 1)

            def queries(h):
                for b in range(2):
                    dve.wait_ge(pj_ps, 8 * h + 3 + b)
                    dve.tensor_tensor(q_dec[h][:, 2 * b:2 * b + 2].rearrange("p j t -> p (j t)"),
                                      pb[:, (2, 3)[b] if h == 0 else (1, 2)[b], :],
                                      t_exp[:, BANK * b:BANK * b + BANK], ALU.mult).then_inc(qdec_ready, 1)

            def causal_att(h):
                if h == 0:
                    dve.wait_ge(zeroed, 2)
                mask = causal[:].bitcast(I32).unsqueeze(1).to_broadcast([P, HALF_A, P])
                for t in range(NT):
                    dve.wait_ge(at_ps, 2 * h + t + 1)
                    dve.copy_predicated(att_m[:, t], mask, bank3(2 + t, P)).then_inc(at_ready, 1)

            def chunk_states(h):
                dve.wait_ge(kv_ps, 3 * h + 1)
                dve.tensor_copy(states[:, 0], bank3(2, P)).then_inc(st_ready, 1)
                for n, b in ((1, 3), (2, 0)):
                    dve.wait_ge(st_ready, 3 * h + n)
                    step.link(dve.tensor_tensor(states[:, n], states[:, n - 1], wide(dl[:, h, n - 1], P), ALU.mult))
                    dve.wait_ge(kv_ps, 3 * h + n + 1)
                    dve.tensor_tensor(states[:, n], states[:, n], bank3(b, P), ALU.add).then_inc(st_ready, 1)

            def head_norm(h):
                dve.wait_ge(osq_done, 2 * h + 2)
                step.link(dve.tensor_reduce(o_small[:, 2], o_sq.rearrange("p (m e) -> p m e", e=P), AX, ALU.add))
                dve.tensor_scalar(o_small[:, 0], o_small[:, 2], 1.0 / P, EPS, ALU.mult, ALU.add).then_inc(oms_ready, 1)
                dve.wait_ge(oroot_ready, h + 1)
                step.link(dve.reciprocal(o_small[:, 2], o_small[:, 1]))
                for t in range(NT):
                    o = hn[:, t, HALF_A * h:HALF_A * h + HALF_A]
                    step.link(dve.tensor_tensor(o, bank3((3, 0)[t], P),
                                                wide(o_small[:, 2, 4 * t:4 * t + 4], P), ALU.mult))
                    dve.wait_ge(og_ready, 2 * h + t + 1)
                    dve.tensor_tensor(o, o, og_tok[:, t].rearrange("p (j e) -> p j e", j=HALF_A),
                                      ALU.mult).then_inc(o_ready, 1)

            def mixed(h, dst, gain):
                for t in range(NT):
                    dve.wait_ge(ot_ps, 2 * h + t + 1)
                    k = 4 * (h % 2)
                    to = dst[:, k:k + 4, P * t:P * t + P]
                    if gain:
                        ins = dve.tensor_tensor(to, bank3(1 + t, P),
                                                wide(cols[:, 2 * A_HEADS + k:2 * A_HEADS + k + 4], P), ALU.mult)
                    else:
                        ins = dve.tensor_copy(to, bank3(2 + t, P))
                    ins.then_inc(ot_ready, 1)

            forget(0)
            decays(0)
            queries(0)
            causal_att(0)
            forget(1)
            chunk_states(0)
            decays(1)
            queries(1)
            head_norm(0)
            mixed(0, hT, True)
            causal_att(1)
            chunk_states(1)
            head_norm(1)
            mixed(1, hT, True)

            def first_hot(hot, dif, eq, cum):
                step.link(dve.tensor_scalar(eq, dif, 0.0, None, ALU.is_equal))
                m = eq.shape[2]
                for t in range(NT):
                    last = dve.tensor_tensor_scan(cum[:, t], ones[:, 0:m], eq[:, t], 0.0, ALU.mult, ALU.add)
                    step.link(last)
                step.link(dve.scalar_tensor_tensor(out=hot, in0=cum, scalar=1.0, in1=eq, op0=ALU.is_equal,
                                                   op1=ALU.mult))

            def moe(layer):
                norm(1 + 3 * layer, acc)
                transposed(1 + 4 * layer, (G_FFN0, G_FFN1)[layer], hT)
                dve.wait_ge(route_in, 16 * 8)
                dve.wait_ge(lg_ps[layer], 1)
                step.link(dve.tensor_tensor(logit, pb[:, 0, 0:P].rearrange("p (t m) -> p t m", t=NT)[:, :, 0:ROUTES],
                                            b_route[:, layer].unsqueeze(1).to_broadcast([P, NT, ROUTES]), ALU.add))
                lg, le = logit[:, :, 0:GROUPS], logit[:, :, GROUPS:]

                def spread(v, m):
                    return v.to_broadcast([P, NT, m])

                step.link(dve.tensor_reduce(g_max[:, :, 0], lg, AX, ALU.max))
                step.link(dve.tensor_tensor(g_dif, lg, spread(g_max, GROUPS), ALU.subtract))
                step.link(dve.tensor_copy(e_log, le))
                dve.tensor_copy(e_cum, le).then_inc(dif_ready[layer], 1)
                first_hot(g_hot, g_dif, g_eq, g_cum)
                step.link(dve.tensor_scalar(g_pen, g_hot, -1.0, -MASKED, ALU.add, ALU.mult))
                e4 = e_log.rearrange("p t (g e) -> p t g e", g=GROUPS)
                step.link(dve.tensor_tensor(e4, e4, wide(g_pen, PER_GROUP), ALU.add))
                step.link(dve.tensor_reduce(top1[:, :, 0], e_log, AX, ALU.max))
                step.link(dve.tensor_tensor(e_dif, e_log, spread(top1, EXPERTS), ALU.subtract))
                first_hot(hot1, e_dif, e_eq, e_cum)
                step.link(dve.scalar_tensor_tensor(out=e_log, in0=hot1, scalar=1e5 * MASKED, in1=e_log,
                                                   op0=ALU.mult, op1=ALU.add))
                step.link(dve.tensor_reduce(top2[:, :, 0], e_log, AX, ALU.max))
                step.link(dve.tensor_tensor(e_dif, e_log, spread(top2, EXPERTS), ALU.subtract))
                dve.tensor_tensor(top_d, top2, top1, ALU.subtract).then_inc(dif_ready[layer], 1)
                first_hot(hot2, e_dif, e_eq, e_cum)
                dve.tensor_tensor(chosen, hot1, hot2, ALU.add).then_inc(chosen_ready[layer], 1)
                dve.wait_ge(rexp_done[layer], 2)
                step.link(dve.tensor_reduce(g_sum[:, :, 0], g_exp, AX, ALU.add))
                step.link(dve.reciprocal(g_w, g_sum))
                step.link(dve.tensor_scalar(top_s, top_x, 1.0, None, ALU.add))
                step.link(dve.reciprocal(w_1, top_s))
                step.link(dve.tensor_tensor(w_1, w_1, g_w, ALU.mult))
                step.link(dve.tensor_tensor(w_2, w_1, top_x, ALU.mult))
                step.link(dve.tensor_tensor(hot1, hot1, spread(w_1, EXPERTS), ALU.mult))
                step.link(dve.tensor_tensor(hot2, hot2, spread(w_2, EXPERTS), ALU.mult))
                step.link(dve.tensor_tensor(gate, hot1, hot2, ALU.add))
                dve.wait_ge(rk_ps[layer], 1)
                ranks = pb[:, 1, 0:2 * EXPERTS].rearrange("p (t e) -> p t e", t=NT)
                step.link(dve.scalar_tensor_tensor(out=rank, in0=ranks, scalar=1.0, in1=chosen, op0=ALU.add,
                                                   op1=ALU.mult))
                step.link(dve.tensor_scalar(rank, rank, -1.0, None, ALU.add))
                step.link(dve.tensor_reduce(most, pb[:, 1, 2 * EXPERTS:3 * EXPERTS], AX, ALU.max))
                step.link(dve.tensor_scalar(over, thresh[:], most, None, ALU.is_lt))
                step.link(dve.tensor_reduce(n_over, over, AX, ALU.add))
                step.link(dve.tensor_copy(more_i[:, layer:layer + 1], n_over))
                dve.tensor_scalar(rounds_i[:, layer:layer + 1], n_over, 1.0, None,
                                  ALU.add).then_inc(rounds_ready[layer], 1)
                dve.wait_ge(rounds_ready[layer], 1)
                rounds = dve.value_load(rounds_i[0:1, layer:layer + 1], min_val=1, max_val=8)
                gain = gains[:, (G_FFN0, G_FFN1)[layer]]
                links = 2 + BATCHES
                with dve.Fori(0, rounds) as r:
                    with dve.Fori(0, BODIES) as i:
                        it = r * BODIES + i
                        body = Count(dve, dve_loop[layer], r * (BODIES * links + 1) + i * links)
                        body.link(dve.tensor_copy(rank8, rank[:, :, bass.ds(i * BODY_E, BODY_E)]))
                        body.link(dve.tensor_copy(gate8, gate[:, :, bass.ds(i * BODY_E, BODY_E)]))
                        for b in range(BATCHES):
                            part = slice(BATCH_E * b, BATCH_E * b + BATCH_E)
                            for t in range(NT):
                                last = dve.tensor_tensor(
                                    pick[:, t], wide(rank8[:, t, part], SLOTS),
                                    iota[:].unsqueeze(1).to_broadcast([P, BATCH_E, SLOTS]), ALU.is_equal)
                            body.link(last)
                            for t in range(NT):
                                last = dve.tensor_tensor(pick_g[:, t], pick[:, t],
                                                         wide(gate8[:, t, part], SLOTS), ALU.mult)
                            last.then_inc(pick_ready[layer], 1)
                            for j in range(2):
                                dve.wait_ge(xg_ps[layer], it * (2 * BATCHES) + (2 * b + j + 1))
                                dve.tensor_tensor(xg[:, 4 * j:4 * j + 4], bank3(j, P),
                                                  wide(gain[:, 4 * j:4 * j + 4], P),
                                                  ALU.mult).then_inc(xg_ready[layer], 1)
                            for e in range(BATCH_E * b, BATCH_E * b + BATCH_E):
                                dve.wait_ge(silu_done[layer], it * BODY_E + (e + 1))
                                dve.tensor_tensor(hid, silu, pb[:, 2, P:2 * P],
                                                  ALU.mult).then_inc(hid_ready[layer], 1)
                                at = SLOTS * (e % BATCH_E)
                                dve.wait_ge(y_ps[layer], it * BODY_E + (e + 1))
                                for g in range(2, COLS):
                                    last = dve.tensor_copy(y_sb[at:at + SLOTS, 256 * g:256 * g + 256],
                                                           pb[SLOTS * g:SLOTS * g + SLOTS, 3, 0:256])
                                last.then_inc(y_dve[layer], 1)
                    after = Count(dve, dve_loop[layer], (r + 1) * (BODIES * links + 1) - 1)
                    after.link(dve.tensor_scalar(rank, rank, -float(SLOTS), None, ALU.add))
                dve.wait_ge(scat_done[layer], rounds * (BODIES * BATCHES))
                norm(2 + 3 * layer, acc)
                transposed(2 + 4 * layer, (G_PLE0, G_PLE1)[layer], hT)

            def embed(layer):
                for j in range(2):
                    for t in range(NT):
                        n = 4 * layer + 2 * j + t
                        dve.wait_ge(sig_ready, n + 1)
                        dve.wait_ge(proj_ps, n + 1)
                        step.link(dve.tensor_tensor(sig[:, t], sig[:, t], pb[:, 2 + t, :], ALU.mult))
                        half = slice(BANK * j, BANK * j + BANK)
                        dve.tensor_tensor(xs[:, t, half], sig[:, t], acc[:, t, half], ALU.add).then_inc(xs_ready, 1)

            moe(0)
            embed(0)
            norm(3, xs)
            transposed(3, G_MIX1, hT2)
            transposed(4, G_KV, hT, swap=True)

            def scores(n):
                dve.wait_ge(s_ps, n + 1)
                if n >= 2:
                    dve.wait_ge(e_ready, n - 1)
                for t, (a, b) in ((1, (0, 256)), (0, (256, 384))):
                    last = dve.tensor_tensor_reduce(score[n % 2][:, a:b], pb[:, n % 2, a:b], bias[:, n, 0:b - a],
                                                    1.0, -3.0e38, ALU.add, ALU.max, s_max[:, n, t:t + 1])
                    step.link(last)
                dve.tensor_scalar(s_neg[:, n], s_max[:, n], -1.0, None, ALU.mult).then_inc(s_ready, 1)

            def turned(n):
                dve.wait_ge(pT_ps, n + 1)
                dve.tensor_copy(probsT[n % 2], pb[:, 2, 0:384]).then_inc(pT_ready, 1)

            def attended(n):
                hs = slice(n - 3, n + 1)
                step.link(dve.reciprocal(s_rec[:, hs], s_sum[:, hs]))
                dve.wait_ge(oa_ps, n // 4 + 1)
                o = hn[:].rearrange("p t c (u e) -> p (c u) t e", u=2)[:, hs]
                dve.tensor_tensor(o, pb[:, 3, :].rearrange("p (h t e) -> p h t e", h=4, t=NT),
                                  wide(s_rec[:, hs], B_DIM), ALU.mult).then_inc(oa_ready, 1)

            dve.wait_ge(late_in, 32)
            dve.wait_ge(bias_mask, 1)
            for h in range(2):
                base = HALF_B * h
                scores(base)
                for n in range(base, base + HALF_B):
                    if n + 1 < base + HALF_B:
                        scores(n + 1)
                    turned(n)
                    if n % 4 == 0 and n > base:
                        attended(n - 1)
                attended(base + HALF_B - 1)
                mixed(2 + h, hT2, False)
            moe(1)
            embed(1)
            norm(6, xs, write=False)
            dve.wait_ge(late_in, 48)
            for t in range(NT):
                dve.scalar_tensor_tensor(out=fin[:, t], in0=xs[:, t], scalar=rstd[:, t:t + 1], in1=fin_gain,
                                         op0=ALU.mult, op1=ALU.mult).then_inc(fin_ready, 1)

        @block.tensor
        def _(pe):
            def inject():
                for t in range(NT):
                    for j in range(2):
                        half = slice(BANK * j, BANK * j + BANK)
                        pe.matmul(acc[:, t, half], ident[:], xs[:, t, half], start=True, stop=True)

            def transposes(stage, n, turn=None, after=0):
                for t in range(NT):
                    pe.wait_ge(hn_ready, 2 * n + t + 1)
                    for j in range(2):
                        if after:
                            pe.wait_ge(ht_ready, after + 2 * t + j + 1)
                        for c in range(4):
                            to = pb[:, 2 * t + j, P * c:P * c + P]
                            if turn is None:
                                last = pe.transpose(to, hn[:, t, 4 * j + c], ident[:])
                            else:
                                last = pe.matmul(to, hn[:, t, 4 * j + c], turn[:], start=True, stop=True)
                        last.then_inc(tr_ps, 1)

            def by_feature(key, src, banks, x_t, free):
                arrived(pe, key)
                w = slot_of(key, src)
                for b in range(2):
                    free(b)
                    for m in range(2):
                        for c in range(NC):
                            at = P * (2 * b + m)
                            last = pe.matmul(pb[:, banks[b], SEQ * m:SEQ * m + SEQ], w[:, c, at:at + P],
                                             x_t[:, c], start=c == 0, stop=c == NC - 1)
                    yield last, b

            def by_token(key, src, banks, x_t, free):
                arrived(pe, key)
                w = slot_of(key, src)
                for t in range(NT):
                    free(t)
                    for c in range(NC):
                        last = pe.matmul(pb[:, banks[t], :], x_t[:, c, P * t:P * t + P], w[:, c, :],
                                         start=c == 0, stop=c == NC - 1)
                    yield last, t

            def add_mixed(phase, j, src, x_t, h):
                arrived(pe, (phase, j))
                w = slot_of((phase, j), src)
                pe.wait_ge(ot_ready, 2 * h + 2)
                for t in range(NT):
                    for m in range(2):
                        for c in range(4):
                            last = pe.matmul(acc[:, t, BANK * m:BANK * m + BANK],
                                             x_t[:, 4 * (h % 2) + c, P * t:P * t + P],
                                             w[:, c, BANK * m:BANK * m + BANK], start=False, stop=True,
                                             skip_group_check=True)
                last.then_inc(added, 1)

            def free_none(b):
                pass

            pe.wait_ge(const_ready, 1)
            pe.wait_ge(small_in, 16 * 9)
            pe.transpose(pb[:, 3, 0:3 * A_HEADS], rows[:], ident[0:3 * A_HEADS, 0:3 * A_HEADS]).then_inc(cols_ps, 1)
            pe.wait_ge(x_in, 16)
            inject()
            transposes(0, 0)

            def project_f(h):
                def free(b):
                    if h == 0:
                        pe.wait_ge(ht_ready, 4)
                    else:
                        pe.wait_ge(kt_ready, 3)
                for last, b in by_feature(("a", 4 * h), blocks_a[4 * h], (0, 1), hT, free):
                    last.then_inc(pj_ps, 1)

            def project_q(h):
                def free(b):
                    if h and b == 0:
                        pe.wait_ge(sig_done, 4)
                    elif h:
                        pe.wait_ge(st_ready, 1)
                banks = (1, 2) if h else (2, 3)
                for last, b in by_feature(("a", 4 * h + 1), blocks_a[4 * h + 1], banks, hT, free):
                    last.then_inc(pj_ps, 1)

            def project_v(h):
                def free(t):
                    if h == 0 and t == 0:
                        pe.wait_ge(sig_done, 2)
                    pe.wait_ge(qdec_ready, 2 * h + 1 + (t if h else 0))
                for last, t in by_token(("a", 4 * h + 2), blocks_a[4 * h + 2], (1, 2), hT, free):
                    last.then_inc(pj_ps, 1)

            def project_og(h):
                def free(t):
                    if h == 0:
                        pe.wait_ge(qdec_ready, 2)
                    else:
                        pe.wait_ge(o_ready, t + 1)
                for last, t in by_token(("a", 4 * h + 3), blocks_a[4 * h + 3], (3, 0), hT, free):
                    last.then_inc(pj_ps, 1)

            def tails(h):
                pe.wait_ge(ktail_ready, h + 1)
                pe.wait_ge(og_ready, 2 * h + 2)
                for j in range(HALF_A):
                    last = pe.transpose(pb[:, 0, P * j:P * j + P], t_log[:, SEQ * j:SEQ * j + P], ident[:])
                last.then_inc(kt_ps, 1)
                if h:
                    pe.wait_ge(ot_ready, 1)
                else:
                    pe.wait_ge(v_ready, 1)
                for j in range(HALF_A):
                    last = pe.transpose(pb[0:64, 1, P * j:P * j + P], t_log[:, SEQ * j + P:SEQ * j + P + 64], ident[:])
                last.then_inc(kt_ps, 1)

            def attention_a(h):
                pe.wait_ge(kinv_ready, h + 1)
                pe.wait_ge(qdec_ready, 2 * h + 2)
                for t in range(NT):
                    if t == 0 and h:
                        pe.wait_ge(ot_ready, 2)
                    elif t == 0:
                        pe.wait_ge(v_ready, 2)
                    for j in range(HALF_A):
                        last = pe.matmul(pb[:, 2 + t, P * j:P * j + P],
                                         k_inv[:, SEQ * j + P * t:SEQ * j + P * t + P],
                                         q_dec[h][:, j, P * t:P * t + P], start=True, stop=True)
                    last.then_inc(at_ps, 1)

            def state_parts(h):
                pe.wait_ge(kt_ready, 3 * h + 3)
                pe.wait_ge(v_ready, 2 * h + 2)
                for n, b in enumerate((2, 3, 0)):
                    if n < 2:
                        pe.wait_ge(at_ready, 2 * h + n + 1)
                    elif h == 0:
                        pe.wait_ge(sig_done, 3)
                    for j in range(HALF_A):
                        last = pe.matmul(pb[:, b, P * j:P * j + P], k_tail[:, n, j],
                                         v_tok[:, n // 2, P * j:P * j + P], start=True, stop=True)
                    last.then_inc(kv_ps, 1)

            def outputs(h):
                pe.wait_ge(st_ready, 3 * h + 3)
                for t, b in ((0, 3), (1, 0)):
                    for j in range(HALF_A):
                        cut = slice(P * j, P * j + P)
                        chunks = [2 * t + u for u in range(2) if 2 * t + u > 0]
                        last = pe.matmul(pb[:, b, cut], att_m[:, t, j], v_tok[:, t, cut], start=True, stop=False,
                                         skip_group_check=True)
                        for n in chunks:
                            u = n % 2
                            last = pe.matmul(pb[64 * u:64 * u + 64, b, cut],
                                             q_dec[h][:, j, CHUNK * n:CHUNK * n + CHUNK], states[:, n - 1, j],
                                             start=False, stop=True, skip_group_check=True)
                    last.then_inc(o_ps, 1)

            def turn_mixed(h, ready, banks):
                for t in range(NT):
                    ready(t)
                    for c in range(4):
                        last = pe.transpose(pb[:, banks[t], P * c:P * c + P], hn[:, t, 4 * (h % 2) + c], ident[:])
                    last.then_inc(ot_ps, 1)

            def a_ready(h):
                def ready(t):
                    pe.wait_ge(o_ready, 2 * h + t + 1)
                    pe.wait_ge(v_ready, 3 + t)
                return ready

            project_f(0)
            project_q(0)
            project_v(0)
            project_og(0)
            tails(0)
            attention_a(0)
            project_f(1)
            state_parts(0)
            project_q(1)
            outputs(0)
            project_v(1)
            project_og(1)
            turn_mixed(0, a_ready(0), (1, 2))
            tails(1)
            attention_a(1)
            state_parts(1)
            add_mixed("a", 8, blocks_a[8], hT, 0)
            outputs(1)
            turn_mixed(1, a_ready(1), (1, 2))
            add_mixed("a", 9, blocks_a[9], hT, 1)

            def moe(layer):
                pe.wait_ge(p_in, 16 * (layer + 1))
                for k in range(D_PLE // P):
                    for t in range(NT):
                        last = pe.transpose(pb[:, 0, SEQ * k + P * t:SEQ * k + P * t + P],
                                            p_tok[:, t, P * k:P * k + P], ident[:])
                last.then_inc(pt_ps, 1)
                pe.wait_ge(pt_ready, layer + 1)
                stage = 1 + 4 * layer
                transposes(stage, 1 + 3 * layer)
                pe.wait_ge(ht_ready, 4 * stage + 4)
                pe.wait_ge(route_in, 16 * 8)
                for t in range(NT):
                    for c in range(NC):
                        last = pe.matmul(pb[:, 0, 64 * t:64 * t + ROUTES], hT[:, c, P * t:P * t + P],
                                         w_route[:, layer, c], start=c == 0, stop=c == NC - 1)
                last.then_inc(lg_ps[layer], 1)
                pe.wait_ge(chosen_ready[layer], 1)
                pe.wait_ge(const_ready, 6)
                ranks = pb[:, 1]
                pe.matmul(ranks[:, 0:EXPERTS], before[:], chosen[:, 0], start=True, stop=True)
                pe.matmul(ranks[:, EXPERTS:2 * EXPERTS], ones[:], chosen[:, 0], start=True, stop=False)
                pe.matmul(ranks[:, EXPERTS:2 * EXPERTS], before[:], chosen[:, 1], start=False, stop=True)
                pe.matmul(ranks[:, 2 * EXPERTS:3 * EXPERTS], ones[:], chosen[:, 0], start=True, stop=False)
                pe.matmul(ranks[:, 2 * EXPERTS:3 * EXPERTS], ones[:], chosen[:, 1], start=False,
                          stop=True).then_inc(rk_ps[layer], 1)
                pe.wait_ge(rounds_ready[layer], 1)
                rounds = pe.value_load(rounds_i[0:1, layer:layer + 1], min_val=1, max_val=8)
                with pe.Fori(0, rounds) as r:
                    with pe.Fori(0, BODIES) as i:
                        it = r * BODIES + i
                        for b in range(BATCHES):
                            experts(layer, it, b)
                return rounds

            def experts(layer, it, b):
                def here(slot, k):
                    pe.wait_ge(moe_landed[layer][slot], it * (16 * BODY_BLOCKS // RING) + 16 * (k // RING + 1))

                pe.wait_ge(pick_ready[layer], it * BATCHES + (b + 1))
                for t in range(NT):
                    last = pe.transpose(pb[:, 3, 256 + P * t:256 + P * t + P],
                                        pick_g[:, t].rearrange("p e s -> p (e s)"), ident[:])
                last.then_inc(pgt_ps[layer], 1)
                for j in range(2):
                    for c in range(4):
                        for t in range(NT):
                            last = pe.matmul(pb[:, j, P * c:P * c + P], hn[:, t, 4 * j + c],
                                             pick[:, t].rearrange("p e s -> p (e s)"), start=t == 0,
                                             stop=t == NT - 1)
                    last.then_inc(xg_ps[layer], 1)
                pe.wait_ge(xg_ready[layer], it * (2 * BATCHES) + (2 * b + 2))
                for e in range(BATCH_E * b, BATCH_E * b + BATCH_E):
                    s_gate, s_up, s_down = expert_slots(layer, e)
                    first = (MOE_AT[layer] + 3 * e) % RING
                    k_of = {(first + n) % RING: 3 * e + n for n in range(3)}
                    at = SLOTS * (e % BATCH_E)
                    here(s_gate, k_of[s_gate])
                    here(s_up, k_of[s_up])
                    for c in range(NC):
                        for g in range(COLS):
                            cut = BANK * c + P * g
                            last = pe.matmul(pb[SLOTS * g:SLOTS * g + SLOTS, 2, 0:256],
                                             xg[:, c, at:at + SLOTS], ring[:, s_gate:s_gate + 2, cut:cut + P],
                                             start=c == 0, stop=c == NC - 1, tile_position=(0, SLOTS * g))
                    last.then_inc(h_ps[layer], 1)
                    pe.wait_ge(hid_ready[layer], it * BODY_E + (e + 1))
                    pe.transpose(pb[:, 2, 256:384], hid, ident[:]).then_inc(hidT_ps[layer], 1)
                    pe.wait_ge(hidT_ready[layer], it * BODY_E + (e + 1))
                    here(s_down, k_of[s_down])
                    if e % BATCH_E == 0:
                        pe.wait_ge(pgt_ready[layer], it * BATCHES + (b + 1))
                    else:
                        pe.wait_ge(y_act[layer], it * BODY_E + e)
                        pe.wait_ge(y_dve[layer], it * BODY_E + e)
                    for c in range(D_EXPERT // P):
                        for g in range(COLS):
                            cut = D * c + 256 * g
                            last = pe.matmul(pb[SLOTS * g:SLOTS * g + SLOTS, 3, 0:256],
                                             hidT[:, SLOTS * c:SLOTS * c + SLOTS], ring[:, s_down, cut:cut + 256],
                                             start=c == 0, stop=c == D_EXPERT // P - 1,
                                             tile_position=(0, SLOTS * g))
                    last.then_inc(y_ps[layer], 1)
                pe.wait_ge(y_act[layer], it * BODY_E + (BATCH_E * b + BATCH_E))
                pe.wait_ge(y_dve[layer], it * BODY_E + (BATCH_E * b + BATCH_E))
                for t in range(NT):
                    for j in range(2):
                        last = pe.matmul(acc[:, t, BANK * j:BANK * j + BANK], pick_gT[:, P * t:P * t + P],
                                         y_sb[:, BANK * j:BANK * j + BANK], start=False, stop=True,
                                         skip_group_check=True)
                last.then_inc(scat_done[layer], 1)

            def embed(layer):
                phase, blocks = ("b", blocks_b) if layer == 0 else ("c", blocks_c)
                stage = 2 + 4 * layer
                transposes(stage, 2 + 3 * layer)
                pe.wait_ge(ht_ready, 4 * stage + 4)
                for j in range(2):
                    def free(t, j=j):
                        if j:
                            pe.wait_ge(sig_ready, 4 * layer + t + 1)
                    for last, t in by_token((phase, j), blocks[j], (0, 1), hT, free):
                        last.then_inc(gate_ps, 1)
                    arrived(pe, (phase, 2))
                    w = slot_of((phase, 2), blocks[2])
                    for t in range(NT):
                        if j:
                            pe.wait_ge(xs_ready, 4 * layer + t + 1)
                        for k in range(D_PLE // P):
                            last = pe.matmul(pb[:, 2 + t, :], pT[:, k, P * t:P * t + P],
                                             w[:, k, BANK * j:BANK * j + BANK], start=k == 0, stop=k == 1)
                        last.then_inc(proj_ps, 1)

            moe(0)
            embed(0)
            pe.wait_ge(xs_ready, 4)
            inject()
            transposes(3, 3)
            transposes(4, 3, turn=flip, after=12)

            def project_qkv(n, free):
                h, kind = divmod(n, 3)
                j = 3 + n
                first = (0, 2, 0, 2, 0, 0)[n]
                banks = (first, first + 1)
                if kind == 2:
                    parts = by_token(("b", j), blocks_b[j], banks, hT, free)
                else:
                    parts = by_feature(("b", j), blocks_b[j], banks, (hT2, hT)[kind], free)
                for last, _ in parts:
                    last.then_inc(qkv_ps, 1)

            def after_evac(count):
                return lambda b: pe.wait_ge(qkv_ready, count + b)

            def q_k(n):
                if n >= 2:
                    pe.wait_ge(s_ready, n - 1)
                h, m = divmod(n, HALF_B)
                rows_h = slice(64 * (m % 2), 64 * (m % 2) + 64)
                j = m // 2
                pe.matmul(pb[:, n % 2, 0:256], qT[h][rows_h, j, P:SEQ], kT[h][rows_h, j], start=True, stop=True)
                pe.matmul(pb[:, n % 2, 256:384], qT[h][rows_h, j, 0:P], kT[h][rows_h, j, P:SEQ],
                          start=True, stop=True).then_inc(s_ps, 1)

            def turn_probs(n):
                pe.wait_ge(e_ready, n + 1)
                if n:
                    pe.wait_ge(pT_ready, n)
                for m in range(3):
                    last = pe.transpose(pb[:, 2, P * m:P * m + P], probs[n % 2][:, P * m:P * m + P], ident[:])
                last.then_inc(pT_ps, 1)

            def p_v(n):
                pe.wait_ge(pT_ready, n + 1)
                if n % 4 == 0 and n:
                    pe.wait_ge(oa_ready, n // 4)
                at = P * (n % 4)
                v = v_rev[:, :, B_DIM * (n % HALF_B):B_DIM * (n % HALF_B) + B_DIM]
                pt = probsT[n % 2]
                pe.matmul(pb[:, 3, at:at + B_DIM], pt[:, 256:384], v[:, 1], start=True, stop=True)
                pe.matmul(pb[:, 3, at + B_DIM:at + P], pt[:, 0:P], v[:, 0], start=True, stop=False)
                last = pe.matmul(pb[:, 3, at + B_DIM:at + P], pt[:, P:256], v[:, 1], start=False, stop=True)
                if n % 4 == 3:
                    last.then_inc(oa_ps, 1)

            def heads(h):
                base = HALF_B * h
                q_k(base)
                for n in range(base, base + HALF_B):
                    if n + 1 < base + HALF_B:
                        q_k(n + 1)
                    turn_probs(n)
                    if n > base:
                        p_v(n - 1)
                p_v(base + HALF_B - 1)

            def b_ready(h):
                def ready(t):
                    pe.wait_ge(oa_ready, 2 * h + 2)
                return ready

            pe.wait_ge(ht_ready, 20)
            project_qkv(0, free_none)
            project_qkv(1, free_none)
            project_qkv(2, after_evac(1))
            project_qkv(3, after_evac(3))
            project_qkv(4, after_evac(5))
            pe.wait_ge(qkv_ready, 10)
            heads(0)
            pe.wait_ge(s_ready, 8)
            project_qkv(5, free_none)
            turn_mixed(2, b_ready(0), (2, 3))
            add_mixed("b", 9, blocks_b[9], hT2, 2)
            pe.wait_ge(qkv_ready, 12)
            heads(1)
            turn_mixed(3, b_ready(1), (2, 3))
            add_mixed("b", 10, blocks_b[10], hT2, 3)
            moe(1)
            embed(1)


_INS = ['x', 'p', 'a_w_in', 'a_lb_logits', 'a_out_norm', 'a_w_o', 'kv_norm', 'w_kv', 'b_w_q', 'b_rel_bias',
        'b_w_o', 'norm_mix', 'norm_ffn', 'norm_ple', 'moe_w_group', 'moe_b_group', 'moe_w_expert',
        'moe_b_expert', 'moe_w_gate', 'moe_w_up', 'moe_w_down', 'ple_w_proj', 'ple_w_gate', 'final_norm']
_OUTS = [((1, 256, 1024), 'float32')]


def kernel(**inputs):
    import numpy as _np
    import concourse.bacc as _bacc
    from concourse import mybir as _mybir
    from concourse.bass_utils import run_bass_kernel_spmd as _run

    nc = _bacc.Bacc("TRN2", target_bir_lowering=False, num_devices=1)
    arrays, args = {}, []
    for name in _INS:
        a = _np.ascontiguousarray(inputs[name])
        arrays[f"in_{name}_dram"] = a
        args.append(nc.dram_tensor(f"in_{name}_dram", a.shape, _mybir.dt.from_np(a.dtype), kind="ExternalInput").ap())
    for i, (shape, dtype) in enumerate(_OUTS):
        dt = _mybir.dt.from_np(_np.dtype(dtype))
        args.append(nc.dram_tensor(f"out_{i}_dram", shape, dt, kind="ExternalOutput").ap())
    build(nc, *args)
    r = _run(nc, [arrays], core_ids=[0])
    got = tuple(r.results[0][f"out_{i}_dram"] for i in range(len(_OUTS)))
    return got[0]
```

```python
from contextlib import ExitStack

import concourse.bass as bass
from concourse import mybir

F32 = mybir.dt.float32
F32R = mybir.dt.float32r
I32 = mybir.dt.int32
ALU = mybir.AluOpType
ACT = mybir.ActivationFunctionType
AX = mybir.AxisListType.X

P = 128
D = 1024
SEQ = 256
NT = SEQ // P
NC = D // P
CHUNK = 64
BANK = 512
A_HEADS = 8
HALF_A = A_HEADS // 2
B_HEADS = 16
B_DIM = D // B_HEADS
HALF_B = B_HEADS // 2
ATTN_SCALE = B_DIM ** -0.5
N_REL = 320
D_PLE = 256
GROUPS = 4
PER_GROUP = 8
EXPERTS = GROUPS * PER_GROUP
D_EXPERT = 512
ROUTES = GROUPS + EXPERTS
EPS = 1e-6
MASKED = -1e30
SLOTS = 32
BATCH_E = P // SLOTS
COLS = P // SLOTS
RING = 8
SLOT = NC * BANK
BODY_E = 8
BODY_BLOCKS = 3 * BODY_E
BODIES = EXPERTS // BODY_E
BATCHES = BODY_E // BATCH_E
BLOCKS_A, BLOCKS_B, BLOCKS_C = 11, 11, 2
PLAIN = (1, 2, 4, 5)
PROJ = 10
DENSE_RING = RING - 1
PIECE = BANK
PIECES = SLOT // PIECE
SPLIT_BUFS = 4
FIRST, REST = range(PIECES // 2), range(PIECES // 2, PIECES)
(G_MIX0, G_MIX1, G_FFN0, G_FFN1, G_PLE0, G_PLE1, G_KV) = range(7)


class Count:

    def __init__(self, eng, sem, base=0):
        self.eng, self.sem, self.base, self.n = eng, sem, base, 0

    def link(self, ins):
        self.n += 1
        ins.then_inc(self.sem, 1)
        self.eng.wait_ge(self.sem, self.base + self.n)


def expert_slots(e):
    s = 3 * e % RING
    if s == RING - 1:
        return 0, 1, s
    return s, s + 1, (s + 2) % RING


def build(nc, x, p, a_w_in, a_lb_logits, a_out_norm, a_w_o, kv_norm, w_kv, b_w_q, b_rel_bias,
          b_w_o, norm_mix, norm_ffn, norm_ple, moe_w_group, moe_b_group, moe_w_expert,
          moe_b_expert, moe_w_gate, moe_w_up, moe_w_down, ple_w_proj, ple_w_gate, final_norm, out):
    ctx = ExitStack()
    with ctx:
        def sb(name, shape, dt=F32):
            return ctx.enter_context(nc.sbuf_tensor(name, shape, dt))

        def sem(name):
            return ctx.enter_context(nc.semaphore(name))

        def sems(name):
            return [sem(f"{name}{layer}") for layer in range(2)]

        ring = sb("ring", [P, RING, SLOT])
        xs = sb("xs", [P, NT, D])
        hn = sb("hn", [P, NT, NC, P])
        hT_hi = sb("hT_hi", [P, NC, SEQ], F32R)
        hT_lo = sb("hT_lo", [P, NC, SEQ], F32R)
        w_hi = sb("w_hi", [P, SPLIT_BUFS, PIECE], F32R)
        w_lo = sb("w_lo", [P, SPLIT_BUFS, PIECE], F32R)
        ident = sb("ident", [P, P])
        flip = sb("flip", [P, P])
        before = sb("before", [P, P])
        ones = sb("ones", [P, P])
        causal = sb("causal", [P, P])
        iota_i = sb("iota_i", [P, SLOTS], I32)
        iota = sb("iota", [P, SLOTS])
        thresh_i = sb("thresh_i", [P, SEQ // SLOTS - 1], I32)
        thresh = sb("thresh", [P, SEQ // SLOTS - 1])
        w_route = sb("w_route", [P, 2, NC, ROUTES])
        b_route = sb("b_route", [P, 2, ROUTES])
        gains = sb("gains", [P, 7, NC])
        rows = sb("rows", [3 * A_HEADS, P])
        cols = sb("cols", [P, 3 * A_HEADS])
        lb = sb("lb", [P, 4, A_HEADS])
        ssq = sb("ssq", [P, NT])
        ms = sb("ms", [P, NT])
        root = sb("root", [P, NT])
        rstd = sb("rstd", [P, NT])
        rounds_i = sb("rounds_i", [P, 2], I32)
        more_i = sb("more_i", [P, 2], I32)
        work = sb("work", [P, 6450])
        bench = ring[:, DENSE_RING]

        def view(at, n):
            return work[:, at:at + n]

        q_dec = [bench[:, 1024 * h:1024 * h + 1024].rearrange("p (j t) -> p j t", j=HALF_A) for h in range(2)]
        t_cum, t_exp = bench[:, 2048:3072], bench[:, 3072:4096]
        k_inv = view(0, 1024)
        k_tail = view(1024, 1536).rearrange("p (n j d) -> p n j d", n=3, j=HALF_A)
        v_tok = view(2560, 1024).rearrange("p (t e) -> p t e", t=NT)
        att_m = view(3584, 1024).rearrange("p (t j s) -> p t j s", t=NT, j=HALF_A)
        states = view(4608, 1536).rearrange("p (n j e) -> p n j e", n=3, j=HALF_A)
        dl = view(6144, 16).rearrange("p (h n j) -> p h n j", h=2, n=2)
        o_small = view(6160, 24).rearrange("p (a m) -> p a m", a=3)
        xs_flat = xs[:].rearrange("p t d -> p (t d)")
        t_key, t_log = xs_flat[:, 0:1024], xs_flat[:, 1024:2048]
        o_sq = t_key
        og_tok = hn[:, :, HALF_A:]
        routeT = xs_flat.rearrange("p (c s) -> p c s", c=NC)
        xg = view(0, 1024).rearrange("p (c s) -> p c s", c=NC)
        pick = view(1024, 256).rearrange("p (t e s) -> p t e s", t=NT, e=BATCH_E)
        pick_g = view(1280, 256).rearrange("p (t e s) -> p t e s", t=NT, e=BATCH_E)
        pick_gT = view(1536, 256)
        silu = view(1792, 128)
        hid = view(1920, 128)
        hidT = view(2048, 128)
        y_sb = view(2176, 1024)
        rank = view(3200, 64).rearrange("p (t e) -> p t e", t=NT)
        gate = view(3264, 64).rearrange("p (t e) -> p t e", t=NT)
        rank8 = view(3328, 16).rearrange("p (t e) -> p t e", t=NT)
        gate8 = view(3344, 16).rearrange("p (t e) -> p t e", t=NT)
        dump = view(0, 2048).rearrange("p (t d) -> p t d", t=NT)

        def pair(at, m):
            return view(at, NT * m).rearrange("p (t m) -> p t m", t=NT)

        logit = pair(3360, ROUTES)
        g_max, g_sum, g_w, top1, top2, top_d, top_x, top_s, w_1, w_2 = (
            pair(3440 + 2 * n, 1) for n in range(10))
        g_dif, g_exp, g_eq, g_cum, g_hot, g_pen = (pair(3464 + 8 * n, GROUPS) for n in range(6))
        e_log, e_dif, e_eq, e_cum, hot1, hot2, chosen = (
            pair(3520 + 64 * n, EXPERTS) for n in range(7))
        most = view(3968, 1)
        over = view(3976, 7)
        n_over = view(3984, 1)
        p_tok = view(4096, 512).rearrange("p (t m) -> p t m", t=NT)
        pT = view(4608, 512).rearrange("p (k s) -> p k s", k=NT)
        sig = view(5120, 1024).rearrange("p (t n) -> p t n", t=NT)
        bias = view(0, 4096).rearrange("p (h j) -> p h j", h=B_HEADS)
        qT = [bench[:, 1024 * h:1024 * h + 1024].rearrange("p (j t) -> p j t", j=4) for h in range(2)]
        kT = [bench[:, 2048 + 1024 * h:3072 + 1024 * h].rearrange("p (j t) -> p j t", j=4) for h in range(2)]
        v_rev = view(4096, 1024).rearrange("p (t e) -> p t e", t=NT)
        probs = [view(5120 + 384 * h, 384) for h in range(2)]
        score = [xs_flat[:, 384 * h:384 * h + 384] for h in range(2)]
        probsT = [xs_flat[:, 768 + 384 * h:1152 + 384 * h] for h in range(2)]
        s_max = view(5888, 32).rearrange("p (h t) -> p h t", t=NT)
        s_neg = view(5920, 32).rearrange("p (h t) -> p h t", t=NT)
        s_sum = view(5952, 32).rearrange("p (h t) -> p h t", t=NT)
        s_rec = view(5984, 32).rearrange("p (h t) -> p h t", t=NT)
        fin_gain = view(0, D)
        fin = hn[:].rearrange("p t c q -> p t (c q)")

        acc = ctx.enter_context(nc.psum_tensor("acc", [P, NT, D], F32))
        pb = ctx.enter_context(nc.psum_tensor("pb", [P, 4, BANK], F32))

        x_in, small_in, route_in, late_in = sem("x_in"), sem("small_in"), sem("route_in"), sem("late_in")
        p_in = sem("p_in")
        landed = [sem(f"landed{s}") for s in range(RING)]
        moe_landed = [[sem(f"moe_landed{la}_{s}") for s in range(RING)] for la in range(2)]
        moe_freed = sems("moe_freed")
        out_done = sem("out_done")
        hi_ready, lo_ready, piece_used = sem("hi_ready"), sem("lo_ready"), sem("piece_used")
        pool_step, const_ready, zeroed, bias_mask = (
            sem("pool_step"), sem("const_ready"), sem("zeroed"), sem("bias_mask"))
        cols_ps, lb_ready, lbe = sem("cols_ps"), sem("lb_ready"), sem("lbe")
        dve_step = sem("dve_step")
        sq_done, ms_ready, root_ready, hn_ready = (
            sem("sq_done"), sem("ms_ready"), sem("root_ready"), sem("hn_ready"))
        tr_ps, ht_ready = sem("tr_ps"), sem("ht_ready")
        rstd_ready, normed, wroute_ready = sem("rstd_ready"), sem("normed"), sem("wroute_ready")
        pj_ps, sig_done, f_ready, ln_done, cum_ready, tail_ready = (
            sem(n) for n in ("pj_ps", "sig_done", "f_ready", "ln_done", "cum_ready", "tail_ready"))
        exp_done, kinv_ready, ktail_ready, qdec_ready, v_ready, og_ready = (
            sem(n) for n in ("exp_done", "kinv_ready", "ktail_ready", "qdec_ready", "v_ready", "og_ready"))
        kt_ps, kt_ready, at_ps, at_ready, kv_ps, st_ready = (
            sem(n) for n in ("kt_ps", "kt_ready", "at_ps", "at_ready", "kv_ps", "st_ready"))
        o_ps, osq_done, oms_ready, oroot_ready, o_ready = (
            sem(n) for n in ("o_ps", "osq_done", "oms_ready", "oroot_ready", "o_ready"))
        ot_ps, ot_ready, added = sem("ot_ps"), sem("ot_ready"), sem("added")
        pt_ps, pt_ready = sem("pt_ps"), sem("pt_ready")
        lg_ps, rk_ps, dif_ready, rexp_done, chosen_ready, rounds_ready = (
            sems(n) for n in ("lg_ps", "rk_ps", "dif_ready", "rexp_done", "chosen_ready", "rounds_ready"))
        pick_ready, pgt_ps, pgt_ready, xg_ps, xg_ready, h_ps = (
            sems(n) for n in ("pick_ready", "pgt_ps", "pgt_ready", "xg_ps", "xg_ready", "h_ps"))
        silu_done, hid_ready, hidT_ps, hidT_ready, y_ps, y_act, y_dve, scat_done, dve_loop = (
            sems(n) for n in ("silu_done", "hid_ready", "hidT_ps", "hidT_ready", "y_ps", "y_act",
                              "y_dve", "scat_done", "dve_loop"))
        gate_ps, proj_ps, pp_ready, sig_ready, xs_ready = (
            sem(n) for n in ("gate_ps", "proj_ps", "pp_ready", "sig_ready", "xs_ready"))
        qkv_ps, qkv_ready, s_ps, s_ready, e_ready, pT_ps, pT_ready, oa_ps, oa_ready = (
            sem(n) for n in ("qkv_ps", "qkv_ready", "s_ps", "s_ready", "e_ready", "pT_ps",
                             "pT_ready", "oa_ps", "oa_ready"))
        fin_ready = sem("fin_ready")

        def over_d(w):
            return w.rearrange("(p c) n -> p c n", c=NC)

        def over_rows(w):
            return w.rearrange("(c p) n -> p c n", p=P)

        blocks_a = [over_d(a_w_in[0][:, s * D + h * 512:s * D + h * 512 + 512])
                    for h in range(2) for s in (1, 0, 2, 3)]
        blocks_a += [over_rows(a_w_o[0][512 * j:512 * j + 512, :]) for j in range(2)]

        def gate_blocks(layer):
            return [over_d(ple_w_gate[layer][:, 512 * j:512 * j + 512]) for j in range(2)]

        blocks_a += [over_rows(ple_w_proj[0])]
        blocks_b = gate_blocks(0)
        blocks_b += [over_d(b_w_q[0][:, 512 * h:512 * h + 512]) for h in range(2)]
        for h in range(2):
            blocks_b += [over_d(w_kv[:, a + 512 * h:a + 512 * h + 512]) for a in (0, D)]
        blocks_b += [over_rows(b_w_o[0][512 * j:512 * j + 512, :]) for j in range(2)]
        blocks_b += [over_rows(ple_w_proj[1])]
        blocks_c = gate_blocks(1)
        assert (len(blocks_a), len(blocks_b), len(blocks_c)) == (BLOCKS_A, BLOCKS_B, BLOCKS_C)
        place, uses, dense = {}, [0] * RING, []
        for phase, blocks in (("a", blocks_a), ("b", blocks_b), ("c", blocks_c)):
            for j in range(len(blocks)):
                s = j % DENSE_RING
                uses[s] += 1
                place[phase, j] = s, 16 * uses[s]
                if j != PROJ:
                    dense.append((phase, j))

        def slot_of(key, src=None):
            s = place[key][0]
            if src is None:
                return ring[:, s]
            return ring[:, s, 0:src.shape[1] * src.shape[2]].rearrange("p (c n) -> p c n", n=src.shape[2])

        QKV = ((0, 0), (1, 0), (0, 1), (0, 2), (1, 1), (1, 2))
        QKV_BANKS = (0, 2, 0, 2, 0, 0)

        def arrived(eng, key):
            s, value = place[key]
            eng.wait_ge(landed[s], value)

        def wait_used(eng, phase, j):
            if (phase, j) in dense:
                eng.wait_ge(lo_ready, PIECES * (dense.index((phase, j)) + 1))
            else:
                eng.wait_ge(proj_ps, 4 if phase == "a" else 8)

        def wait_product(eng, phase, j):
            if phase != "c" and j >= 8:
                eng.wait_ge(added, (3 if phase == "b" else 1) + j - 8)
            elif phase == "a":
                eng.wait_ge(pj_ps, 2 * j + 2)
            elif j < 2:
                eng.wait_ge(gate_ps, (4 if phase == "c" else 0) + 2 * j + 2)
            else:
                eng.wait_ge(qkv_ps, 2 * (j - 2) + 2)

        def high(act, key, pieces):
            n = dense.index(key)
            arrived(act, key)
            for u in pieces:
                k = PIECES * n + u
                m, v = divmod(k - SPLIT_BUFS, PIECES)
                if m >= 0 and v < PIECES - 1:
                    act.wait_ge(piece_used, (PIECES - 1) * m + v + 1)
                elif m >= 0:
                    wait_product(act, *dense[m])
                act.activation(w_hi[:, k % SPLIT_BUFS], ring[:, place[key][0], PIECE * u:PIECE * u + PIECE],
                               ACT.Copy).then_inc(hi_ready, 1)

        def low(pool, key):
            n = dense.index(key)
            for u in range(PIECES):
                k = PIECES * n + u
                pool.wait_ge(hi_ready, k + 1)
                pool.tensor_tensor(w_lo[:, k % SPLIT_BUFS], ring[:, place[key][0], PIECE * u:PIECE * u + PIECE],
                                   w_hi[:, k % SPLIT_BUFS].bitcast(F32), ALU.subtract).then_inc(lo_ready, 1)

        def bank3(b, m):
            return pb[:, b, :].rearrange("p (a n) -> p a n", n=m)

        def wide(ap, n):
            return ap.unsqueeze(len(ap.shape)).to_broadcast(list(ap.shape) + [n])

        block = ctx.enter_context(nc.Block())

        @block.sync
        def _(sp):
            def load(key, src):
                sp.dma_start(slot_of(key, src), src).then_inc(landed[place[key][0]], 16)

            def load_expert(layer, i, k):
                e = k // 3
                s = k % RING
                kind = expert_slots(e % BODY_E).index(s)
                if kind < 2:
                    w = (moe_w_gate, moe_w_up)[kind]
                    src = w[layer][i * BODY_E + e].rearrange("(p c) n -> p (c n)", c=NC)
                    dst = ring[:, s, :]
                else:
                    src = moe_w_down[layer][i * BODY_E + e].rearrange("(c p) n -> p c n", p=P)
                    dst = ring[:, s, :].rearrange("p (c n) -> p c n", c=4)
                sp.dma_start(dst, src).then_inc(moe_landed[layer][s], 16)

            def experts(layer, phase, blocks):
                rounds = sp.alloc_register(f"sp_rounds{layer}")
                sp.reg_mov(rounds, 1)
                with sp.Fori(0, rounds) as r:
                    sp.wait_ge(moe_freed[layer], r * EXPERTS + 1)
                    for j in range(len(blocks) - DENSE_RING, len(blocks)):
                        wait_used(sp, phase, j)
                        load_expert(layer, 0, place[phase, j][0])
                    if layer == 0:
                        sp.wait_ge(o_ps, 4)
                    else:
                        sp.wait_ge(s_ps, B_HEADS)
                    load_expert(layer, 0, DENSE_RING)
                    with sp.Fori(0, BODIES - 1) as i:
                        it = r * BODIES + i
                        for k in range(BODY_BLOCKS):
                            sp.wait_ge(moe_freed[layer], it * BODY_E + (k // 3 + 2))
                            load_expert(layer, i, k + RING)
                    for k in range(BODY_BLOCKS - RING):
                        sp.wait_ge(moe_freed[layer], r * EXPERTS + (EXPERTS - BODY_E + k // 3 + 2))
                        load_expert(layer, BODIES - 1, k + RING)
                    sp.wait_ge(rounds_ready[layer], 1)
                    sp.reg_load(rounds, rounds_i[0:1, layer:layer + 1])

            def after_experts(layer, phase, blocks):
                more = sp.value_load(more_i[0:1, layer:layer + 1], min_val=0, max_val=7)
                for j, src in enumerate(blocks):
                    if j < DENSE_RING:
                        done = EXPERTS - BODY_E + (BODY_BLOCKS - RING + place[phase, j][0]) // 3 + 2
                        sp.wait_ge(moe_freed[layer], more * EXPERTS + done)
                    else:
                        wait_used(sp, phase, j - DENSE_RING)
                    load((phase, j), src)

            sp.dma_start(xs[:], x[0].rearrange("(t p) d -> p t d", p=P)).then_inc(x_in, 16)
            sp.dma_start(rows[0:2 * A_HEADS, :], a_lb_logits.rearrange("r (h p) -> (r h) p", p=P)).then_inc(small_in, 16)
            sp.dma_start(rows[2 * A_HEADS:3 * A_HEADS, :], a_out_norm[0].rearrange("(h p) -> h p", p=P)).then_inc(small_in, 16)
            for n, g in ((G_MIX0, norm_mix), (G_FFN0, norm_ffn), (G_PLE0, norm_ple)):
                sp.dma_start(gains[:, n:n + 2, :], g.rearrange("r (p c) -> p r c", c=NC)).then_inc(small_in, 16)
            sp.dma_start(gains[:, G_KV, :], kv_norm.rearrange("(p c) -> p c", c=NC)).then_inc(small_in, 16)
            for j, src in enumerate(blocks_a):
                if j >= DENSE_RING:
                    wait_used(sp, "a", j - DENSE_RING)
                load(("a", j), src)
            experts(0, "a", blocks_a)
            after_experts(0, "b", blocks_b)
            experts(1, "b", blocks_b)
            after_experts(1, "c", blocks_c)
            for t in range(NT):
                sp.wait_ge(fin_ready, t + 1)
                sp.dma_start(out[0].rearrange("(t p) d -> p t d", p=P)[:, t], fin[:, t]).then_inc(out_done, 16)
            sp.wait_ge(out_done, 16 * NT)

        @block.gpsimd
        def _(pool):
            step = Count(pool, pool_step)
            for m, value in ((ident, 0.0), (flip, 0.0), (ones, 1.0), (before, 1.0)):
                pool.memset(m[:], value).then_inc(pool_step, 1)
            pool.iota(iota_i[:], pattern=[[1, SLOTS]], base=0, channel_multiplier=0).then_inc(pool_step, 1)
            pool.iota(thresh_i[:], pattern=[[SLOTS, SEQ // SLOTS - 1]], base=SLOTS,
                      channel_multiplier=0).then_inc(pool_step, 1)
            step.n = 6
            step.link(pool.memset(causal[:], 1.0))
            pool.affine_select(out=ident[:], in_=ident[:], compare_op=ALU.not_equal, fill=1.0, base=0,
                               pattern=[[-1, P]], channel_multiplier=1).then_inc(const_ready, 1)
            pool.affine_select(out=flip[:], in_=flip[:], compare_op=ALU.not_equal, fill=1.0, base=1 - P,
                               pattern=[[1, P]], channel_multiplier=1).then_inc(const_ready, 1)
            pool.affine_select(out=before[:], in_=before[:], compare_op=ALU.is_gt, fill=0.0, base=0,
                               pattern=[[1, P]], channel_multiplier=-1).then_inc(const_ready, 1)
            pool.tensor_copy(iota[:], iota_i[:]).then_inc(const_ready, 1)
            pool.tensor_copy(thresh[:], thresh_i[:]).then_inc(const_ready, 1)
            step.link(pool.affine_select(out=causal[:], in_=causal[:], compare_op=ALU.is_ge, fill=0.0,
                                         base=0, pattern=[[1, P]], channel_multiplier=-1))
            pool.affine_select(out=causal[:, CHUNK:], in_=causal[:, CHUNK:], compare_op=ALU.is_ge, fill=0.0,
                               base=-CHUNK, pattern=[[0, CHUNK]], channel_multiplier=1).then_inc(const_ready, 1)
            for la in range(2):
                pool.memset(more_i[:, la:la + 1], 0).then_inc(moe_freed[la], 1)
            pool.memset(view(1024, 1536), 0.0).then_inc(zeroed, 1)
            pool.memset(view(3584, 1024), 0.0).then_inc(zeroed, 1)
            for key in dense[:BLOCKS_A - 1]:
                low(pool, key)
            pool.wait_ge(small_in, 16 * 6)
            pool.wait_ge(route_in, 16 * 8)
            for la, gain in enumerate((G_FFN0, G_FFN1)):
                pool.tensor_tensor(w_route[:, la], w_route[:, la], wide(gains[:, gain], ROUTES),
                                   ALU.mult).then_inc(wroute_ready, 1)

            def normalise(layer):
                pool.wait_ge(tr_ps, 4 * (1 + 4 * layer) + 4)
                pool.wait_ge(rstd_ready, 2 + 3 * layer)
                for t in range(NT):
                    pool.tensor_scalar(hn[:, t], hn[:, t], rstd[:, t:t + 1], None, ALU.mult).then_inc(normed, 1)

            normalise(0)
            pool.wait_ge(sq_done, 6)
            pool.memset(bias[0:CHUNK, :, 0:CHUNK], MASKED).then_inc(bias_mask, 1)
            for key in dense[BLOCKS_A - 1:BLOCKS_A + BLOCKS_B - 2]:
                low(pool, key)
            normalise(1)
            for key in dense[BLOCKS_A + BLOCKS_B - 2:]:
                low(pool, key)

        @block.scalar
        def _(act):
            for la in range(2):
                act.dma_start(w_route[:, la, :, 0:GROUPS], over_d(moe_w_group[la])).then_inc(route_in, 16)
                act.dma_start(w_route[:, la, :, GROUPS:], over_d(moe_w_expert[la])).then_inc(route_in, 16)
                act.dma_start(b_route[:, la, 0:GROUPS], moe_b_group[la].partition_broadcast(P)).then_inc(route_in, 16)
                act.dma_start(b_route[:, la, GROUPS:], moe_b_expert[la].partition_broadcast(P)).then_inc(route_in, 16)

            def norm(n, src):
                squares(src, hn[:].rearrange("p t c q -> p t (c q)"))
                roots(n)

            def squares(src, dump, ready=None):
                for t in range(NT):
                    if ready:
                        ready(t)
                    act.activation(dump[:, t], src[:, t], ACT.Square,
                                   accum_out=ssq[:, t:t + 1]).then_inc(sq_done, 1)

            def plain(n):
                act.activation(hn[:, 1], acc[:, 1].rearrange("p (q c) -> p c q", c=NC), ACT.Copy).then_inc(hn_ready, 1)
                act.wait_ge(hn_ready, 2 * n + 2)
                squares(hn[:].rearrange("p t c q -> p t (c q)"), dump)

            def roots(n):
                act.wait_ge(ms_ready, n + 1)
                act.activation(root[:], ms[:], ACT.Sqrt).then_inc(root_ready, 1)

            act.wait_ge(x_in, 16)
            norm(0, xs)
            act.wait_ge(lb_ready, 1)
            act.activation(lb[:, 2:4, :], lb[:, 2:4, :], ACT.Exp).then_inc(lbe, 1)

            def gates_f(h):
                for b in range(2):
                    act.wait_ge(pj_ps, 8 * h + b + 1)
                    act.activation(t_key[:, BANK * b:BANK * b + BANK], pb[:, b, :], ACT.Sigmoid).then_inc(sig_done, 1)

            def decay_exps(h):
                act.wait_ge(f_ready, h + 1)
                act.activation(t_log, t_key, ACT.Ln).then_inc(ln_done, 1)
                high(act, ("a", 4 * h + 1), REST)
                act.wait_ge(cum_ready, h + 1)
                act.activation(t_exp, t_cum, ACT.Exp).then_inc(exp_done, 1)
                act.activation(k_inv, t_cum, ACT.Exp, scale=-1.0).then_inc(exp_done, 1)
                act.wait_ge(tail_ready, h + 1)
                act.activation(t_log, t_log, ACT.Exp).then_inc(exp_done, 1)

            def values(h):
                high(act, ("a", 4 * h + 3), FIRST)
                for t in range(NT):
                    act.wait_ge(pj_ps, 8 * h + 5 + t)
                    act.activation(v_tok[:, t], pb[:, 1 + t, :], ACT.Copy).then_inc(v_ready, 1)
                high(act, ("a", 4 * h + 3), REST)
                high(act, ("a", 4 * h + 4), FIRST)
                for t in range(NT):
                    act.wait_ge(pj_ps, 8 * h + 7 + t)
                    if h:
                        act.wait_ge(o_ready, t + 1)
                    act.activation(og_tok[:, t], bank3((3, 0)[t], P), ACT.Silu).then_inc(og_ready, 1)

            def keys_tail(h):
                act.wait_ge(kt_ps, 2 * h + 1)
                if h == 0:
                    act.wait_ge(zeroed, 1)
                act.activation(k_tail[0:64, 0], bank3(0, P)[0:64], ACT.Copy).then_inc(kt_ready, 1)
                act.activation(k_tail[64:128, 1], bank3(0, P)[64:128], ACT.Copy).then_inc(kt_ready, 1)
                act.wait_ge(kt_ps, 2 * h + 2)
                act.activation(k_tail[0:64, 2], bank3(1, P)[0:64], ACT.Copy).then_inc(kt_ready, 1)

            def out_squares(h):
                act.wait_ge(ktail_ready, 2)
                for t in range(NT):
                    act.wait_ge(o_ps, 2 * h + t + 1)
                    act.activation(o_sq[:, BANK * t:BANK * t + BANK], pb[:, (3, 0)[t], :],
                                   ACT.Square).then_inc(osq_done, 1)
                act.wait_ge(oms_ready, h + 1)
                act.activation(o_small[:, 1], o_small[:, 0], ACT.Sqrt).then_inc(oroot_ready, 1)

            high(act, ("a", 0), range(PIECES))
            high(act, ("a", 1), FIRST)
            gates_f(0)
            decay_exps(0)
            high(act, ("a", 2), range(PIECES))
            values(0)
            keys_tail(0)
            high(act, ("a", 4), REST)
            high(act, ("a", 5), FIRST)
            gates_f(1)
            decay_exps(1)
            high(act, ("a", 6), FIRST)
            out_squares(0)
            high(act, ("a", 6), REST)
            values(1)
            keys_tail(1)
            high(act, ("a", 8), REST)
            high(act, ("a", 9), FIRST)
            out_squares(1)
            high(act, ("a", 9), REST)

            def projected(layer, j):
                for t in range(NT):
                    act.wait_ge(proj_ps, 4 * layer + 2 * j + t + 1)
                    act.activation(xs[:, t, BANK * j:BANK * j + BANK], pb[:, 2 + t, :], ACT.Copy).then_inc(pp_ready, 1)

            def moe(layer):
                act.wait_ge(added, 2 * layer + 2)
                act.dma_start(p_tok, p[layer, 0].rearrange("(t q) m -> q t m", q=P)).then_inc(p_in, 16)
                plain(1 + 3 * layer)
                stage = 1 + 4 * layer
                for j in range(2):
                    act.wait_ge(tr_ps, 4 * stage + 2 * j + 2)
                    act.activation(routeT[:, 4 * j:4 * j + 4, P:2 * P], bank3(2 + j, P), ACT.Copy).then_inc(ht_ready, 1)
                roots(1 + 3 * layer)
                act.wait_ge(pt_ps, layer + 1)
                act.activation(pT.rearrange("p k s -> p (k s)"), pb[:, 1, :], ACT.Copy).then_inc(pt_ready, 1)
                act.wait_ge(dif_ready[layer], 1)
                act.activation(g_exp, g_dif, ACT.Exp).then_inc(rexp_done[layer], 1)
                projected(layer, 0)
                act.wait_ge(dif_ready[layer], 2)
                act.activation(top_x, top_d, ACT.Exp).then_inc(rexp_done[layer], 1)
                projected(layer, 1)
                act.wait_ge(rounds_ready[layer], 1)
                rounds = act.value_load(rounds_i[0:1, layer:layer + 1], min_val=1, max_val=8)
                with act.Fori(0, rounds) as r:
                    with act.Fori(0, BODIES) as i:
                        it = r * BODIES + i
                        for b in range(BATCHES):
                            act.wait_ge(pgt_ps[layer], it * BATCHES + (b + 1))
                            act.activation(pick_gT, pb[:, 3, 256:512], ACT.Copy).then_inc(pgt_ready[layer], 1)
                            for e in range(BATCH_E * b, BATCH_E * b + BATCH_E):
                                act.wait_ge(h_ps[layer], it * BODY_E + (e + 1))
                                act.activation(silu, pb[:, 2, 0:P], ACT.Silu).then_inc(silu_done[layer], 1)
                                act.wait_ge(hidT_ps[layer], it * BODY_E + (e + 1))
                                act.activation(hidT, pb[:, 2, 256:384], ACT.Copy).then_inc(hidT_ready[layer], 1)
                                at = SLOTS * (e % BATCH_E)
                                act.wait_ge(y_ps[layer], it * BODY_E + (e + 1))
                                for g, done in ((0, moe_freed), (1, y_act)):
                                    act.activation(y_sb[at:at + SLOTS, 256 * g:256 * g + 256],
                                                   pb[SLOTS * g:SLOTS * g + SLOTS, 3, 0:256],
                                                   ACT.Copy).then_inc(done[layer], 1)
                high(act, ("bc"[layer], 0), FIRST)
                act.wait_ge(scat_done[layer], rounds * (BODIES * BATCHES))
                plain(2 + 3 * layer)
                roots(2 + 3 * layer)
                if layer == 0:
                    rel = b_rel_bias[0]
                    act.dma_start(bias[CHUNK:P], bass.AP(tensor=rel.tensor, offset=rel.offset,
                                  ap=[[1, CHUNK], [N_REL, B_HEADS], [1, SEQ]])).then_inc(late_in, 16)
                    act.dma_start(bias[0:CHUNK, :, CHUNK:], bass.AP(tensor=rel.tensor, offset=rel.offset,
                                  ap=[[1, CHUNK], [N_REL, B_HEADS], [1, SEQ - CHUNK]])).then_inc(late_in, 16)
                else:
                    act.dma_start(fin_gain, final_norm.partition_broadcast(P)).then_inc(late_in, 16)

            def embed(layer):
                phase = "bc"[layer]
                high(act, (phase, 0), REST)
                high(act, (phase, 1), FIRST)
                for j in range(2):
                    for t in range(NT):
                        n = 4 * layer + 2 * j + t
                        act.wait_ge(gate_ps, n + 1)
                        if j:
                            act.wait_ge(xs_ready, n - 1)
                        act.wait_ge(rstd_ready, 3 + 3 * layer)
                        act.activation(sig[:, t], pb[:, 2 * j + t, :], ACT.Sigmoid,
                                       scale=rstd[:, t:t + 1]).then_inc(sig_ready, 1)
                    if j == 0:
                        high(act, (phase, 1), REST)
                if layer == 0:
                    high(act, ("b", 2), FIRST)
                squares(xs, hn[:].rearrange("p t c q -> p t (c q)"),
                        lambda t: act.wait_ge(xs_ready, 4 * layer + 3 + t))
                roots(3 + 3 * layer)

            moe(0)
            embed(0)

            def qkv(n):
                h, kind = QKV[n]
                first = QKV_BANKS[n]
                for b in range(2):
                    dst = (qT[h], kT[h], v_rev)[kind]
                    dst = dst[:, b] if kind == 2 else dst[:, 2 * b:2 * b + 2].rearrange("p j t -> p (j t)")
                    act.wait_ge(qkv_ps, 2 * n + b + 1)
                    act.activation(dst, pb[:, first + b, :], ACT.Copy,
                                   scale=ATTN_SCALE if kind == 0 else 1.0).then_inc(qkv_ready, 1)

            def exps(n):
                act.wait_ge(s_ready, n + 1)
                if n >= 2:
                    act.wait_ge(pT_ps, n - 1)
                for t, (a, b) in ((1, (0, 256)), (0, (256, 384))):
                    last = act.activation(probs[n % 2][:, a:b], score[n % 2][:, a:b], ACT.Exp,
                                          bias=s_neg[:, n, t:t + 1], accum_out=s_sum[:, n, t:t + 1])
                last.then_inc(e_ready, 1)

            high(act, ("b", 2), REST)
            for n in range(5):
                high(act, ("b", 3 + n), FIRST)
                qkv(n)
                if n < 4:
                    high(act, ("b", 3 + n), REST)
            for n in range(HALF_B):
                exps(n)
            high(act, ("b", 7), REST)
            high(act, ("b", 8), FIRST)
            qkv(5)
            high(act, ("b", 8), REST)
            high(act, ("b", 9), FIRST)
            for n in range(HALF_B, B_HEADS):
                exps(n)
            high(act, ("b", 9), REST)
            moe(1)
            embed(1)

        @block.vector
        def _(dve):
            step = Count(dve, dve_step)

            def mean_square(n):
                dve.wait_ge(sq_done, 2 * n + 2)
                dve.tensor_scalar(ms[:], ssq[:], 1.0 / D, EPS, ALU.mult, ALU.add).then_inc(ms_ready, 1)

            def inverse_root(n):
                dve.wait_ge(root_ready, n + 1)
                dve.reciprocal(rstd[:], root[:]).then_inc(rstd_ready, 1)
                dve.wait_ge(rstd_ready, n + 1)

            def plain(n):
                dve.tensor_copy(hn[:, 0], acc[:, 0].rearrange("p (q c) -> p c q", c=NC)).then_inc(hn_ready, 1)

            def norm(n, src, write=True):
                mean_square(n)
                inverse_root(n)
                for t in range(NT if write else 0):
                    dve.tensor_scalar(hn[:, t], src[:, t].rearrange("p (q c) -> p c q", c=NC),
                                      rstd[:, t:t + 1], None, ALU.mult).then_inc(hn_ready, 1)

            def split(bank, hi, lo, gain=None):
                if gain is None:
                    step.link(dve.tensor_copy(hi, bank))
                    return dve.tensor_tensor(lo, bank, hi.bitcast(F32), ALU.subtract)
                step.link(dve.tensor_tensor(hi, bank, wide(gain, P), ALU.mult))
                for c in range(4):
                    last = dve.scalar_tensor_tensor(out=lo[:, c], in0=bank[:, c], scalar=gain[:, c:c + 1],
                                                    in1=hi[:, c].bitcast(F32), op0=ALU.mult, op1=ALU.subtract)
                return last

            def transposed(stage, gain, swap=False):
                for j in range(2):
                    for t in range(NT):
                        dve.wait_ge(tr_ps, 4 * stage + 2 * j + t + 1)
                        to = P * (NT - 1 - t if swap else t)
                        at = slice(4 * j, 4 * j + 4), slice(to, to + P)
                        g = gains[:, gain, 4 * j:4 * j + 4]
                        split(bank3(2 * t + j, P), hT_hi[:, at[0], at[1]], hT_lo[:, at[0], at[1]],
                              g).then_inc(ht_ready, 1)

            dve.wait_ge(cols_ps, 1)
            step.link(dve.tensor_copy(cols[:], pb[:, 3, 0:3 * A_HEADS]))
            step.link(dve.tensor_tensor(lb[:, 0], cols[:, 0:A_HEADS], cols[:, A_HEADS:2 * A_HEADS], ALU.max))
            step.link(dve.tensor_tensor(lb[:, 2:4], cols[:, 0:2 * A_HEADS].rearrange("p (r h) -> p r h", r=2),
                                        lb[:, 0].unsqueeze(1).to_broadcast([P, 2, A_HEADS]), ALU.subtract))
            dve.tensor_copy(lb[:, 1], lb[:, 0]).then_inc(lb_ready, 1)
            norm(0, xs)
            dve.wait_ge(small_in, 16 * 6)
            transposed(0, G_MIX0)
            dve.wait_ge(lbe, 1)
            step.link(dve.tensor_tensor(lb[:, 1], lb[:, 2], lb[:, 3], ALU.add))
            step.link(dve.reciprocal(lb[:, 0], lb[:, 1]))
            step.link(dve.tensor_tensor(lb[:, 0], lb[:, 0], lb[:, 2], ALU.mult))
            step.link(dve.tensor_scalar(lb[:, 1], lb[:, 0], -1.0, 1.0, ALU.mult, ALU.add))
            dve.wait_ge(const_ready, 6)

            def forget(h):
                dve.wait_ge(sig_done, 2 * h + 2)
                for j in range(HALF_A):
                    hd = HALF_A * h + j
                    part = t_key[:, SEQ * j:SEQ * j + SEQ]
                    last = dve.tensor_scalar(part, part, lb[:, 1, hd:hd + 1], lb[:, 0, hd:hd + 1], ALU.mult, ALU.add)
                last.then_inc(f_ready, 1)

            def decays(h):
                dve.wait_ge(ln_done, h + 1)
                for n in range(HALF_A * SEQ // CHUNK):
                    part = slice(CHUNK * n, CHUNK * n + CHUNK)
                    last = dve.tensor_tensor_scan(t_cum[:, part], ones[:, 0:CHUNK], t_log[:, part], 0.0,
                                                  ALU.mult, ALU.add)
                last.then_inc(cum_ready, 1)
                dve.wait_ge(cum_ready, h + 1)
                g3 = t_cum.rearrange("p (n s) -> p n s", s=CHUNK)
                dve.tensor_tensor(t_log.rearrange("p (n s) -> p n s", s=CHUNK), wide(g3[:, :, CHUNK - 1], CHUNK),
                                  g3, ALU.subtract).then_inc(tail_ready, 1)
                step.link(dve.tensor_scalar(t_key, t_key, -1.0, 1.0, ALU.mult, ALU.add))
                dve.wait_ge(exp_done, 3 * h + 2)
                dve.tensor_tensor(k_inv, k_inv, t_key, ALU.mult).then_inc(kinv_ready, 1)
                e4 = t_exp.rearrange("p (j n s) -> p n j s", j=HALF_A, s=CHUNK)
                step.link(dve.tensor_copy(dl[:, h], e4[:, 1:3, :, CHUNK - 1]))
                dve.wait_ge(exp_done, 3 * h + 3)
                dve.tensor_tensor(t_log, t_log, t_key, ALU.mult).then_inc(ktail_ready, 1)

            def queries(h):
                for b in range(2):
                    dve.wait_ge(pj_ps, 8 * h + 3 + b)
                    dve.tensor_tensor(q_dec[h][:, 2 * b:2 * b + 2].rearrange("p j t -> p (j t)"),
                                      pb[:, (2, 3)[b] if h == 0 else (1, 2)[b], :],
                                      t_exp[:, BANK * b:BANK * b + BANK], ALU.mult).then_inc(qdec_ready, 1)

            def causal_att(h):
                if h == 0:
                    dve.wait_ge(zeroed, 2)
                mask = causal[:].bitcast(I32).unsqueeze(1).to_broadcast([P, HALF_A, P])
                for t in range(NT):
                    dve.wait_ge(at_ps, 2 * h + t + 1)
                    dve.copy_predicated(att_m[:, t], mask, bank3(2 + t, P)).then_inc(at_ready, 1)

            def chunk_states(h):
                dve.wait_ge(kv_ps, 3 * h + 1)
                dve.tensor_copy(states[:, 0], bank3(2, P)).then_inc(st_ready, 1)
                for n, b in ((1, 3), (2, 0)):
                    dve.wait_ge(st_ready, 3 * h + n)
                    step.link(dve.tensor_tensor(states[:, n], states[:, n - 1], wide(dl[:, h, n - 1], P), ALU.mult))
                    dve.wait_ge(kv_ps, 3 * h + n + 1)
                    dve.tensor_tensor(states[:, n], states[:, n], bank3(b, P), ALU.add).then_inc(st_ready, 1)

            def head_norm(h):
                dve.wait_ge(osq_done, 2 * h + 2)
                step.link(dve.tensor_reduce(o_small[:, 2], o_sq.rearrange("p (m e) -> p m e", e=P), AX, ALU.add))
                dve.tensor_scalar(o_small[:, 0], o_small[:, 2], 1.0 / P, EPS, ALU.mult, ALU.add).then_inc(oms_ready, 1)
                dve.wait_ge(oroot_ready, h + 1)
                step.link(dve.reciprocal(o_small[:, 2], o_small[:, 1]))
                for t in range(NT):
                    dve.wait_ge(og_ready, 2 * h + t + 1)
                    step.link(dve.tensor_tensor(og_tok[:, t], og_tok[:, t],
                                                wide(o_small[:, 2, 4 * t:4 * t + 4], P), ALU.mult))
                    dve.tensor_tensor(hn[:, t, HALF_A * h:HALF_A * h + HALF_A], bank3((3, 0)[t], P),
                                      og_tok[:, t], ALU.mult).then_inc(o_ready, 1)

            def mixed(h, first_bank, gain):
                for t in range(NT):
                    dve.wait_ge(ot_ps, 2 * h + t + 1)
                    k = 4 * (h % 2)
                    at = slice(k, k + 4), slice(P * t, P * t + P)
                    g = cols[:, 2 * A_HEADS + k:2 * A_HEADS + k + 4] if gain else None
                    split(bank3(first_bank + t, P), hT_hi[:, at[0], at[1]], hT_lo[:, at[0], at[1]],
                          g).then_inc(ot_ready, 1)

            forget(0)
            decays(0)
            queries(0)
            causal_att(0)
            forget(1)
            chunk_states(0)
            decays(1)
            queries(1)
            head_norm(0)
            mixed(0, 1, True)
            causal_att(1)
            chunk_states(1)
            head_norm(1)
            mixed(1, 1, True)

            def first_hot(hot, dif, eq, cum):
                step.link(dve.tensor_scalar(eq, dif, 0.0, None, ALU.is_equal))
                m = eq.shape[2]
                for t in range(NT):
                    last = dve.tensor_tensor_scan(cum[:, t], ones[:, 0:m], eq[:, t], 0.0, ALU.mult, ALU.add)
                    step.link(last)
                step.link(dve.scalar_tensor_tensor(out=hot, in0=cum, scalar=1.0, in1=eq, op0=ALU.is_equal,
                                                   op1=ALU.mult))

            def moe(layer):
                dve.wait_ge(added, 2 * layer + 2)
                plain(1 + 3 * layer)
                stage = 1 + 4 * layer
                for j in range(2):
                    dve.wait_ge(tr_ps, 4 * stage + 2 * j + 1)
                    dve.tensor_copy(routeT[:, 4 * j:4 * j + 4, 0:P], bank3(j, P)).then_inc(ht_ready, 1)
                mean_square(1 + 3 * layer)
                inverse_root(1 + 3 * layer)
                dve.wait_ge(route_in, 16 * 8)
                dve.wait_ge(lg_ps[layer], 1)
                for t in range(NT):
                    last = dve.scalar_tensor_tensor(out=logit[:, t], in0=pb[:, 0, 64 * t:64 * t + ROUTES],
                                                    scalar=rstd[:, t:t + 1], in1=b_route[:, layer],
                                                    op0=ALU.mult, op1=ALU.add)
                step.link(last)
                lg, le = logit[:, :, 0:GROUPS], logit[:, :, GROUPS:]

                def spread(v, m):
                    return v.to_broadcast([P, NT, m])

                step.link(dve.tensor_reduce(g_max[:, :, 0], lg, AX, ALU.max))
                step.link(dve.tensor_tensor(g_dif, lg, spread(g_max, GROUPS), ALU.subtract))
                step.link(dve.tensor_copy(e_log, le))
                dve.tensor_copy(e_cum, le).then_inc(dif_ready[layer], 1)
                first_hot(g_hot, g_dif, g_eq, g_cum)
                step.link(dve.tensor_scalar(g_pen, g_hot, -1.0, -MASKED, ALU.add, ALU.mult))
                e4 = e_log.rearrange("p t (g e) -> p t g e", g=GROUPS)
                step.link(dve.tensor_tensor(e4, e4, wide(g_pen, PER_GROUP), ALU.add))
                step.link(dve.tensor_reduce(top1[:, :, 0], e_log, AX, ALU.max))
                step.link(dve.tensor_tensor(e_dif, e_log, spread(top1, EXPERTS), ALU.subtract))
                first_hot(hot1, e_dif, e_eq, e_cum)
                step.link(dve.scalar_tensor_tensor(out=e_log, in0=hot1, scalar=1e5 * MASKED, in1=e_log,
                                                   op0=ALU.mult, op1=ALU.add))
                step.link(dve.tensor_reduce(top2[:, :, 0], e_log, AX, ALU.max))
                step.link(dve.tensor_tensor(e_dif, e_log, spread(top2, EXPERTS), ALU.subtract))
                dve.tensor_tensor(top_d, top2, top1, ALU.subtract).then_inc(dif_ready[layer], 1)
                first_hot(hot2, e_dif, e_eq, e_cum)
                dve.tensor_tensor(chosen, hot1, hot2, ALU.add).then_inc(chosen_ready[layer], 1)
                dve.wait_ge(rexp_done[layer], 2)
                step.link(dve.tensor_reduce(g_sum[:, :, 0], g_exp, AX, ALU.add))
                step.link(dve.reciprocal(g_w, g_sum))
                step.link(dve.tensor_scalar(top_s, top_x, 1.0, None, ALU.add))
                step.link(dve.reciprocal(w_1, top_s))
                step.link(dve.tensor_tensor(w_1, w_1, g_w, ALU.mult))
                step.link(dve.tensor_tensor(w_2, w_1, top_x, ALU.mult))
                step.link(dve.tensor_tensor(hot1, hot1, spread(w_1, EXPERTS), ALU.mult))
                step.link(dve.tensor_tensor(hot2, hot2, spread(w_2, EXPERTS), ALU.mult))
                step.link(dve.tensor_tensor(gate, hot1, hot2, ALU.add))
                dve.wait_ge(rk_ps[layer], 1)
                ranks = pb[:, 1, 0:2 * EXPERTS].rearrange("p (t e) -> p t e", t=NT)
                step.link(dve.scalar_tensor_tensor(out=rank, in0=ranks, scalar=1.0, in1=chosen, op0=ALU.add,
                                                   op1=ALU.mult))
                step.link(dve.tensor_scalar(rank, rank, -1.0, None, ALU.add))
                step.link(dve.tensor_reduce(most, pb[:, 1, 2 * EXPERTS:3 * EXPERTS], AX, ALU.max))
                step.link(dve.tensor_scalar(over, thresh[:], most, None, ALU.is_lt))
                step.link(dve.tensor_reduce(n_over, over, AX, ALU.add))
                step.link(dve.tensor_copy(more_i[:, layer:layer + 1], n_over))
                dve.tensor_scalar(rounds_i[:, layer:layer + 1], n_over, 1.0, None,
                                  ALU.add).then_inc(rounds_ready[layer], 1)
                dve.wait_ge(rounds_ready[layer], 1)
                rounds = dve.value_load(rounds_i[0:1, layer:layer + 1], min_val=1, max_val=8)
                gain = gains[:, (G_FFN0, G_FFN1)[layer]]
                links = 2 + BATCHES
                with dve.Fori(0, rounds) as r:
                    with dve.Fori(0, BODIES) as i:
                        it = r * BODIES + i
                        body = Count(dve, dve_loop[layer], r * (BODIES * links + 1) + i * links)
                        body.link(dve.tensor_copy(rank8, rank[:, :, bass.ds(i * BODY_E, BODY_E)]))
                        body.link(dve.tensor_copy(gate8, gate[:, :, bass.ds(i * BODY_E, BODY_E)]))
                        for b in range(BATCHES):
                            part = slice(BATCH_E * b, BATCH_E * b + BATCH_E)
                            for t in range(NT):
                                last = dve.tensor_tensor(
                                    pick[:, t], wide(rank8[:, t, part], SLOTS),
                                    iota[:].unsqueeze(1).to_broadcast([P, BATCH_E, SLOTS]), ALU.is_equal)
                            body.link(last)
                            for t in range(NT):
                                last = dve.tensor_tensor(pick_g[:, t], pick[:, t],
                                                         wide(gate8[:, t, part], SLOTS), ALU.mult)
                            last.then_inc(pick_ready[layer], 1)
                            for j in range(2):
                                dve.wait_ge(xg_ps[layer], it * (2 * BATCHES) + (2 * b + j + 1))
                                dve.tensor_tensor(xg[:, 4 * j:4 * j + 4], bank3(j, P),
                                                  wide(gain[:, 4 * j:4 * j + 4], P),
                                                  ALU.mult).then_inc(xg_ready[layer], 1)
                            for e in range(BATCH_E * b, BATCH_E * b + BATCH_E):
                                dve.wait_ge(silu_done[layer], it * BODY_E + (e + 1))
                                dve.tensor_tensor(hid, silu, pb[:, 2, P:2 * P],
                                                  ALU.mult).then_inc(hid_ready[layer], 1)
                                at = SLOTS * (e % BATCH_E)
                                dve.wait_ge(y_ps[layer], it * BODY_E + (e + 1))
                                for g in range(2, COLS):
                                    last = dve.tensor_copy(y_sb[at:at + SLOTS, 256 * g:256 * g + 256],
                                                           pb[SLOTS * g:SLOTS * g + SLOTS, 3, 0:256])
                                last.then_inc(y_dve[layer], 1)
                    after = Count(dve, dve_loop[layer], (r + 1) * (BODIES * links + 1) - 1)
                    after.link(dve.tensor_scalar(rank, rank, -float(SLOTS), None, ALU.add))
                dve.wait_ge(scat_done[layer], rounds * (BODIES * BATCHES))
                plain(2 + 3 * layer)
                transposed(2 + 4 * layer, (G_PLE0, G_PLE1)[layer])
                mean_square(2 + 3 * layer)
                inverse_root(2 + 3 * layer)

            def embed(layer):
                dve.wait_ge(pp_ready, 4 * layer + 4)
                for j in range(2):
                    for t in range(NT):
                        n = 4 * layer + 2 * j + t
                        half = slice(BANK * j, BANK * j + BANK)
                        dve.wait_ge(sig_ready, n + 1)
                        step.link(dve.tensor_tensor(sig[:, t], sig[:, t], xs[:, t, half], ALU.mult))
                        dve.tensor_tensor(xs[:, t, half], sig[:, t], acc[:, t, half], ALU.add).then_inc(xs_ready, 1)

            moe(0)
            embed(0)
            norm(3, xs)
            transposed(3, G_MIX1)
            dve.wait_ge(qkv_ps, 4)
            transposed(4, G_KV, swap=True)

            def scores(n):
                dve.wait_ge(s_ps, n + 1)
                if n >= 2:
                    dve.wait_ge(e_ready, n - 1)
                for t, (a, b) in ((1, (0, 256)), (0, (256, 384))):
                    last = dve.tensor_tensor_reduce(score[n % 2][:, a:b], pb[:, n % 2, a:b], bias[:, n, 0:b - a],
                                                    1.0, -3.0e38, ALU.add, ALU.max, s_max[:, n, t:t + 1])
                    step.link(last)
                dve.tensor_scalar(s_neg[:, n], s_max[:, n], -1.0, None, ALU.mult).then_inc(s_ready, 1)

            def turned(n):
                dve.wait_ge(pT_ps, n + 1)
                dve.tensor_copy(probsT[n % 2], pb[:, 2, 0:384]).then_inc(pT_ready, 1)

            def attended(n):
                hs = slice(n - 3, n + 1)
                step.link(dve.reciprocal(s_rec[:, hs], s_sum[:, hs]))
                dve.wait_ge(oa_ps, n // 4 + 1)
                o = hn[:].rearrange("p t c (u e) -> p (c u) t e", u=2)[:, hs]
                dve.tensor_tensor(o, pb[:, 3, :].rearrange("p (h t e) -> p h t e", h=4, t=NT),
                                  wide(s_rec[:, hs], B_DIM), ALU.mult).then_inc(oa_ready, 1)

            dve.wait_ge(late_in, 32)
            dve.wait_ge(bias_mask, 1)
            for h in range(2):
                base = HALF_B * h
                scores(base)
                for n in range(base, base + HALF_B):
                    if n + 1 < base + HALF_B:
                        scores(n + 1)
                    turned(n)
                    if n % 4 == 0 and n > base:
                        attended(n - 1)
                attended(base + HALF_B - 1)
                mixed(2 + h, 2, False)
            moe(1)
            embed(1)
            norm(6, xs, write=False)
            dve.wait_ge(late_in, 48)
            for t in range(NT):
                dve.scalar_tensor_tensor(out=fin[:, t], in0=xs[:, t], scalar=rstd[:, t:t + 1], in1=fin_gain,
                                         op0=ALU.mult, op1=ALU.mult).then_inc(fin_ready, 1)

        @block.tensor
        def _(pe):
            def inject():
                for t in range(NT):
                    for j in range(2):
                        half = slice(BANK * j, BANK * j + BANK)
                        pe.matmul(acc[:, t, half], ident[:], xs[:, t, half], start=True, stop=True)

            def transposes(stage, n, turn=None, after=None):
                for j in range(2):
                    for t in range(NT):
                        pe.wait_ge(hn_ready, 2 * n + (2 if n in PLAIN else t + 1))
                        if after:
                            after(t, j)
                        for c in range(4):
                            to = pb[:, 2 * t + j, P * c:P * c + P]
                            if turn is None:
                                last = pe.transpose(to, hn[:, t, 4 * j + c], ident[:])
                            else:
                                last = pe.matmul(to, hn[:, t, 4 * j + c], turn[:], start=True, stop=True)
                        last.then_inc(tr_ps, 1)

            def parts(key, u):
                k = PIECES * dense.index(key) + u
                pe.wait_ge(lo_ready, k + 1)
                at = k % SPLIT_BUFS
                return ((w_hi[:, at], hT_hi), (w_hi[:, at], hT_lo), (w_lo[:, at], hT_hi))

            def by_feature(key, banks, free):
                for b in range(2):
                    free(b)
                for c in range(NC):
                    three = parts(key, c)
                    for m in range(4):
                        for n, (w, x_t) in enumerate(three):
                            last = pe.matmul(pb[:, banks[m // 2], SEQ * (m % 2):SEQ * (m % 2) + SEQ],
                                             w[:, P * m:P * m + P], x_t[:, c],
                                             start=c == 0 and m % 2 == 0 and n == 0,
                                             stop=c == NC - 1 and n == 2, skip_group_check=True)
                        if c == NC - 1 and m == 1:
                            yield last
                    if c < NC - 1:
                        last.then_inc(piece_used, 1)
                yield last

            def by_token(key, banks, free):
                for t in range(NT):
                    free(t)
                for c in range(NC):
                    three = parts(key, c)
                    for t in range(NT):
                        for n, (w, x_t) in enumerate(three):
                            last = pe.matmul(pb[:, banks[t], :], x_t[:, c, P * t:P * t + P], w,
                                             start=c == 0 and n == 0, stop=c == NC - 1 and n == 2)
                        if c == NC - 1 and t == 0:
                            yield last
                    if c < NC - 1:
                        last.then_inc(piece_used, 1)
                yield last

            def add_mixed(phase, j, h):
                pe.wait_ge(ot_ready, 2 * h + 2)
                for u in range(PIECES):
                    c, m = divmod(u, 2)
                    for w, x_t in parts((phase, j), u):
                        for t in range(NT):
                            last = pe.matmul(acc[:, t, BANK * m:BANK * m + BANK],
                                             x_t[:, 4 * (h % 2) + c, P * t:P * t + P], w,
                                             start=False, stop=True, skip_group_check=True)
                    if u < PIECES - 1:
                        last.then_inc(piece_used, 1)
                last.then_inc(added, 1)

            def free_none(b):
                pass

            pe.wait_ge(const_ready, 1)
            pe.wait_ge(small_in, 16 * 6)
            pe.transpose(pb[:, 3, 0:3 * A_HEADS], rows[:], ident[0:3 * A_HEADS, 0:3 * A_HEADS]).then_inc(cols_ps, 1)
            pe.wait_ge(x_in, 16)
            inject()
            transposes(0, 0)

            def project_f(h):
                def free(b):
                    if h == 0:
                        pe.wait_ge(ht_ready, 4)
                    else:
                        pe.wait_ge(kt_ready, 3)
                for last in by_feature(("a", 4 * h), (0, 1), free):
                    last.then_inc(pj_ps, 1)

            def project_q(h):
                def free(b):
                    if h and b == 0:
                        pe.wait_ge(sig_done, 4)
                    elif h:
                        pe.wait_ge(st_ready, 1)
                banks = (1, 2) if h else (2, 3)
                for last in by_feature(("a", 4 * h + 1), banks, free):
                    last.then_inc(pj_ps, 1)

            def project_v(h):
                def free(t):
                    if h == 0 and t == 0:
                        pe.wait_ge(sig_done, 2)
                    pe.wait_ge(qdec_ready, 2 * h + 1 + (t if h else 0))
                for last in by_token(("a", 4 * h + 2), (1, 2), free):
                    last.then_inc(pj_ps, 1)

            def project_og(h):
                def free(t):
                    if h == 0:
                        pe.wait_ge(qdec_ready, 2)
                    else:
                        pe.wait_ge(o_ready, t + 1)
                for last in by_token(("a", 4 * h + 3), (3, 0), free):
                    last.then_inc(pj_ps, 1)

            def tails(h):
                pe.wait_ge(ktail_ready, h + 1)
                pe.wait_ge(og_ready, 2 * h + 2)
                for j in range(HALF_A):
                    last = pe.transpose(pb[:, 0, P * j:P * j + P], t_log[:, SEQ * j:SEQ * j + P], ident[:])
                last.then_inc(kt_ps, 1)
                if h:
                    pe.wait_ge(ot_ready, 1)
                else:
                    pe.wait_ge(v_ready, 1)
                for j in range(HALF_A):
                    last = pe.transpose(pb[0:64, 1, P * j:P * j + P], t_log[:, SEQ * j + P:SEQ * j + P + 64], ident[:])
                last.then_inc(kt_ps, 1)

            def attention_a(h):
                pe.wait_ge(kinv_ready, h + 1)
                pe.wait_ge(qdec_ready, 2 * h + 2)
                for t in range(NT):
                    if t == 0 and h:
                        pe.wait_ge(ot_ready, 2)
                    elif t == 0:
                        pe.wait_ge(v_ready, 2)
                    for j in range(HALF_A):
                        last = pe.matmul(pb[:, 2 + t, P * j:P * j + P],
                                         k_inv[:, SEQ * j + P * t:SEQ * j + P * t + P],
                                         q_dec[h][:, j, P * t:P * t + P], start=True, stop=True)
                    last.then_inc(at_ps, 1)

            def state_parts(h):
                pe.wait_ge(kt_ready, 3 * h + 3)
                pe.wait_ge(v_ready, 2 * h + 2)
                for n, b in enumerate((2, 3, 0)):
                    if n < 2:
                        pe.wait_ge(at_ready, 2 * h + n + 1)
                    elif h == 0:
                        pe.wait_ge(sig_done, 3)
                    for j in range(HALF_A):
                        last = pe.matmul(pb[:, b, P * j:P * j + P], k_tail[:, n, j],
                                         v_tok[:, n // 2, P * j:P * j + P], start=True, stop=True)
                    last.then_inc(kv_ps, 1)

            def outputs(h):
                pe.wait_ge(st_ready, 3 * h + 3)
                for t, b in ((0, 3), (1, 0)):
                    for j in range(HALF_A):
                        cut = slice(P * j, P * j + P)
                        chunks = [2 * t + u for u in range(2) if 2 * t + u > 0]
                        last = pe.matmul(pb[:, b, cut], att_m[:, t, j], v_tok[:, t, cut], start=True, stop=False,
                                         skip_group_check=True)
                        for n in chunks:
                            u = n % 2
                            last = pe.matmul(pb[64 * u:64 * u + 64, b, cut],
                                             q_dec[h][:, j, CHUNK * n:CHUNK * n + CHUNK], states[:, n - 1, j],
                                             start=False, stop=True, skip_group_check=True)
                    last.then_inc(o_ps, 1)

            def turn_mixed(h, ready, banks):
                for t in range(NT):
                    ready(t)
                    for c in range(4):
                        last = pe.transpose(pb[:, banks[t], P * c:P * c + P], hn[:, t, 4 * (h % 2) + c], ident[:])
                    last.then_inc(ot_ps, 1)

            def a_ready(h):
                def ready(t):
                    pe.wait_ge(o_ready, 2 * h + t + 1)
                    pe.wait_ge(v_ready, 3 + t)
                return ready

            project_f(0)
            project_q(0)
            project_v(0)
            project_og(0)
            tails(0)
            attention_a(0)
            project_f(1)
            state_parts(0)
            project_q(1)
            outputs(0)
            project_v(1)
            project_og(1)
            turn_mixed(0, a_ready(0), (1, 2))
            tails(1)
            attention_a(1)
            state_parts(1)
            add_mixed("a", 8, 0)
            outputs(1)
            turn_mixed(1, a_ready(1), (1, 2))
            add_mixed("a", 9, 1)

            def moe(layer):
                stage = 1 + 4 * layer
                transposes(stage, 1 + 3 * layer)
                pe.wait_ge(ht_ready, 4 * stage + 4)
                pe.wait_ge(wroute_ready, 2)
                for t in range(NT):
                    for c in range(NC):
                        last = pe.matmul(pb[:, 0, 64 * t:64 * t + ROUTES], routeT[:, c, P * t:P * t + P],
                                         w_route[:, layer, c], start=c == 0, stop=c == NC - 1)
                last.then_inc(lg_ps[layer], 1)
                pe.wait_ge(p_in, 16 * (layer + 1))
                for k in range(D_PLE // P):
                    for t in range(NT):
                        last = pe.transpose(pb[:, 1, SEQ * k + P * t:SEQ * k + P * t + P],
                                            p_tok[:, t, P * k:P * k + P], ident[:])
                last.then_inc(pt_ps, 1)
                pe.wait_ge(pt_ready, layer + 1)
                key, w_src = (("a", PROJ), blocks_a[PROJ]) if layer == 0 else (("b", PROJ), blocks_b[PROJ])
                arrived(pe, key)
                w = slot_of(key, w_src)

                def embedding_half(j):
                    for t in range(NT):
                        if j:
                            pe.wait_ge(pp_ready, 4 * layer + t + 1)
                        for k in range(D_PLE // P):
                            last = pe.matmul(pb[:, 2 + t, :], pT[:, k, P * t:P * t + P],
                                             w[:, k, BANK * j:BANK * j + BANK], start=k == 0, stop=k == 1)
                        last.then_inc(proj_ps, 1)

                embedding_half(0)
                pe.wait_ge(chosen_ready[layer], 1)
                pe.wait_ge(const_ready, 6)
                ranks = pb[:, 1]
                pe.matmul(ranks[:, 0:EXPERTS], before[:], chosen[:, 0], start=True, stop=True)
                pe.matmul(ranks[:, EXPERTS:2 * EXPERTS], ones[:], chosen[:, 0], start=True, stop=False)
                pe.matmul(ranks[:, EXPERTS:2 * EXPERTS], before[:], chosen[:, 1], start=False, stop=True)
                pe.matmul(ranks[:, 2 * EXPERTS:3 * EXPERTS], ones[:], chosen[:, 0], start=True, stop=False)
                pe.matmul(ranks[:, 2 * EXPERTS:3 * EXPERTS], ones[:], chosen[:, 1], start=False,
                          stop=True).then_inc(rk_ps[layer], 1)
                embedding_half(1)
                pe.wait_ge(pp_ready, 4 * layer + 4)
                pe.wait_ge(normed, 2 * layer + 2)
                pe.wait_ge(rounds_ready[layer], 1)
                rounds = pe.value_load(rounds_i[0:1, layer:layer + 1], min_val=1, max_val=8)
                with pe.Fori(0, rounds) as r:
                    with pe.Fori(0, BODIES) as i:
                        it = r * BODIES + i
                        for b in range(BATCHES):
                            experts(layer, it, b)
                return rounds

            def experts(layer, it, b):
                def here(slot, k):
                    pe.wait_ge(moe_landed[layer][slot], it * (16 * BODY_BLOCKS // RING) + 16 * (k // RING + 1))

                pe.wait_ge(pick_ready[layer], it * BATCHES + (b + 1))
                for t in range(NT):
                    last = pe.transpose(pb[:, 3, 256 + P * t:256 + P * t + P],
                                        pick_g[:, t].rearrange("p e s -> p (e s)"), ident[:])
                last.then_inc(pgt_ps[layer], 1)
                for j in range(2):
                    for c in range(4):
                        for t in range(NT):
                            last = pe.matmul(pb[:, j, P * c:P * c + P], hn[:, t, 4 * j + c],
                                             pick[:, t].rearrange("p e s -> p (e s)"), start=t == 0,
                                             stop=t == NT - 1)
                    last.then_inc(xg_ps[layer], 1)
                pe.wait_ge(xg_ready[layer], it * (2 * BATCHES) + (2 * b + 2))
                for e in range(BATCH_E * b, BATCH_E * b + BATCH_E):
                    s_gate, s_up, s_down = expert_slots(e)
                    first = 3 * e % RING
                    k_of = {(first + n) % RING: 3 * e + n for n in range(3)}
                    at = SLOTS * (e % BATCH_E)
                    here(s_gate, k_of[s_gate])
                    here(s_up, k_of[s_up])
                    for c in range(NC):
                        for g in range(COLS):
                            cut = BANK * c + P * g
                            last = pe.matmul(pb[SLOTS * g:SLOTS * g + SLOTS, 2, 0:256],
                                             xg[:, c, at:at + SLOTS], ring[:, s_gate:s_gate + 2, cut:cut + P],
                                             start=c == 0, stop=c == NC - 1, tile_position=(0, SLOTS * g))
                    last.then_inc(h_ps[layer], 1)
                    pe.wait_ge(hid_ready[layer], it * BODY_E + (e + 1))
                    pe.transpose(pb[:, 2, 256:384], hid, ident[:]).then_inc(hidT_ps[layer], 1)
                    pe.wait_ge(hidT_ready[layer], it * BODY_E + (e + 1))
                    here(s_down, k_of[s_down])
                    if e % BATCH_E == 0:
                        pe.wait_ge(pgt_ready[layer], it * BATCHES + (b + 1))
                    else:
                        pe.wait_ge(y_act[layer], it * BODY_E + e)
                        pe.wait_ge(y_dve[layer], it * BODY_E + e)
                    for c in range(D_EXPERT // P):
                        for g in range(COLS):
                            cut = D * c + 256 * g
                            last = pe.matmul(pb[SLOTS * g:SLOTS * g + SLOTS, 3, 0:256],
                                             hidT[:, SLOTS * c:SLOTS * c + SLOTS], ring[:, s_down, cut:cut + 256],
                                             start=c == 0, stop=c == D_EXPERT // P - 1,
                                             tile_position=(0, SLOTS * g))
                    last.then_inc(y_ps[layer], 1)
                pe.wait_ge(y_act[layer], it * BODY_E + (BATCH_E * b + BATCH_E))
                pe.wait_ge(y_dve[layer], it * BODY_E + (BATCH_E * b + BATCH_E))
                for t in range(NT):
                    for j in range(2):
                        last = pe.matmul(acc[:, t, BANK * j:BANK * j + BANK], pick_gT[:, P * t:P * t + P],
                                         y_sb[:, BANK * j:BANK * j + BANK], start=False, stop=True,
                                         skip_group_check=True)
                last.then_inc(scat_done[layer], 1)

            def embed(layer):
                stage = 2 + 4 * layer
                transposes(stage, 2 + 3 * layer)
                pe.wait_ge(ht_ready, 4 * stage + 4)
                for j in range(2):
                    for last in by_token(("bc"[layer], j), (2 * j, 2 * j + 1), free_none):
                        last.then_inc(gate_ps, 1)

            moe(0)
            embed(0)
            pe.wait_ge(xs_ready, 4)
            inject()
            transposes(3, 3)

            def project_qkv(n, free):
                kind, first = QKV[n][1], QKV_BANKS[n]
                project = by_token if kind == 2 else by_feature
                for last in project(("b", 2 + n), (first, first + 1), free):
                    last.then_inc(qkv_ps, 1)

            def after_evac(count):
                return lambda b: pe.wait_ge(qkv_ready, count + b)

            def q_k(n):
                if n >= 2:
                    pe.wait_ge(s_ready, n - 1)
                h, m = divmod(n, HALF_B)
                rows_h = slice(64 * (m % 2), 64 * (m % 2) + 64)
                j = m // 2
                pe.matmul(pb[:, n % 2, 0:256], qT[h][rows_h, j, P:SEQ], kT[h][rows_h, j], start=True, stop=True)
                pe.matmul(pb[:, n % 2, 256:384], qT[h][rows_h, j, 0:P], kT[h][rows_h, j, P:SEQ],
                          start=True, stop=True).then_inc(s_ps, 1)

            def turn_probs(n):
                pe.wait_ge(e_ready, n + 1)
                if n:
                    pe.wait_ge(pT_ready, n)
                for m in range(3):
                    last = pe.transpose(pb[:, 2, P * m:P * m + P], probs[n % 2][:, P * m:P * m + P], ident[:])
                last.then_inc(pT_ps, 1)

            def p_v(n):
                pe.wait_ge(pT_ready, n + 1)
                if n % 4 == 0 and n:
                    pe.wait_ge(oa_ready, n // 4)
                at = P * (n % 4)
                v = v_rev[:, :, B_DIM * (n % HALF_B):B_DIM * (n % HALF_B) + B_DIM]
                pt = probsT[n % 2]
                pe.matmul(pb[:, 3, at:at + B_DIM], pt[:, 256:384], v[:, 1], start=True, stop=True)
                pe.matmul(pb[:, 3, at + B_DIM:at + P], pt[:, 0:P], v[:, 0], start=True, stop=False)
                last = pe.matmul(pb[:, 3, at + B_DIM:at + P], pt[:, P:256], v[:, 1], start=False, stop=True)
                if n % 4 == 3:
                    last.then_inc(oa_ps, 1)

            def heads(h):
                base = HALF_B * h
                q_k(base)
                for n in range(base, base + HALF_B):
                    if n + 1 < base + HALF_B:
                        q_k(n + 1)
                    turn_probs(n)
                    if n > base:
                        p_v(n - 1)
                p_v(base + HALF_B - 1)

            def b_ready(h):
                def ready(t):
                    pe.wait_ge(oa_ready, 2 * h + 2)
                return ready

            pe.wait_ge(ht_ready, 16)
            project_qkv(0, free_none)
            project_qkv(1, free_none)
            transposes(4, 3, turn=flip, after=lambda t, j: pe.wait_ge(qkv_ready, 2 * t + j + 1))
            pe.wait_ge(ht_ready, 20)
            project_qkv(2, free_none)
            project_qkv(3, free_none)
            project_qkv(4, after_evac(5))
            pe.wait_ge(qkv_ready, 10)
            heads(0)
            pe.wait_ge(s_ready, 8)
            project_qkv(5, free_none)
            turn_mixed(2, b_ready(0), (2, 3))
            add_mixed("b", 8, 2)
            pe.wait_ge(qkv_ready, 12)
            heads(1)
            turn_mixed(3, b_ready(1), (2, 3))
            add_mixed("b", 9, 3)
            moe(1)
            embed(1)


_INS = ['x', 'p', 'a_w_in', 'a_lb_logits', 'a_out_norm', 'a_w_o', 'kv_norm', 'w_kv', 'b_w_q', 'b_rel_bias',
        'b_w_o', 'norm_mix', 'norm_ffn', 'norm_ple', 'moe_w_group', 'moe_b_group', 'moe_w_expert',
        'moe_b_expert', 'moe_w_gate', 'moe_w_up', 'moe_w_down', 'ple_w_proj', 'ple_w_gate', 'final_norm']
_OUTS = [((1, 256, 1024), 'float32')]


def kernel(**inputs):
    import numpy as _np
    import concourse.bacc as _bacc
    from concourse import mybir as _mybir
    from concourse.bass_utils import run_bass_kernel_spmd as _run

    nc = _bacc.Bacc("TRN2", target_bir_lowering=False, num_devices=1)
    arrays, args = {}, []
    for name in _INS:
        a = _np.ascontiguousarray(inputs[name])
        arrays[f"in_{name}_dram"] = a
        args.append(nc.dram_tensor(f"in_{name}_dram", a.shape, _mybir.dt.from_np(a.dtype), kind="ExternalInput").ap())
    for i, (shape, dtype) in enumerate(_OUTS):
        dt = _mybir.dt.from_np(_np.dtype(dtype))
        args.append(nc.dram_tensor(f"out_{i}_dram", shape, dt, kind="ExternalOutput").ap())
    build(nc, *args)
    r = _run(nc, [arrays], core_ids=[0])
    got = tuple(r.results[0][f"out_{i}_dram"] for i in range(len(_OUTS)))
    return got[0]
```

```python
from contextlib import ExitStack

import concourse.bass as bass
from concourse import mybir

F32 = mybir.dt.float32
F32R = mybir.dt.float32r
I32 = mybir.dt.int32
ALU = mybir.AluOpType
ACT = mybir.ActivationFunctionType
AX = mybir.AxisListType.X

P = 128
D = 1024
SEQ = 256
NT = SEQ // P
NC = D // P
CHUNK = 64
BANK = 512
A_HEADS = 8
HALF_A = A_HEADS // 2
B_HEADS = 16
B_DIM = D // B_HEADS
HALF_B = B_HEADS // 2
ATTN_SCALE = B_DIM ** -0.5
N_REL = 320
D_PLE = 256
GROUPS = 4
PER_GROUP = 8
EXPERTS = GROUPS * PER_GROUP
D_EXPERT = 512
ROUTES = GROUPS + EXPERTS
EPS = 1e-6
MASKED = -1e30
SLOTS = 32
BATCH_E = P // SLOTS
COLS = P // SLOTS
RING = 8
SLOT = NC * BANK
BODY_E = 8
BODY_BLOCKS = 3 * BODY_E
BODIES = EXPERTS // BODY_E
BATCHES = BODY_E // BATCH_E
BLOCKS_A, BLOCKS_B, BLOCKS_C = 11, 11, 2
PLAIN = (1, 2, 4, 5)
HALVES = (3, 6)
SPLIT_STAGES = (0, 2, 3, 5)
PROJ = 10
DENSE_RING = RING - 1
PIECE = BANK
PIECES = SLOT // PIECE
SPLIT_BUFS = 4
FIRST, REST = range(PIECES // 2), range(PIECES // 2, PIECES)
(G_MIX0, G_MIX1, G_FFN0, G_FFN1, G_PLE0, G_PLE1, G_KV) = range(7)


class Count:

    def __init__(self, eng, sem, base=0):
        self.eng, self.sem, self.base, self.n = eng, sem, base, 0

    def link(self, ins):
        self.n += 1
        ins.then_inc(self.sem, 1)
        self.eng.wait_ge(self.sem, self.base + self.n)


def expert_slots(e):
    s = 3 * e % RING
    if s == RING - 1:
        return 0, 1, s
    return s, s + 1, (s + 2) % RING


def build(nc, x, p, a_w_in, a_lb_logits, a_out_norm, a_w_o, kv_norm, w_kv, b_w_q, b_rel_bias,
          b_w_o, norm_mix, norm_ffn, norm_ple, moe_w_group, moe_b_group, moe_w_expert,
          moe_b_expert, moe_w_gate, moe_w_up, moe_w_down, ple_w_proj, ple_w_gate, final_norm, out):
    ctx = ExitStack()
    with ctx:
        def sb(name, shape, dt=F32):
            return ctx.enter_context(nc.sbuf_tensor(name, shape, dt))

        def sem(name):
            return ctx.enter_context(nc.semaphore(name))

        def sems(name):
            return [sem(f"{name}{layer}") for layer in range(2)]

        ring = sb("ring", [P, RING, SLOT])
        xs = sb("xs", [P, NT, D])
        hn = sb("hn", [P, NT, NC, P])
        hT_hi = sb("hT_hi", [P, NC, SEQ], F32R)
        hT_lo = sb("hT_lo", [P, NC, SEQ], F32R)
        w_hi = sb("w_hi", [P, SPLIT_BUFS, PIECE], F32R)
        w_lo = sb("w_lo", [P, SPLIT_BUFS, PIECE], F32R)
        ident = sb("ident", [P, P])
        before = sb("before", [P, P])
        ones = sb("ones", [P, P])
        causal = sb("causal", [P, P])
        iota_i = sb("iota_i", [P, SLOTS], I32)
        iota = sb("iota", [P, SLOTS])
        fresh_g = sb("fresh_g", [P, NT * GROUPS])
        fresh_e = sb("fresh_e", [P, NT * EXPERTS])
        thresh_i = sb("thresh_i", [P, SEQ // SLOTS - 1], I32)
        thresh = sb("thresh", [P, SEQ // SLOTS - 1])
        w_route = sb("w_route", [P, 2, NC, ROUTES])
        b_route = sb("b_route", [P, 2, ROUTES])
        gains = sb("gains", [P, 7, NC])
        rows = sb("rows", [3 * A_HEADS, P])
        cols = sb("cols", [P, 3 * A_HEADS])
        lb = sb("lb", [P, 4, A_HEADS])
        ssq = sb("ssq", [P, NT])
        ssq_0 = sb("ssq_0", [P, NT])
        ms_0 = sb("ms_0", [P, NT])
        spare = sb("spare", [P, 7])
        ms = sb("ms", [P, NT])
        root = sb("root", [P, NT])
        rstd = sb("rstd", [P, NT])
        rounds_i = sb("rounds_i", [P, 2], I32)
        more_i = sb("more_i", [P, 2], I32)
        work = sb("work", [P, 6450])
        bench = ring[:, DENSE_RING]

        def view(at, n):
            return work[:, at:at + n]

        q_dec = [bench[:, 1024 * h:1024 * h + 1024].rearrange("p (j t) -> p j t", j=HALF_A) for h in range(2)]
        t_cum, t_exp = bench[:, 2048:3072], bench[:, 3072:4096]
        k_inv = view(0, 1024)
        k_tail = view(1024, 1536).rearrange("p (n j d) -> p n j d", n=3, j=HALF_A)
        v_tok = view(2560, 1024).rearrange("p (t e) -> p t e", t=NT)
        att_m = view(3584, 1024).rearrange("p (t j s) -> p t j s", t=NT, j=HALF_A)
        states = view(4608, 1536).rearrange("p (n j e) -> p n j e", n=3, j=HALF_A)
        dl = view(6144, 16).rearrange("p (h n j) -> p h n j", h=2, n=2)
        o_small = view(6160, 24).rearrange("p (a m) -> p a m", a=3)
        xs_flat = xs[:].rearrange("p t d -> p (t d)")
        t_key, t_log = xs_flat[:, 0:1024], xs_flat[:, 1024:2048]
        o_sq = t_key
        og_tok = hn[:, :, HALF_A:]
        routeT = xs_flat.rearrange("p (c s) -> p c s", c=NC)
        xg = view(0, 1024).rearrange("p (c s) -> p c s", c=NC)
        pick = view(1024, 256).rearrange("p (t e s) -> p t e s", t=NT, e=BATCH_E)
        pick_g = view(1280, 256).rearrange("p (t e s) -> p t e s", t=NT, e=BATCH_E)
        pick_gT = view(1536, 256)
        silu = view(1792, 128)
        hid = view(1920, 128)
        hidT = view(2048, 128)
        y_sb = view(2176, 1024)
        rank = view(3200, 64).rearrange("p (t e) -> p t e", t=NT)
        gate = view(3264, 64).rearrange("p (t e) -> p t e", t=NT)
        rank8 = view(3328, 16).rearrange("p (t e) -> p t e", t=NT)
        gate8 = view(3344, 16).rearrange("p (t e) -> p t e", t=NT)
        dump = view(0, 2048).rearrange("p (t d) -> p t d", t=NT)

        def pair(at, m):
            return view(at, NT * m).rearrange("p (t m) -> p t m", t=NT)

        logit = pair(3360, ROUTES)
        g_max, g_sum, g_w, top1, top2, top_d, top_x, top_s, w_1, w_2 = (
            pair(3440 + 2 * n, 1) for n in range(10))
        g_dif, g_exp, g_eq, g_cum, g_hot, g_pen = (pair(3464 + 8 * n, GROUPS) for n in range(6))
        e_log, e_dif, e_eq, e_cum, hot1, hot2, chosen = (
            pair(3520 + 64 * n, EXPERTS) for n in range(7))
        most = view(3968, 1)
        over = view(3976, 7)
        n_over = view(3984, 1)
        p_tok = view(4096, 512).rearrange("p (t m) -> p t m", t=NT)
        pT = view(4608, 512).rearrange("p (k s) -> p k s", k=NT)
        sig = view(5120, 1024).rearrange("p (t n) -> p t n", t=NT)
        bias = view(0, 4096).rearrange("p (h j) -> p h j", h=B_HEADS)
        qT = [bench[:, 1024 * h:1024 * h + 1024].rearrange("p (j t) -> p j t", j=4) for h in range(2)]
        kT = [bench[:, 2048 + 1024 * h:3072 + 1024 * h].rearrange("p (j t) -> p j t", j=4) for h in range(2)]
        v_keys = view(4096, 1024).rearrange("p (t e) -> p t e", t=NT)
        probs = [view(5120 + 384 * h, 384) for h in range(2)]
        score = [xs_flat[:, 384 * h:384 * h + 384] for h in range(2)]
        probsT = [xs_flat[:, 768 + 384 * n:1152 + 384 * n] for n in range(3)]
        s_max = view(5888, 32).rearrange("p (h t) -> p h t", t=NT)
        s_neg = view(5920, 32).rearrange("p (h t) -> p h t", t=NT)
        s_sum = view(5952, 32).rearrange("p (h t) -> p h t", t=NT)
        s_rec = view(5984, 32).rearrange("p (h t) -> p h t", t=NT)
        oT = hn[:].rearrange("p t c q -> p (t c q)").rearrange("p (c s) -> p c s", c=NC)
        fin_gain = view(0, D)
        fin = view(D, NT * D).rearrange("p (t d) -> p t d", t=NT)

        acc = ctx.enter_context(nc.psum_tensor("acc", [P, NT, D], F32))
        pb = ctx.enter_context(nc.psum_tensor("pb", [P, 4, BANK], F32))

        x_in, small_in, route_in, late_in = sem("x_in"), sem("small_in"), sem("route_in"), sem("late_in")
        p_in = sem("p_in")
        first_half_in = sem("first_half_in")
        landed = [sem(f"landed{s}") for s in range(RING)]
        moe_landed = [[sem(f"moe_landed{la}_{s}") for s in range(RING)] for la in range(2)]
        moe_freed = sems("moe_freed")
        out_done = sem("out_done")
        scaled = sem("scaled")
        hi_ready, lo_ready, piece_used = sem("hi_ready"), sem("lo_ready"), sem("piece_used")
        pool_step, const_ready, zeroed, bias_mask = (
            sem("pool_step"), sem("const_ready"), sem("zeroed"), sem("bias_mask"))
        cols_ps, lb_ready, lbe = sem("cols_ps"), sem("lb_ready"), sem("lbe")
        dve_step = sem("dve_step")
        sq_done, ms_ready, root_ready, hn_ready = (
            sem("sq_done"), sem("ms_ready"), sem("root_ready"), sem("hn_ready"))
        tr_ps, ht_ready = sem("tr_ps"), sem("ht_ready")
        hT_hi_ready = sem("hT_hi_ready")
        rt_dve, rt_act = sem("rt_dve"), sem("rt_act")
        rstd_ready, normed_0, normed_1, wroute_ready = (
            sem(n) for n in ("rstd_ready", "normed_0", "normed_1", "wroute_ready"))
        pj_ps, sig_done, f_ready, ln_done, cum_ready, tail_ready = (
            sem(n) for n in ("pj_ps", "sig_done", "f_ready", "ln_done", "cum_ready", "tail_ready"))
        exp_done, kinv_ready, ktail_ready, qdec_ready, v_ready, og_ready = (
            sem(n) for n in ("exp_done", "kinv_ready", "ktail_ready", "qdec_ready", "v_ready", "og_ready"))
        kt_ps, kt_ready, at_ps, at_ready, kv_ps, st_ready = (
            sem(n) for n in ("kt_ps", "kt_ready", "at_ps", "at_ready", "kv_ps", "st_ready"))
        o_ps, osq_done, oms_ready, oroot_ready, o_ready = (
            sem(n) for n in ("o_ps", "osq_done", "oms_ready", "oroot_ready", "o_ready"))
        ot_ps, ot_ready, added = sem("ot_ps"), sem("ot_ready"), sem("added")
        pt_ps, pt_ready = sem("pt_ps"), sem("pt_ready")
        lg_ps, rk_ps, dif_ready, rexp_done, chosen_ready, rounds_ready = (
            sems(n) for n in ("lg_ps", "rk_ps", "dif_ready", "rexp_done", "chosen_ready", "rounds_ready"))
        pickg_ready = sems("pickg_ready")
        pick_ready, pgt_ps, pgt_ready, xg_ps, xg_ready, h_ps = (
            sems(n) for n in ("pick_ready", "pgt_ps", "pgt_ready", "xg_ps", "xg_ready", "h_ps"))
        silu_done, hid_ready, hidT_ps, hidT_ready, y_ps, y_act, y_dve, scat_done, dve_loop = (
            sems(n) for n in ("silu_done", "hid_ready", "hidT_ps", "hidT_ready", "y_ps", "y_act",
                              "y_dve", "scat_done", "dve_loop"))
        gate_ps, proj_ps, pp_ready, sig_ready, xs_ready = (
            sem(n) for n in ("gate_ps", "proj_ps", "pp_ready", "sig_ready", "xs_ready"))
        qkv_ps, qkv_ready, s_ps, s_ready, e_ready, pT_ps, pT_ready, oa_ps, oa_ready = (
            sem(n) for n in ("qkv_ps", "qkv_ready", "s_ps", "s_ready", "e_ready", "pT_ps",
                             "pT_ready", "oa_ps", "oa_ready"))
        injected = sem("injected")
        rec_ready, weighed = sem("rec_ready"), sem("weighed")
        pre_ready, fin_0, fin_1 = sem("pre_ready"), sem("fin_0"), sem("fin_1")

        def over_d(w):
            return w.rearrange("(p c) n -> p c n", c=NC)

        def over_rows(w):
            return w.rearrange("(c p) n -> p c n", p=P)

        blocks_a = [over_d(a_w_in[0][:, s * D + h * 512:s * D + h * 512 + 512])
                    for h in range(2) for s in (1, 0, 2, 3)]
        blocks_a += [over_rows(a_w_o[0][512 * j:512 * j + 512, :]) for j in range(2)]

        def gate_blocks(layer):
            return [over_d(ple_w_gate[layer][:, 512 * j:512 * j + 512]) for j in range(2)]

        blocks_a += [over_rows(ple_w_proj[0])]
        blocks_b = gate_blocks(0)
        blocks_b += [over_d(b_w_q[0][:, 512 * h:512 * h + 512]) for h in range(2)]
        for h in range(2):
            blocks_b += [over_d(w_kv[:, a + 512 * h:a + 512 * h + 512]) for a in (0, D)]
        blocks_b += [over_rows(b_w_o[0][512 * j:512 * j + 512, :]) for j in range(2)]
        blocks_b += [over_rows(ple_w_proj[1])]
        blocks_c = gate_blocks(1)
        assert (len(blocks_a), len(blocks_b), len(blocks_c)) == (BLOCKS_A, BLOCKS_B, BLOCKS_C)
        place, uses, dense = {}, [0] * RING, []
        for phase, blocks in (("a", blocks_a), ("b", blocks_b), ("c", blocks_c)):
            for j in range(len(blocks)):
                s = j % DENSE_RING
                uses[s] += 1
                place[phase, j] = s, 16 * uses[s]
                if j != PROJ:
                    dense.append((phase, j))

        def slot_of(key, src=None):
            s = place[key][0]
            if src is None:
                return ring[:, s]
            return ring[:, s, 0:src.shape[1] * src.shape[2]].rearrange("p (c n) -> p c n", n=src.shape[2])

        QKV = ((0, 0), (1, 0), (0, 1), (0, 2), (1, 1), (1, 2))
        QKV_BANKS = (0, 2, 0, 2, 0, 0)

        def arrived(eng, key):
            s, value = place[key]
            eng.wait_ge(landed[s], value)

        def wait_used(eng, phase, j):
            if (phase, j) in dense:
                eng.wait_ge(lo_ready, PIECES * (dense.index((phase, j)) + 1))
            else:
                eng.wait_ge(proj_ps, 4 if phase == "a" else 8)

        def wait_product(eng, phase, j):
            if phase != "c" and j >= 8:
                eng.wait_ge(added, (3 if phase == "b" else 1) + j - 8)
            elif phase == "a":
                eng.wait_ge(pj_ps, 2 * j + 2)
            elif j < 2:
                eng.wait_ge(gate_ps, (4 if phase == "c" else 0) + 2 * j + 2)
            else:
                eng.wait_ge(qkv_ps, 2 * (j - 2) + 2)

        def gain_of(key, u):
            phase, j = key
            if phase == "a" and j >= 8:
                at = 2 * A_HEADS + HALF_A * (j - 8) + u // 2
                return cols[:, at:at + 1]
            if phase == "b" and j >= 8:
                return None
            kind = G_MIX0 if phase == "a" else G_PLE1 if phase == "c" else (G_PLE0, G_MIX1, G_KV, G_KV)[j // 2]
            return gains[:, kind, u:u + 1]

        gained = [key for key in dense if gain_of(key, 0) is not None]

        def piece(key, u):
            return ring[:, place[key][0], PIECE * u:PIECE * u + PIECE]

        def scale(dve, key, pieces=range(PIECES)):
            if key == ("a", 0) and pieces == FIRST:
                dve.wait_ge(first_half_in, 16)
            else:
                arrived(dve, key)
            for u in pieces:
                dve.tensor_scalar(piece(key, u), piece(key, u), gain_of(key, u), None,
                                  ALU.mult).then_inc(scaled, 1)

        def squares_until(n):
            return sum(2 * NT if m in HALVES else NT for m in range(n + 1))

        def high(act, key, pieces):
            n = dense.index(key)
            if key not in gained:
                arrived(act, key)
            for u in pieces:
                if key in gained:
                    act.wait_ge(scaled, PIECES * gained.index(key) + u + 1)
                k = PIECES * n + u
                m, v = divmod(k - SPLIT_BUFS, PIECES)
                if m >= 0 and v < PIECES - 1:
                    act.wait_ge(piece_used, (PIECES - 1) * m + v + 1)
                elif m >= 0:
                    wait_product(act, *dense[m])
                act.activation(w_hi[:, k % SPLIT_BUFS], piece(key, u), ACT.Copy).then_inc(hi_ready, 1)

        def low(pool, key):
            n = dense.index(key)
            for u in range(PIECES):
                k = PIECES * n + u
                at = k % SPLIT_BUFS
                pool.wait_ge(hi_ready, k + 1)
                pool.tensor_tensor(w_lo[:, at], piece(key, u), w_hi[:, at].bitcast(F32),
                                   ALU.subtract).then_inc(lo_ready, 1)

        def bank3(b, m):
            return pb[:, b, :].rearrange("p (a n) -> p a n", n=m)

        def wide(ap, n):
            return ap.unsqueeze(len(ap.shape)).to_broadcast(list(ap.shape) + [n])

        block = ctx.enter_context(nc.Block())

        @block.sync
        def _(sp):
            def load(key, src):
                sp.dma_start(slot_of(key, src), src).then_inc(landed[place[key][0]], 16)

            def load_expert(layer, i, k):
                e = k // 3
                s = k % RING
                kind = expert_slots(e % BODY_E).index(s)
                if kind < 2:
                    w = (moe_w_gate, moe_w_up)[kind]
                    src = w[layer][i * BODY_E + e].rearrange("(p c) n -> p (c n)", c=NC)
                    dst = ring[:, s, :]
                else:
                    src = moe_w_down[layer][i * BODY_E + e].rearrange("(c p) n -> p c n", p=P)
                    dst = ring[:, s, :].rearrange("p (c n) -> p c n", c=4)
                sp.dma_start(dst, src).then_inc(moe_landed[layer][s], 16)

            def wait_read(layer, before, k):
                e, s = k // 3, k % RING
                done = y_ps if expert_slots(e % BODY_E)[2] == s else h_ps
                sp.wait_ge(done[layer], before + (e + 1))

            def experts(layer, phase, blocks):
                rounds = sp.alloc_register(f"sp_rounds{layer}")
                sp.reg_mov(rounds, 1)
                with sp.Fori(0, rounds) as r:
                    sp.wait_ge(moe_freed[layer], r * EXPERTS + 1)
                    for j in range(len(blocks) - DENSE_RING, len(blocks)):
                        if j == PROJ:
                            if layer == 0:
                                sp.wait_ge(o_ps, 4)
                            else:
                                sp.wait_ge(s_ps, B_HEADS)
                            load_expert(layer, 0, DENSE_RING)
                        wait_used(sp, phase, j)
                        load_expert(layer, 0, place[phase, j][0])
                    with sp.Fori(0, BODIES - 1) as i:
                        it = r * BODIES + i
                        for k in range(BODY_BLOCKS):
                            wait_read(layer, it * BODY_E, k)
                            load_expert(layer, i, k + RING)
                    for k in range(BODY_BLOCKS - RING):
                        wait_read(layer, r * EXPERTS + (EXPERTS - BODY_E), k)
                        load_expert(layer, BODIES - 1, k + RING)
                    sp.wait_ge(rounds_ready[layer], 1)
                    sp.reg_load(rounds, rounds_i[0:1, layer:layer + 1])

            def after_experts(layer, phase, blocks):
                more = sp.value_load(more_i[0:1, layer:layer + 1], min_val=0, max_val=7)
                for j, src in enumerate(blocks):
                    if j < DENSE_RING:
                        wait_read(layer, more * EXPERTS + (EXPERTS - BODY_E), BODY_BLOCKS - RING + place[phase, j][0])
                    else:
                        wait_used(sp, phase, j - DENSE_RING)
                    load((phase, j), src)

            sp.dma_start(xs[:], x[0].rearrange("(t p) d -> p t d", p=P)).then_inc(x_in, 16)
            sp.dma_start(rows[0:2 * A_HEADS, :], a_lb_logits.rearrange("r (h p) -> (r h) p", p=P)).then_inc(small_in, 16)
            sp.dma_start(rows[2 * A_HEADS:3 * A_HEADS, :], a_out_norm[0].rearrange("(h p) -> h p", p=P)).then_inc(small_in, 16)
            for n, g in ((G_MIX0, norm_mix), (G_FFN0, norm_ffn), (G_PLE0, norm_ple)):
                sp.dma_start(gains[:, n:n + 2, :], g.rearrange("r (p c) -> p r c", c=NC)).then_inc(small_in, 16)
            sp.dma_start(gains[:, G_KV, :], kv_norm.rearrange("(p c) -> p c", c=NC)).then_inc(small_in, 16)
            for j, src in enumerate(blocks_a):
                if j == DENSE_RING:
                    for la in range(2):
                        sp.dma_start(w_route[:, la, :, 0:GROUPS], over_d(moe_w_group[la])).then_inc(route_in, 16)
                        sp.dma_start(w_route[:, la, :, GROUPS:], over_d(moe_w_expert[la])).then_inc(route_in, 16)
                        sp.dma_start(b_route[:, la, 0:GROUPS], moe_b_group[la].partition_broadcast(P)).then_inc(route_in, 16)
                        sp.dma_start(b_route[:, la, GROUPS:], moe_b_expert[la].partition_broadcast(P)).then_inc(route_in, 16)
                if j >= DENSE_RING:
                    wait_used(sp, "a", j - DENSE_RING)
                if j == 0:
                    sp.dma_start(slot_of(("a", 0), src)[:, 0:NC // 2], src[:, 0:NC // 2]).then_inc(first_half_in, 16)
                    sp.dma_start(slot_of(("a", 0), src)[:, NC // 2:], src[:, NC // 2:]).then_inc(landed[0], 16)
                else:
                    load(("a", j), src)
            experts(0, "a", blocks_a)
            after_experts(0, "b", blocks_b)
            experts(1, "b", blocks_b)
            after_experts(1, "c", blocks_c)
            for t in range(NT):
                sp.wait_ge((fin_0, fin_1)[t], 1)
                sp.dma_start(out[0].rearrange("(t p) d -> p t d", p=P)[:, t], fin[:, t]).then_inc(out_done, 16)
            sp.wait_ge(out_done, 16 * NT)

        @block.gpsimd
        def _(pool):
            step = Count(pool, pool_step)
            for m, value in ((ident, 0.0), (ones, 1.0), (before, 1.0)):
                pool.memset(m[:], value).then_inc(pool_step, 1)
            pool.iota(iota_i[:], pattern=[[1, SLOTS]], base=1, channel_multiplier=0).then_inc(pool_step, 1)
            pool.iota(thresh_i[:], pattern=[[SLOTS, SEQ // SLOTS - 1]], base=SLOTS,
                      channel_multiplier=0).then_inc(pool_step, 1)
            for fresh, m in ((fresh_g, GROUPS), (fresh_e, EXPERTS)):
                pool.memset(fresh[:], 1.0).then_inc(pool_step, 1)
            step.n = 7
            step.link(pool.memset(causal[:], 1.0))
            pool.affine_select(out=ident[:], in_=ident[:], compare_op=ALU.not_equal, fill=1.0, base=0,
                               pattern=[[-1, P]], channel_multiplier=1).then_inc(const_ready, 1)
            pool.affine_select(out=before[:], in_=before[:], compare_op=ALU.is_gt, fill=0.0, base=0,
                               pattern=[[1, P]], channel_multiplier=-1).then_inc(const_ready, 1)
            for fresh, m in ((fresh_g, GROUPS), (fresh_e, EXPERTS)):
                pool.memset(fresh[:, m:m + 1], 0.0)
            pool.tensor_copy(iota[:], iota_i[:]).then_inc(const_ready, 1)
            pool.tensor_copy(thresh[:], thresh_i[:]).then_inc(const_ready, 1)
            step.link(pool.affine_select(out=causal[:], in_=causal[:], compare_op=ALU.is_ge, fill=0.0,
                                         base=0, pattern=[[1, P]], channel_multiplier=-1))
            pool.affine_select(out=causal[:, CHUNK:], in_=causal[:, CHUNK:], compare_op=ALU.is_ge, fill=0.0,
                               base=-CHUNK, pattern=[[0, CHUNK]], channel_multiplier=1).then_inc(const_ready, 1)
            for la in range(2):
                pool.memset(more_i[:, la:la + 1], 0).then_inc(moe_freed[la], 1)
            pool.memset(view(1024, 1536), 0.0).then_inc(zeroed, 1)
            pool.memset(view(3584, 1024), 0.0).then_inc(zeroed, 1)
            for key in dense[:BLOCKS_A - 1]:
                low(pool, key)
            pool.wait_ge(small_in, 16 * 6)
            pool.wait_ge(route_in, 16 * 8)
            for la, gain in enumerate((G_FFN0, G_FFN1)):
                pool.tensor_tensor(w_route[:, la], w_route[:, la], wide(gains[:, gain], ROUTES),
                                   ALU.mult).then_inc(wroute_ready, 1)

            def normalise(layer):
                pool.wait_ge(tr_ps, 4 * (1 + 3 * layer) + 4)
                pool.wait_ge(rstd_ready, 2 + 3 * layer)
                pool.tensor_scalar(hn[:, 0], hn[:, 0], rstd[:, 0:1], None, ALU.mult).then_inc(normed_0, 1)

            normalise(0)
            for key in dense[BLOCKS_A - 1:BLOCKS_A + 1]:
                low(pool, key)
            pool.wait_ge(sq_done, 6)
            pool.memset(bias[0:CHUNK, :, 0:CHUNK], MASKED).then_inc(bias_mask, 1)
            for key in dense[BLOCKS_A + 1:BLOCKS_A + BLOCKS_B - 2]:
                low(pool, key)
            normalise(1)
            for key in dense[BLOCKS_A + BLOCKS_B - 2:]:
                low(pool, key)

        @block.scalar
        def _(act):
            def sqrt_table(n, known):
                act.activation(spare[:, n:n + 1], known[:, 0:1], ACT.Sqrt)

            def squares(src, dump):
                for t in range(NT):
                    act.activation(dump[:, t], src[:, t], ACT.Square,
                                   accum_out=ssq[:, t:t + 1]).then_inc(sq_done, 1)

            def half_squares(j, t):
                half = slice(BANK * j, BANK * j + BANK)
                act.activation(hn[:].rearrange("p t c q -> p t (c q)")[:, t, half], xs[:, t, half], ACT.Square,
                               accum_out=(ssq_0, ssq)[j][:, t:t + 1]).then_inc(sq_done, 1)

            def roots(n):
                act.wait_ge(ms_ready, n + 1)
                act.activation(root[:], ms[:], ACT.Sqrt).then_inc(root_ready, 1)

            def load_p(layer):
                act.dma_start(p_tok, p[layer, 0].rearrange("(t q) m -> q t m", q=P)).then_inc(p_in, 16)

            def turned_high(k):
                for j in range(2):
                    for t in range(NT):
                        act.wait_ge(tr_ps, 4 * SPLIT_STAGES[k] + 2 * j + t + 1)
                        act.activation(hT_hi[:, 4 * j:4 * j + 4, P * t:P * t + P], bank3(2 * t + j, P),
                                       ACT.Copy).then_inc(hT_hi_ready, 1)

            def plain(n):
                act.activation(hn[:, 1], acc[:, 1].rearrange("p (q c) -> p c q", c=NC), ACT.Copy).then_inc(hn_ready, 1)
                act.wait_ge(hn_ready, 2 * n + 2)
                if n in SPLIT_STAGES:
                    turned_high(SPLIT_STAGES.index(n))
                    high(act, ("bc"[n // 3], 0), FIRST)
                else:
                    layer = n // 3
                    act.wait_ge(pt_ps, layer + 1)
                    act.activation(pT.rearrange("p k s -> p (k s)"), pb[:, 3, :], ACT.Copy).then_inc(pt_ready, 1)
                    for j in range(2):
                        act.wait_ge(tr_ps, 4 * n + 2 * j + 2)
                        act.activation(routeT[:, 4 * j:4 * j + 4, P:2 * P], bank3(2 + j, P),
                                       ACT.Copy).then_inc(rt_act, 1)
                sqrt_table(n, root)
                squares(hn[:].rearrange("p t c q -> p t (c q)"), dump)

            def roots(n):
                act.wait_ge(ms_ready, n + 1)
                act.activation(root[:], ms[:], ACT.Sqrt).then_inc(root_ready, 1)

            act.wait_ge(const_ready, 1)
            sqrt_table(0, ones)
            act.wait_ge(x_in, 16)
            squares(xs, hn[:].rearrange("p t c q -> p t (c q)"))
            roots(0)

            def gates_f(h):
                for b in range(2):
                    act.wait_ge(pj_ps, 8 * h + b + 1)
                    act.activation(t_key[:, BANK * b:BANK * b + BANK], pb[:, b, :], ACT.Sigmoid).then_inc(sig_done, 1)

            def decay_exps(h):
                if h == 0:
                    act.wait_ge(injected, 1)
                act.wait_ge(f_ready, h + 1)
                act.activation(t_log, t_key, ACT.Ln).then_inc(ln_done, 1)
                high(act, ("a", 4 * h + 1), REST)
                act.wait_ge(cum_ready, h + 1)
                act.activation(t_exp, t_cum, ACT.Exp).then_inc(exp_done, 1)
                act.activation(k_inv, t_cum, ACT.Exp, scale=-1.0).then_inc(exp_done, 1)
                act.wait_ge(tail_ready, h + 1)
                act.activation(t_log, t_log, ACT.Exp).then_inc(exp_done, 1)

            def values(h):
                high(act, ("a", 4 * h + 3), FIRST)
                for t in range(NT):
                    act.wait_ge(pj_ps, 8 * h + 5 + t)
                    act.activation(v_tok[:, t], pb[:, 1 + t, :], ACT.Copy).then_inc(v_ready, 1)
                high(act, ("a", 4 * h + 3), REST)
                high(act, ("a", 4 * h + 4), FIRST)
                for t in range(NT):
                    act.wait_ge(pj_ps, 8 * h + 7 + t)
                    if h:
                        act.wait_ge(o_ready, t + 1)
                    act.activation(og_tok[:, t], bank3((3, 0)[t], P), ACT.Silu).then_inc(og_ready, 1)

            def keys_tail(h):
                if h == 0:
                    act.wait_ge(zeroed, 1)

                def tail_01(nth):
                    act.wait_ge(kt_ps, 2 * h + nth)
                    act.activation(k_tail[0:64, 0], bank3(0, P)[0:64], ACT.Copy).then_inc(kt_ready, 1)
                    act.activation(k_tail[64:128, 1], bank3(0, P)[64:128], ACT.Copy).then_inc(kt_ready, 1)

                def tail_2(nth):
                    act.wait_ge(kt_ps, 2 * h + nth)
                    act.activation(k_tail[0:64, 2], bank3(1, P)[0:64], ACT.Copy).then_inc(kt_ready, 1)

                if h:
                    tail_01(1)
                    tail_2(2)
                else:
                    tail_2(1)
                    tail_01(2)

            def out_squares(h):
                act.wait_ge(ktail_ready, 2)
                for t in range(NT):
                    act.wait_ge(o_ps, 2 * h + t + 1)
                    act.activation(o_sq[:, BANK * t:BANK * t + BANK], pb[:, (3, 0)[t], :],
                                   ACT.Square).then_inc(osq_done, 1)
                act.wait_ge(oms_ready, h + 1)
                act.activation(o_small[:, 1], o_small[:, 0], ACT.Sqrt).then_inc(oroot_ready, 1)

            turned_high(0)
            high(act, ("a", 0), range(PIECES))
            act.wait_ge(lb_ready, 1)
            act.activation(lb[:, 2:4, :], lb[:, 2:4, :], ACT.Exp).then_inc(lbe, 1)
            high(act, ("a", 1), FIRST)
            gates_f(0)
            decay_exps(0)
            high(act, ("a", 2), range(PIECES))
            values(0)
            keys_tail(0)
            high(act, ("a", 4), REST)
            high(act, ("a", 5), FIRST)
            gates_f(1)
            decay_exps(1)
            high(act, ("a", 6), FIRST)
            out_squares(0)
            high(act, ("a", 6), REST)
            values(1)
            keys_tail(1)
            high(act, ("a", 8), REST)
            out_squares(1)
            high(act, ("a", 9), FIRST)
            load_p(0)
            high(act, ("a", 9), REST)

            def projected(layer, j, t):
                act.wait_ge(proj_ps, 4 * layer + 2 * j + t + 1)
                act.activation(xs[:, t, BANK * j:BANK * j + BANK], pb[:, 2 + t, :], ACT.Copy).then_inc(pp_ready, 1)

            def moe(layer):
                act.wait_ge(added, 2 * layer + 2)
                stage = 1 + 3 * layer
                plain(stage)
                roots(stage)
                act.wait_ge(rstd_ready, stage + 1)
                act.activation(hn[:, 1], hn[:, 1], ACT.Copy, scale=rstd[:, 1:2]).then_inc(normed_1, 1)
                act.wait_ge(dif_ready[layer], 1)
                for t in range(NT):
                    act.activation(g_exp[:, t], g_dif[:, t], ACT.Exp,
                                   accum_out=g_sum[:, t]).then_inc(rexp_done[layer], 1)
                projected(layer, 0, 0)
                act.wait_ge(dif_ready[layer], 2)
                act.activation(top_x, top_d, ACT.Exp).then_inc(rexp_done[layer], 1)
                projected(layer, 0, 1)
                projected(layer, 1, 0)
                projected(layer, 1, 1)
                act.wait_ge(rounds_ready[layer], 1)
                rounds = act.value_load(rounds_i[0:1, layer:layer + 1], min_val=1, max_val=8)
                with act.Fori(0, rounds) as r:
                    with act.Fori(0, BODIES) as i:
                        it = r * BODIES + i
                        for b in range(BATCHES):
                            act.wait_ge(pgt_ps[layer], it * BATCHES + (b + 1))
                            act.activation(pick_gT, pb[:, 3, 256:512], ACT.Copy).then_inc(pgt_ready[layer], 1)
                            for e in range(BATCH_E * b, BATCH_E * b + BATCH_E):
                                act.wait_ge(h_ps[layer], it * BODY_E + (e + 1))
                                act.activation(silu, pb[:, 2, 0:P], ACT.Silu).then_inc(silu_done[layer], 1)
                                act.wait_ge(hidT_ps[layer], it * BODY_E + (e + 1))
                                act.activation(hidT, pb[:, 2, 256:384], ACT.Copy).then_inc(hidT_ready[layer], 1)
                                at = SLOTS * (e % BATCH_E)
                                act.wait_ge(y_ps[layer], it * BODY_E + (e + 1))
                                for g, done in ((0, moe_freed), (1, y_act)):
                                    act.activation(y_sb[at:at + SLOTS, 256 * g:256 * g + 256],
                                                   pb[SLOTS * g:SLOTS * g + SLOTS, 3, 0:256],
                                                   ACT.Copy).then_inc(done[layer], 1)
                act.wait_ge(scat_done[layer], rounds * (BODIES * BATCHES))
                plain(2 + 3 * layer)
                roots(2 + 3 * layer)
                if layer == 0:
                    rel = b_rel_bias[0]
                    act.dma_start(bias[CHUNK:P], bass.AP(tensor=rel.tensor, offset=rel.offset,
                                  ap=[[1, CHUNK], [N_REL, B_HEADS], [1, SEQ]])).then_inc(late_in, 16)
                    act.dma_start(bias[0:CHUNK, :, CHUNK:], bass.AP(tensor=rel.tensor, offset=rel.offset,
                                  ap=[[1, CHUNK], [N_REL, B_HEADS], [1, SEQ - CHUNK]])).then_inc(late_in, 16)
                else:
                    act.dma_start(fin_gain, final_norm.partition_broadcast(P)).then_inc(late_in, 16)

            def embed(layer):
                phase = "bc"[layer]
                high(act, (phase, 0), REST)
                high(act, (phase, 1), FIRST)
                for j in range(2):
                    for t in range(NT):
                        n = 4 * layer + 2 * j + t
                        act.wait_ge(gate_ps, n + 1)
                        if j:
                            act.wait_ge(xs_ready, n - 1)
                        act.wait_ge(rstd_ready, 3 + 3 * layer)
                        act.activation(sig[:, t], pb[:, 2 * j + t, :], ACT.Sigmoid,
                                       scale=rstd[:, t:t + 1]).then_inc(sig_ready, 1)
                    if j == 0:
                        high(act, (phase, 1), REST)
                        for t in range(NT):
                            act.wait_ge(xs_ready, 4 * layer + t + 1)
                            half_squares(0, t)
                sqrt_table(3 + 3 * layer, root)
                for t in range(NT):
                    act.wait_ge(xs_ready, 4 * layer + 3 + t)
                    half_squares(1, t)
                roots(3 + 3 * layer)
                if layer == 0:
                    high(act, ("b", 2), FIRST)

            moe(0)
            embed(0)

            def qkv(n):
                h, kind = QKV[n]
                first = QKV_BANKS[n]
                for b in range(2):
                    dst = (qT[h], kT[h], v_keys)[kind]
                    dst = dst[:, b] if kind == 2 else dst[:, 2 * b:2 * b + 2].rearrange("p j t -> p (j t)")
                    act.wait_ge(qkv_ps, 2 * n + b + 1)
                    act.activation(dst, pb[:, first + b, :], ACT.Copy,
                                   scale=ATTN_SCALE if kind == 0 else 1.0).then_inc(qkv_ready, 1)

            def exps(n):
                act.wait_ge(s_ready, n + 1)
                if n >= 2:
                    act.wait_ge(pT_ps, n - 1)
                for t, (a, b) in ((1, (0, 256)), (0, (256, 384))):
                    last = act.activation(probs[n % 2][:, a:b], score[n % 2][:, a:b], ACT.Exp,
                                          bias=s_neg[:, n, t:t + 1], accum_out=s_sum[:, n, t:t + 1])
                last.then_inc(e_ready, 1)

            turned_high(2)
            def weigh(n):
                act.wait_ge(rec_ready, n + 1)
                for t, (a, b) in ((1, (0, 256)), (0, (256, 384))):
                    last = act.activation(probs[n % 2][:, a:b], probs[n % 2][:, a:b], ACT.Copy,
                                          scale=s_rec[:, n, t:t + 1])
                last.then_inc(weighed, 1)

            def softmaxes(h):
                first, end = HALF_B * h, HALF_B * h + HALF_B
                exps(first)
                exps(first + 1)
                weigh(first)
                for n in range(first + 1, end):
                    weigh(n)
                    if n + 1 < end:
                        exps(n + 1)

            high(act, ("b", 2), REST)
            for n in range(5):
                high(act, ("b", 3 + n), FIRST)
                qkv(n)
                if n < 4:
                    high(act, ("b", 3 + n), REST)
            softmaxes(0)
            high(act, ("b", 7), REST)
            high(act, ("b", 8), FIRST)
            act.wait_ge(oa_ps, 2)
            qkv(5)
            softmaxes(1)
            high(act, ("b", 8), REST)
            act.wait_ge(oa_ps, 4)
            load_p(1)
            high(act, ("b", 9), FIRST)
            high(act, ("b", 9), REST)
            moe(1)
            embed(1)
            act.wait_ge(rstd_ready, 7)
            act.wait_ge(pre_ready, 4)
            act.activation(fin[:, 1], fin[:, 1], ACT.Copy, scale=rstd[:, 1:2]).then_inc(fin_1, 1)

        @block.vector
        def _(dve):
            step = Count(dve, dve_step)

            def mean_square(n):
                dve.wait_ge(sq_done, squares_until(n))
                if n in HALVES:
                    dve.scalar_tensor_tensor(out=ms[:], in0=ssq[:], scalar=1.0 / D, in1=ms_0[:], op0=ALU.mult,
                                             op1=ALU.add).then_inc(ms_ready, 1)
                else:
                    dve.tensor_scalar(ms[:], ssq[:], 1.0 / D, EPS, ALU.mult, ALU.add).then_inc(ms_ready, 1)

            def mean_square_half(n):
                dve.wait_ge(sq_done, squares_until(n) - NT)
                step.link(dve.tensor_scalar(ms_0[:], ssq_0[:], 1.0 / D, EPS, ALU.mult, ALU.add))

            def inverse_root(n):
                dve.wait_ge(root_ready, n + 1)
                dve.reciprocal(rstd[:], root[:]).then_inc(rstd_ready, 1)
                dve.wait_ge(rstd_ready, n + 1)

            def plain(n):
                dve.tensor_copy(hn[:, 0], acc[:, 0].rearrange("p (q c) -> p c q", c=NC)).then_inc(hn_ready, 1)

            def norm(n, src):
                mean_square(n)
                inverse_root(n)
                for t in range(NT):
                    dve.tensor_scalar(hn[:, t], src[:, t].rearrange("p (q c) -> p c q", c=NC),
                                      rstd[:, t:t + 1], None, ALU.mult).then_inc(hn_ready, 1)

            def turned_low(k):
                for j in range(2):
                    for t in range(NT):
                        at = slice(4 * j, 4 * j + 4), slice(P * t, P * t + P)
                        dve.wait_ge(hT_hi_ready, 4 * k + 2 * j + t + 1)
                        dve.tensor_tensor(hT_lo[:, at[0], at[1]], bank3(2 * t + j, P),
                                          hT_hi[:, at[0], at[1]].bitcast(F32), ALU.subtract).then_inc(ht_ready, 1)

            dve.wait_ge(cols_ps, 1)
            step.link(dve.tensor_copy(cols[:], pb[:, 3, 0:3 * A_HEADS]))
            step.link(dve.tensor_tensor(lb[:, 0], cols[:, 0:A_HEADS], cols[:, A_HEADS:2 * A_HEADS], ALU.max))
            step.link(dve.tensor_tensor(lb[:, 2:4], cols[:, 0:2 * A_HEADS].rearrange("p (r h) -> p r h", r=2),
                                        lb[:, 0].unsqueeze(1).to_broadcast([P, 2, A_HEADS]), ALU.subtract))
            dve.tensor_copy(lb[:, 1], lb[:, 0]).then_inc(lb_ready, 1)
            norm(0, xs)
            dve.wait_ge(small_in, 16 * 6)
            scale(dve, ("a", 0), FIRST)
            turned_low(0)
            scale(dve, ("a", 0), REST)
            for j in range(1, 3):
                scale(dve, ("a", j))
            dve.wait_ge(lbe, 1)
            step.link(dve.tensor_tensor(lb[:, 1], lb[:, 2], lb[:, 3], ALU.add))
            step.link(dve.reciprocal(lb[:, 0], lb[:, 1]))
            step.link(dve.tensor_tensor(lb[:, 0], lb[:, 0], lb[:, 2], ALU.mult))
            step.link(dve.tensor_scalar(lb[:, 1], lb[:, 0], -1.0, 1.0, ALU.mult, ALU.add))
            dve.wait_ge(const_ready, 5)

            def forget(h):
                dve.wait_ge(sig_done, 2 * h + 2)
                for j in range(HALF_A):
                    hd = HALF_A * h + j
                    part = t_key[:, SEQ * j:SEQ * j + SEQ]
                    last = dve.tensor_scalar(part, part, lb[:, 1, hd:hd + 1], lb[:, 0, hd:hd + 1], ALU.mult, ALU.add)
                last.then_inc(f_ready, 1)

            def decays(h):
                dve.wait_ge(ln_done, h + 1)
                for n in range(HALF_A * SEQ // CHUNK):
                    part = slice(CHUNK * n, CHUNK * n + CHUNK)
                    last = dve.tensor_tensor_scan(t_cum[:, part], ones[:, 0:CHUNK], t_log[:, part], 0.0,
                                                  ALU.mult, ALU.add)
                last.then_inc(cum_ready, 1)
                dve.wait_ge(cum_ready, h + 1)
                g3 = t_cum.rearrange("p (n s) -> p n s", s=CHUNK)
                dve.tensor_tensor(t_log.rearrange("p (n s) -> p n s", s=CHUNK), wide(g3[:, :, CHUNK - 1], CHUNK),
                                  g3, ALU.subtract).then_inc(tail_ready, 1)
                step.link(dve.tensor_scalar(t_key, t_key, -1.0, 1.0, ALU.mult, ALU.add))
                dve.wait_ge(exp_done, 3 * h + 2)
                dve.tensor_tensor(k_inv, k_inv, t_key, ALU.mult).then_inc(kinv_ready, 1)
                e4 = t_exp.rearrange("p (j n s) -> p n j s", j=HALF_A, s=CHUNK)
                step.link(dve.tensor_copy(dl[:, h], e4[:, 1:3, :, CHUNK - 1]))
                dve.wait_ge(exp_done, 3 * h + 3)
                dve.tensor_tensor(t_log, t_log, t_key, ALU.mult).then_inc(ktail_ready, 1)

            def queries(h):
                for b in range(2):
                    dve.wait_ge(pj_ps, 8 * h + 3 + b)
                    dve.tensor_tensor(q_dec[h][:, 2 * b:2 * b + 2].rearrange("p j t -> p (j t)"),
                                      pb[:, (2, 3)[b] if h == 0 else (1, 2)[b], :],
                                      t_exp[:, BANK * b:BANK * b + BANK], ALU.mult).then_inc(qdec_ready, 1)

            def causal_att(h):
                if h == 0:
                    dve.wait_ge(zeroed, 2)
                mask = causal[:].bitcast(I32).unsqueeze(1).to_broadcast([P, HALF_A, P])
                for t in range(NT):
                    dve.wait_ge(at_ps, 2 * h + t + 1)
                    dve.copy_predicated(att_m[:, t], mask, bank3(2 + t, P)).then_inc(at_ready, 1)

            def chunk_states(h):
                dve.wait_ge(kv_ps, 3 * h + 1)
                dve.tensor_copy(states[:, 0], bank3(2, P)).then_inc(st_ready, 1)
                for n, b in ((1, 3), (2, 0)):
                    dve.wait_ge(st_ready, 3 * h + n)
                    step.link(dve.tensor_tensor(states[:, n], states[:, n - 1], wide(dl[:, h, n - 1], P), ALU.mult))
                    dve.wait_ge(kv_ps, 3 * h + n + 1)
                    dve.tensor_tensor(states[:, n], states[:, n], bank3(b, P), ALU.add).then_inc(st_ready, 1)

            def head_norm(h):
                dve.wait_ge(osq_done, 2 * h + 2)
                step.link(dve.tensor_reduce(o_small[:, 2], o_sq.rearrange("p (m e) -> p m e", e=P), AX, ALU.add))
                dve.tensor_scalar(o_small[:, 0], o_small[:, 2], 1.0 / P, EPS, ALU.mult, ALU.add).then_inc(oms_ready, 1)
                dve.wait_ge(oroot_ready, h + 1)
                step.link(dve.reciprocal(o_small[:, 2], o_small[:, 1]))
                for t in range(NT):
                    dve.wait_ge(og_ready, 2 * h + t + 1)
                    step.link(dve.tensor_tensor(og_tok[:, t], og_tok[:, t],
                                                wide(o_small[:, 2, 4 * t:4 * t + 4], P), ALU.mult))
                    dve.tensor_tensor(hn[:, t, HALF_A * h:HALF_A * h + HALF_A], bank3((3, 0)[t], P),
                                      og_tok[:, t], ALU.mult).then_inc(o_ready, 1)

            def mixed(h, first_bank):
                for t in range(NT):
                    dve.wait_ge(ot_ps, 2 * h + t + 1)
                    k = 4 * (h % 2)
                    hi, lo = (x_t[:, k:k + 4, P * t:P * t + P] for x_t in (hT_hi, hT_lo))
                    bank = bank3(first_bank + t, P)
                    step.link(dve.tensor_copy(hi, bank))
                    dve.tensor_tensor(lo, bank, hi.bitcast(F32), ALU.subtract).then_inc(ot_ready, 1)

            forget(0)
            decays(0)
            queries(0)
            for j in range(3, 10):
                scale(dve, ("a", j))
            causal_att(0)
            forget(1)
            chunk_states(0)
            decays(1)
            queries(1)
            head_norm(0)
            mixed(0, 1)
            causal_att(1)
            chunk_states(1)
            head_norm(1)
            mixed(1, 1)

            def first_hot(hot, v, most, eq, cum):
                m = eq.shape[2]
                step.link(dve.tensor_tensor(eq, v, most.to_broadcast([P, NT, m]), ALU.is_equal))
                step.link(dve.tensor_tensor_scan(cum.rearrange("p t m -> p (t m)"), {GROUPS: fresh_g, EXPERTS: fresh_e}[m][:],
                                                 eq.rearrange("p t m -> p (t m)"), 0.0, ALU.mult, ALU.add))
                step.link(dve.scalar_tensor_tensor(out=hot, in0=cum, scalar=1.0, in1=eq, op0=ALU.is_equal,
                                                   op1=ALU.mult))

            def moe(layer):
                dve.wait_ge(added, 2 * layer + 2)
                plain(1 + 3 * layer)
                stage = 1 + 3 * layer
                for j in range(2):
                    dve.wait_ge(tr_ps, 4 * stage + 2 * j + 1)
                    dve.tensor_copy(routeT[:, 4 * j:4 * j + 4, 0:P], bank3(j, P)).then_inc(rt_dve, 1)
                mean_square(1 + 3 * layer)
                inverse_root(1 + 3 * layer)
                dve.wait_ge(route_in, 16 * 8)
                dve.wait_ge(lg_ps[layer], 1)
                for t in range(NT):
                    last = dve.scalar_tensor_tensor(out=logit[:, t], in0=pb[:, 0, 64 * t:64 * t + ROUTES],
                                                    scalar=rstd[:, t:t + 1], in1=b_route[:, layer],
                                                    op0=ALU.mult, op1=ALU.add)
                step.link(last)
                lg, le = logit[:, :, 0:GROUPS], logit[:, :, GROUPS:]

                step.link(dve.tensor_reduce(g_max[:, :, 0], lg, AX, ALU.max))
                dve.tensor_tensor(g_dif, lg, g_max.to_broadcast([P, NT, GROUPS]), ALU.subtract).then_inc(dif_ready[layer], 1)
                first_hot(g_hot, lg, g_max, g_eq, g_cum)
                step.link(dve.tensor_scalar(g_pen, g_hot, -1.0, -MASKED, ALU.add, ALU.mult))
                for t in range(NT):
                    last = dve.tensor_tensor(e_log[:, t].rearrange("p (g e) -> p g e", g=GROUPS),
                                             le[:, t].rearrange("p (g e) -> p g e", g=GROUPS),
                                             wide(g_pen[:, t], PER_GROUP), ALU.add)
                step.link(last)
                step.link(dve.tensor_reduce(top1[:, :, 0], e_log, AX, ALU.max))
                first_hot(hot1, e_log, top1, e_eq, e_cum)
                step.link(dve.scalar_tensor_tensor(out=e_log, in0=hot1, scalar=1e5 * MASKED, in1=e_log,
                                                   op0=ALU.mult, op1=ALU.add))
                step.link(dve.tensor_reduce(top2[:, :, 0], e_log, AX, ALU.max))
                dve.tensor_tensor(top_d, top2, top1, ALU.subtract).then_inc(dif_ready[layer], 1)
                first_hot(hot2, e_log, top2, e_eq, e_cum)
                dve.tensor_tensor(chosen, hot1, hot2, ALU.add).then_inc(chosen_ready[layer], 1)
                dve.wait_ge(rexp_done[layer], NT + 1)
                step.link(dve.scalar_tensor_tensor(out=top_s, in0=top_x, scalar=1.0, in1=g_sum, op0=ALU.add,
                                                   op1=ALU.mult))
                step.link(dve.reciprocal(w_1, top_s))
                step.link(dve.tensor_tensor(w_2, w_1, top_x, ALU.mult))
                for hot, w in ((hot1, w_1), (hot2, w_2)):
                    step.link(dve.tensor_tensor(hot, hot, w.to_broadcast([P, NT, EXPERTS]), ALU.mult))
                step.link(dve.tensor_tensor(gate, hot1, hot2, ALU.add))
                dve.wait_ge(rk_ps[layer], 1)
                ranks = pb[:, 1, 0:2 * EXPERTS].rearrange("p (t e) -> p t e", t=NT)
                dve.scalar_tensor_tensor(out=rank, in0=ranks, scalar=1.0, in1=chosen, op0=ALU.add, op1=ALU.mult)
                step.link(dve.tensor_reduce(most, pb[:, 1, 2 * EXPERTS:3 * EXPERTS], AX, ALU.max))
                step.link(dve.tensor_scalar(over, thresh[:], most, None, ALU.is_lt))
                step.link(dve.tensor_reduce(n_over, over, AX, ALU.add))
                dve.tensor_copy(more_i[:, layer:layer + 1], n_over)
                dve.tensor_scalar(rounds_i[:, layer:layer + 1], n_over, 1.0, None,
                                  ALU.add).then_inc(rounds_ready[layer], 1)
                dve.wait_ge(rounds_ready[layer], 1)
                rounds = dve.value_load(rounds_i[0:1, layer:layer + 1], min_val=1, max_val=8)
                gain = gains[:, (G_FFN0, G_FFN1)[layer]]
                links = 2
                with dve.Fori(0, rounds) as r:
                    with dve.Fori(0, BODIES) as i:
                        it = r * BODIES + i
                        body = Count(dve, dve_loop[layer], r * (BODIES * links + 1) + i * links)
                        body.link(dve.tensor_copy(rank8, rank[:, :, bass.ds(i * BODY_E, BODY_E)]))
                        body.link(dve.tensor_copy(gate8, gate[:, :, bass.ds(i * BODY_E, BODY_E)]))
                        for b in range(BATCHES):
                            part = slice(BATCH_E * b, BATCH_E * b + BATCH_E)
                            for t in range(NT):
                                last = dve.tensor_tensor(
                                    pick[:, t], wide(rank8[:, t, part], SLOTS),
                                    iota[:].unsqueeze(1).to_broadcast([P, BATCH_E, SLOTS]), ALU.is_equal)
                            last.then_inc(pick_ready[layer], 1)
                            dve.wait_ge(pick_ready[layer], it * BATCHES + (b + 1))
                            for t in range(NT):
                                last = dve.tensor_tensor(pick_g[:, t], pick[:, t],
                                                         wide(gate8[:, t, part], SLOTS), ALU.mult)
                            last.then_inc(pickg_ready[layer], 1)
                            for j in range(2):
                                dve.wait_ge(xg_ps[layer], it * (2 * BATCHES) + (2 * b + j + 1))
                                dve.tensor_tensor(xg[:, 4 * j:4 * j + 4], bank3(j, P),
                                                  wide(gain[:, 4 * j:4 * j + 4], P),
                                                  ALU.mult).then_inc(xg_ready[layer], 1)
                            for e in range(BATCH_E * b, BATCH_E * b + BATCH_E):
                                dve.wait_ge(silu_done[layer], it * BODY_E + (e + 1))
                                dve.tensor_tensor(hid, silu, pb[:, 2, P:2 * P],
                                                  ALU.mult).then_inc(hid_ready[layer], 1)
                                at = SLOTS * (e % BATCH_E)
                                dve.wait_ge(y_ps[layer], it * BODY_E + (e + 1))
                                for g in range(2, COLS):
                                    last = dve.tensor_copy(y_sb[at:at + SLOTS, 256 * g:256 * g + 256],
                                                           pb[SLOTS * g:SLOTS * g + SLOTS, 3, 0:256])
                                last.then_inc(y_dve[layer], 1)
                    after = Count(dve, dve_loop[layer], (r + 1) * (BODIES * links + 1) - 1)
                    after.link(dve.tensor_scalar(rank, rank, -float(SLOTS), None, ALU.add))
                scale(dve, ("bc"[layer], 0), FIRST)
                dve.wait_ge(scat_done[layer], rounds * (BODIES * BATCHES))
                plain(2 + 3 * layer)
                turned_low(1 + 2 * layer)
                scale(dve, ("bc"[layer], 0), REST)
                scale(dve, ("bc"[layer], 1))
                mean_square(2 + 3 * layer)
                inverse_root(2 + 3 * layer)

            def embed(layer):
                dve.wait_ge(pp_ready, 4 * layer + 4)
                if layer:
                    dve.wait_ge(late_in, 48)
                for j in range(2):
                    half = slice(BANK * j, BANK * j + BANK)
                    if layer == 0:
                        scale(dve, ("b", 2 + j))
                    if j:
                        mean_square_half(3 + 3 * layer)
                    for t in range(NT):
                        n = 4 * layer + 2 * j + t
                        dve.wait_ge(sig_ready, n + 1)
                        step.link(dve.tensor_tensor(sig[:, t], sig[:, t], xs[:, t, half], ALU.mult))
                        dve.tensor_tensor(xs[:, t, half], sig[:, t], acc[:, t, half], ALU.add).then_inc(xs_ready, 1)
                    for t in range(NT if layer else 0):
                        dve.wait_ge(xs_ready, 4 * layer + 2 * j + t + 1)
                        dve.tensor_tensor(fin[:, t, half], xs[:, t, half], fin_gain[:, half],
                                          ALU.mult).then_inc(pre_ready, 1)

            moe(0)
            embed(0)
            norm(3, xs)
            turned_low(2)
            for j in range(4, 8):
                scale(dve, ("b", j))

            def scores(n):
                dve.wait_ge(s_ps, n + 1)
                if n >= 2:
                    dve.wait_ge(e_ready, n - 1)
                for t, (a, b) in ((1, (0, 256)), (0, (256, 384))):
                    last = dve.tensor_tensor_reduce(score[n % 2][:, a:b], pb[:, n % 2, a:b], bias[:, n, 0:b - a][:, ::-1],
                                                    1.0, -3.0e38, ALU.add, ALU.max, s_max[:, n, t:t + 1])
                    step.link(last)
                dve.tensor_scalar(s_neg[:, n], s_max[:, n], -1.0, None, ALU.mult).then_inc(s_ready, 1)

            def turned(n):
                dve.wait_ge(pT_ps, n + 1)
                dve.tensor_copy(probsT[n % 3], pb[:, 2, 0:384]).then_inc(pT_ready, 1)

            def reciprocals(n):
                dve.wait_ge(e_ready, n + 1)
                dve.reciprocal(s_rec[:, n], s_sum[:, n]).then_inc(rec_ready, 1)

            def attended(g):
                dve.wait_ge(oa_ps, g + 1)
                bank = pb[:, 3, :].rearrange("p (c s) -> p c s", c=2)
                if g < 2:
                    dve.tensor_copy(oT[:, 2 * g:2 * g + 2], bank).then_inc(oa_ready, 1)
                else:
                    hi, lo = (x_t[:, 2 * g:2 * g + 2] for x_t in (hT_hi, hT_lo))
                    step.link(dve.tensor_copy(hi, bank))
                    dve.tensor_tensor(lo, bank, hi.bitcast(F32), ALU.subtract).then_inc(ot_ready, 1)

            dve.wait_ge(late_in, 32)
            dve.wait_ge(bias_mask, 1)
            for h in range(2):
                first, end = HALF_B * h, HALF_B * h + HALF_B
                scores(first)
                scores(first + 1)
                reciprocals(first)
                reciprocals(first + 1)
                for n in range(first, end):
                    if n + 2 < end:
                        scores(n + 2)
                    if first < n < end - 1:
                        reciprocals(n + 1)
                    turned(n)
                    if n == first + 4:
                        attended(2 * h)
                attended(2 * h + 1)
                if h == 0:
                    dve.wait_ge(qkv_ps, 12)
                    dve.wait_ge(oa_ready, 2)
                    for c in (slice(0, 2), slice(2, 4)):
                        step.link(dve.tensor_copy(hT_hi[:, c], oT[:, c]))
                        dve.tensor_tensor(hT_lo[:, c], oT[:, c], hT_hi[:, c].bitcast(F32),
                                          ALU.subtract).then_inc(ot_ready, 1)
            moe(1)
            embed(1)
            mean_square(6)
            inverse_root(6)
            dve.wait_ge(pre_ready, 4)
            dve.tensor_scalar(fin[:, 0], fin[:, 0], rstd[:, 0:1], None, ALU.mult).then_inc(fin_0, 1)

        @block.tensor
        def _(pe):
            def inject(tiles=range(NT), first=None):
                for j in range(2):
                    for t in tiles:
                        if first is not None:
                            pe.wait_ge(xs_ready, first + 2 * j + t)
                        half = slice(BANK * j, BANK * j + BANK)
                        last = pe.matmul(acc[:, t, half], ident[:], xs[:, t, half], start=True, stop=True)
                return last

            def transposes(n, before_last=None):
                for j in range(2):
                    for t in range(NT):
                        if before_last and (j, t) == (1, NT - 1):
                            before_last()
                        pe.wait_ge(hn_ready, 2 * n + (2 if n in PLAIN else t + 1))
                        for c in range(4):
                            last = pe.transpose(pb[:, 2 * t + j, P * c:P * c + P], hn[:, t, 4 * j + c], ident[:])
                        last.then_inc(tr_ps, 1)

            def parts(key, u):
                k = PIECES * dense.index(key) + u
                pe.wait_ge(lo_ready, k + 1)
                at = k % SPLIT_BUFS
                return ((w_hi[:, at], hT_hi), (w_hi[:, at], hT_lo), (w_lo[:, at], hT_hi))

            def by_feature(key, banks, free):
                for b in range(2):
                    free(b)
                for c in range(NC):
                    three = parts(key, c)
                    for m in range(4):
                        for n, (w, x_t) in enumerate(three):
                            last = pe.matmul(pb[:, banks[m // 2], SEQ * (m % 2):SEQ * (m % 2) + SEQ],
                                             w[:, P * m:P * m + P], x_t[:, c],
                                             start=c == 0 and m % 2 == 0 and n == 0,
                                             stop=c == NC - 1 and n == 2, skip_group_check=True)
                        if c == NC - 1 and m == 1:
                            yield last
                    if c < NC - 1:
                        last.then_inc(piece_used, 1)
                yield last

            def by_token(key, banks, free):
                for t in range(NT):
                    free(t)
                for c in range(NC):
                    three = parts(key, c)
                    for t in range(NT):
                        for n, (w, x_t) in enumerate(three):
                            last = pe.matmul(pb[:, banks[t], :], x_t[:, c, P * t:P * t + P], w,
                                             start=c == 0 and n == 0, stop=c == NC - 1 and n == 2)
                        if c == NC - 1 and t == 0:
                            yield last
                    if c < NC - 1:
                        last.then_inc(piece_used, 1)
                yield last

            def add_mixed(phase, j, h, pieces=range(PIECES)):
                pe.wait_ge(ot_ready, 2 * h + 2)
                for u in pieces:
                    c, m = divmod(u, 2)
                    for w, x_t in parts((phase, j), u):
                        for t in range(NT):
                            last = pe.matmul(acc[:, t, BANK * m:BANK * m + BANK],
                                             x_t[:, 4 * (h % 2) + c, P * t:P * t + P], w,
                                             start=False, stop=True, skip_group_check=True)
                    last.then_inc(piece_used if u < PIECES - 1 else added, 1)

            def free_none(b):
                pass

            pe.wait_ge(const_ready, 1)
            pe.wait_ge(small_in, 16 * 6)
            pe.transpose(pb[:, 3, 0:3 * A_HEADS], rows[:], ident[0:3 * A_HEADS, 0:3 * A_HEADS]).then_inc(cols_ps, 1)
            pe.wait_ge(x_in, 16)
            inject(tiles=(0,))
            transposes(0)

            def project_f(h):
                def free(b):
                    if h == 0:
                        pe.wait_ge(ht_ready, 4)
                    else:
                        pe.wait_ge(kt_ready, 3)
                for last in by_feature(("a", 4 * h), (0, 1), free):
                    last.then_inc(pj_ps, 1)

            def project_q(h):
                def free(b):
                    if h and b == 0:
                        pe.wait_ge(sig_done, 4)
                    elif h:
                        pe.wait_ge(st_ready, 1)
                banks = (1, 2) if h else (2, 3)
                for last in by_feature(("a", 4 * h + 1), banks, free):
                    last.then_inc(pj_ps, 1)

            def project_v(h):
                def free(t):
                    if h == 0 and t == 0:
                        pe.wait_ge(sig_done, 2)
                    pe.wait_ge(qdec_ready, 2 * h + 1 + (t if h else 0))
                for last in by_token(("a", 4 * h + 2), (1, 2), free):
                    last.then_inc(pj_ps, 1)

            def project_og(h):
                def free(t):
                    if h == 0:
                        pe.wait_ge(qdec_ready, 2)
                    else:
                        pe.wait_ge(o_ready, t + 1)
                for last in by_token(("a", 4 * h + 3), (3, 0), free):
                    last.then_inc(pj_ps, 1)

            def tail_01(h):
                pe.wait_ge(ktail_ready, h + 1)
                pe.wait_ge(og_ready, 2 * h + 2)
                for j in range(HALF_A):
                    last = pe.transpose(pb[:, 0, P * j:P * j + P], t_log[:, SEQ * j:SEQ * j + P], ident[:])
                last.then_inc(kt_ps, 1)

            def tail_2(h):
                pe.wait_ge(ktail_ready, h + 1)
                if h:
                    pe.wait_ge(ot_ready, 1)
                else:
                    pe.wait_ge(v_ready, 1)
                for j in range(HALF_A):
                    last = pe.transpose(pb[0:64, 1, P * j:P * j + P], t_log[:, SEQ * j + P:SEQ * j + P + 64], ident[:])
                last.then_inc(kt_ps, 1)

            def attention_a(h, t):
                pe.wait_ge(kinv_ready, h + 1)
                pe.wait_ge(qdec_ready, 2 * h + 2)
                if t == 0 and h:
                    pe.wait_ge(ot_ready, 2)
                elif t == 0:
                    pe.wait_ge(v_ready, 2)
                else:
                    pe.wait_ge(og_ready, 2 * h + 1)
                for j in range(HALF_A):
                    last = pe.matmul(pb[:, 2 + t, P * j:P * j + P],
                                     k_inv[:, SEQ * j + P * t:SEQ * j + P * t + P],
                                     q_dec[h][:, j, P * t:P * t + P], start=True, stop=True)
                last.then_inc(at_ps, 1)

            def state_parts(h):
                pe.wait_ge(kt_ready, 3 * h + 3)
                pe.wait_ge(v_ready, 2 * h + 2)
                for n, b in enumerate((2, 3, 0)):
                    if n < 2:
                        pe.wait_ge(at_ready, 2 * h + n + 1)
                    elif h == 0:
                        pe.wait_ge(sig_done, 3)
                    for j in range(HALF_A):
                        last = pe.matmul(pb[:, b, P * j:P * j + P], k_tail[:, n, j],
                                         v_tok[:, n // 2, P * j:P * j + P], start=True, stop=True)
                    last.then_inc(kv_ps, 1)

            def outputs(h):
                pe.wait_ge(st_ready, 3 * h + 3)
                for t, b in ((0, 3), (1, 0)):
                    for j in range(HALF_A):
                        cut = slice(P * j, P * j + P)
                        chunks = [2 * t + u for u in range(2) if 2 * t + u > 0]
                        last = pe.matmul(pb[:, b, cut], att_m[:, t, j], v_tok[:, t, cut], start=True, stop=False,
                                         skip_group_check=True)
                        for n in chunks:
                            u = n % 2
                            last = pe.matmul(pb[64 * u:64 * u + 64, b, cut],
                                             q_dec[h][:, j, CHUNK * n:CHUNK * n + CHUNK], states[:, n - 1, j],
                                             start=False, stop=True, skip_group_check=True)
                    last.then_inc(o_ps, 1)

            def turn_mixed(h, ready, banks):
                for t in range(NT):
                    ready(t)
                    for c in range(4):
                        last = pe.transpose(pb[:, banks[t], P * c:P * c + P], hn[:, t, 4 * (h % 2) + c], ident[:])
                    last.then_inc(ot_ps, 1)

            def a_ready(h):
                def ready(t):
                    pe.wait_ge(o_ready, 2 * h + t + 1)
                    pe.wait_ge(v_ready, 3 + t)
                return ready

            project_f(0)
            inject(tiles=(1,)).then_inc(injected, 1)
            project_q(0)
            project_v(0)
            project_og(0)
            tail_2(0)
            attention_a(0, 0)
            attention_a(0, 1)
            tail_01(0)
            project_f(1)
            state_parts(0)
            project_q(1)
            outputs(0)
            project_v(1)
            project_og(1)
            turn_mixed(0, a_ready(0), (1, 2))
            tail_01(1)
            tail_2(1)
            attention_a(1, 0)
            attention_a(1, 1)
            state_parts(1)
            add_mixed("a", 8, 0, range(0, 4))
            outputs(1)
            add_mixed("a", 8, 0, range(4, 7))
            turn_mixed(1, a_ready(1), (1, 2))
            add_mixed("a", 8, 0, range(7, 8))
            add_mixed("a", 9, 1)

            def moe(layer):
                pe.wait_ge(p_in, 16 * (layer + 1))
                for k in range(D_PLE // P):
                    for t in range(NT):
                        last = pe.transpose(pb[:, 3, SEQ * k + P * t:SEQ * k + P * t + P],
                                            p_tok[:, t, P * k:P * k + P], ident[:])
                last.then_inc(pt_ps, 1)
                transposes(1 + 3 * layer, lambda: pe.wait_ge(pt_ready, layer + 1))
                pe.wait_ge(wroute_ready, 2)
                pe.wait_ge(rt_dve, 2 * layer + 1)
                for c in range(NC):
                    for t in range(NT):
                        if c % 4 == 0:
                            pe.wait_ge((rt_dve, rt_act)[t], 2 * layer + c // 4 + 1)
                        last = pe.matmul(pb[:, 0, 64 * t:64 * t + ROUTES], routeT[:, c, P * t:P * t + P],
                                         w_route[:, layer, c], start=c == 0 and t == 0, stop=c == NC - 1,
                                         skip_group_check=True)
                last.then_inc(lg_ps[layer], 1)
                key, w_src = (("a", PROJ), blocks_a[PROJ]) if layer == 0 else (("b", PROJ), blocks_b[PROJ])
                arrived(pe, key)
                w = slot_of(key, w_src)

                def embedding(j, t):
                    if j:
                        pe.wait_ge(pp_ready, 4 * layer + t + 1)
                    for k in range(D_PLE // P):
                        last = pe.matmul(pb[:, 2 + t, :], pT[:, k, P * t:P * t + P],
                                         w[:, k, BANK * j:BANK * j + BANK], start=k == 0, stop=k == 1)
                    last.then_inc(proj_ps, 1)

                embedding(0, 0)
                embedding(0, 1)
                pe.wait_ge(chosen_ready[layer], 1)
                pe.wait_ge(const_ready, 5)
                ranks = pb[:, 1]
                pe.matmul(ranks[:, 0:EXPERTS], before[:], chosen[:, 0], start=True, stop=True)
                pe.matmul(ranks[:, EXPERTS:2 * EXPERTS], ones[:], chosen[:, 0], start=True, stop=False)
                pe.matmul(ranks[:, EXPERTS:2 * EXPERTS], before[:], chosen[:, 1], start=False, stop=True)
                pe.matmul(ranks[:, 2 * EXPERTS:3 * EXPERTS], ones[:], chosen[:, 0], start=True, stop=False)
                pe.matmul(ranks[:, 2 * EXPERTS:3 * EXPERTS], ones[:], chosen[:, 1], start=False,
                          stop=True).then_inc(rk_ps[layer], 1)
                embedding(1, 0)
                embedding(1, 1)
                pe.wait_ge(normed_0, layer + 1)
                pe.wait_ge(normed_1, layer + 1)
                pe.wait_ge(rounds_ready[layer], 1)
                rounds = pe.value_load(rounds_i[0:1, layer:layer + 1], min_val=1, max_val=8)
                with pe.Fori(0, rounds) as r:
                    with pe.Fori(0, BODIES) as i:
                        it = r * BODIES + i
                        for b in range(BATCHES):
                            experts(layer, it, b)
                return rounds

            def experts(layer, it, b):
                def here(slot, k):
                    pe.wait_ge(moe_landed[layer][slot], it * (16 * BODY_BLOCKS // RING) + 16 * (k // RING + 1))

                pe.wait_ge(pick_ready[layer], it * BATCHES + (b + 1))
                for j in range(2):
                    for c in range(4):
                        for t in range(NT):
                            last = pe.matmul(pb[:, j, P * c:P * c + P], hn[:, t, 4 * j + c],
                                             pick[:, t].rearrange("p e s -> p (e s)"), start=t == 0,
                                             stop=t == NT - 1)
                    last.then_inc(xg_ps[layer], 1)
                pe.wait_ge(pp_ready, 4 * layer + 4)
                pe.wait_ge(pickg_ready[layer], it * BATCHES + (b + 1))
                for t in range(NT):
                    last = pe.transpose(pb[:, 3, 256 + P * t:256 + P * t + P],
                                        pick_g[:, t].rearrange("p e s -> p (e s)"), ident[:])
                last.then_inc(pgt_ps[layer], 1)
                for e in range(BATCH_E * b, BATCH_E * b + BATCH_E):
                    s_gate, s_up, s_down = expert_slots(e)
                    first = 3 * e % RING
                    k_of = {(first + n) % RING: 3 * e + n for n in range(3)}
                    at = SLOTS * (e % BATCH_E)
                    here(s_gate, k_of[s_gate])
                    here(s_up, k_of[s_up])
                    for c in range(NC):
                        if e % BATCH_E == 0 and c % 4 == 0:
                            pe.wait_ge(xg_ready[layer], it * (2 * BATCHES) + (2 * b + c // 4 + 1))
                        for g in range(COLS):
                            cut = BANK * c + P * g
                            last = pe.matmul(pb[SLOTS * g:SLOTS * g + SLOTS, 2, 0:256],
                                             xg[:, c, at:at + SLOTS], ring[:, s_gate:s_gate + 2, cut:cut + P],
                                             start=c == 0, stop=c == NC - 1, tile_position=(0, SLOTS * g))
                    last.then_inc(h_ps[layer], 1)
                    pe.wait_ge(hid_ready[layer], it * BODY_E + (e + 1))
                    pe.transpose(pb[:, 2, 256:384], hid, ident[:]).then_inc(hidT_ps[layer], 1)
                    pe.wait_ge(hidT_ready[layer], it * BODY_E + (e + 1))
                    here(s_down, k_of[s_down])
                    if e % BATCH_E == 0:
                        pe.wait_ge(pgt_ready[layer], it * BATCHES + (b + 1))
                    else:
                        pe.wait_ge(y_act[layer], it * BODY_E + e)
                        pe.wait_ge(y_dve[layer], it * BODY_E + e)
                    for c in range(D_EXPERT // P):
                        for g in range(COLS):
                            cut = D * c + 256 * g
                            last = pe.matmul(pb[SLOTS * g:SLOTS * g + SLOTS, 3, 0:256],
                                             hidT[:, SLOTS * c:SLOTS * c + SLOTS], ring[:, s_down, cut:cut + 256],
                                             start=c == 0, stop=c == D_EXPERT // P - 1,
                                             tile_position=(0, SLOTS * g))
                    last.then_inc(y_ps[layer], 1)
                pe.wait_ge(y_act[layer], it * BODY_E + (BATCH_E * b + BATCH_E))
                pe.wait_ge(y_dve[layer], it * BODY_E + (BATCH_E * b + BATCH_E))
                for t in range(NT):
                    for j in range(2):
                        last = pe.matmul(acc[:, t, BANK * j:BANK * j + BANK], pick_gT[:, P * t:P * t + P],
                                         y_sb[:, BANK * j:BANK * j + BANK], start=False, stop=True,
                                         skip_group_check=True)
                last.then_inc(scat_done[layer], 1)

            def embed(layer):
                stage = 2 + 3 * layer
                transposes(stage)
                pe.wait_ge(ht_ready, 4 * SPLIT_STAGES.index(stage) + 4)
                for j in range(2):
                    for last in by_token(("bc"[layer], j), (2 * j, 2 * j + 1), free_none):
                        last.then_inc(gate_ps, 1)

            moe(0)
            embed(0)
            inject(first=1)
            transposes(3)

            def project_qkv(n, free):
                kind, first = QKV[n][1], QKV_BANKS[n]
                project = by_token if kind == 2 else by_feature
                for last in project(("b", 2 + n), (first, first + 1), free):
                    last.then_inc(qkv_ps, 1)

            def after_evac(count):
                return lambda b: pe.wait_ge(qkv_ready, count + b)

            def q_k(n):
                if n >= 2:
                    pe.wait_ge(s_ready, n)
                h, j = n // HALF_B, n % HALF_B // 2
                for a, b, queries, keys in ((0, 256, slice(P, SEQ), slice(0, SEQ)), (256, 384, slice(0, P), slice(0, P))):
                    for m in range(2):
                        rows_h = slice(B_DIM * m, B_DIM * m + B_DIM)
                        last = pe.matmul(pb[:, m, a:b], qT[h][rows_h, j, queries], kT[h][rows_h, j, keys],
                                         start=True, stop=True, tile_position=(B_DIM * m, 0))
                        if b == 384:
                            last.then_inc(s_ps, 1)

            def turn_probs(n):
                pe.wait_ge(weighed, n + 1)
                if n:
                    pe.wait_ge(pT_ready, n)
                for m in range(3):
                    to = P * ((m + 1) % 3)
                    last = pe.transpose(pb[:, 2, to:to + P], probs[n % 2][:, P * m:P * m + P], ident[:])
                last.then_inc(pT_ps, 1)

            def p_v(n):
                pe.wait_ge(pT_ready, n + 2)
                if n % 4 == 0 and n:
                    if n < 12:
                        pe.wait_ge(oa_ready, n // 4)
                    else:
                        pe.wait_ge(ot_ready, 7)
                at, v_at = SEQ * (n // 2 % 2), B_DIM * (n % HALF_B)
                for tile, queries, weights in ((0, slice(at, at + SEQ), slice(0, SEQ)),
                                               (1, slice(at + P, at + SEQ), slice(SEQ, SEQ + P))):
                    for m in range(2):
                        last = pe.matmul(pb[B_DIM * m:B_DIM * m + B_DIM, 3, queries],
                                         v_keys[:, tile, v_at + B_DIM * m:v_at + B_DIM * m + B_DIM],
                                         probsT[(n + m) % 3][:, weights], start=tile == 0, stop=tile == 1,
                                         tile_position=(0, B_DIM * m), skip_group_check=True)
                if n % 4 == 2:
                    last.then_inc(oa_ps, 1)

            def heads(h, before_last=None):
                base, end = HALF_B * h, HALF_B * h + HALF_B
                for n in range(base, end, 2):
                    if n + 2 < end:
                        q_k(n + 2)
                    elif before_last:
                        before_last()
                    turn_probs(n)
                    if n > base:
                        p_v(n - 2)
                    turn_probs(n + 1)
                p_v(end - 2)

            pe.wait_ge(ht_ready, 12)
            project_qkv(0, free_none)
            project_qkv(1, free_none)
            project_qkv(2, after_evac(1))
            project_qkv(3, after_evac(3))
            project_qkv(4, after_evac(5))
            pe.wait_ge(qkv_ready, 10)
            q_k(0)

            def last_values():
                pe.wait_ge(s_ready, 8)
                project_qkv(5, free_none)

            heads(0, last_values)
            pe.wait_ge(qkv_ready, 12)
            q_k(HALF_B)
            heads(1, lambda: add_mixed("b", 8, 2, range(0, 4)))
            add_mixed("b", 8, 2, range(4, 8))
            add_mixed("b", 9, 3)
            moe(1)
            embed(1)


_INS = ['x', 'p', 'a_w_in', 'a_lb_logits', 'a_out_norm', 'a_w_o', 'kv_norm', 'w_kv', 'b_w_q', 'b_rel_bias',
        'b_w_o', 'norm_mix', 'norm_ffn', 'norm_ple', 'moe_w_group', 'moe_b_group', 'moe_w_expert',
        'moe_b_expert', 'moe_w_gate', 'moe_w_up', 'moe_w_down', 'ple_w_proj', 'ple_w_gate', 'final_norm']
_OUTS = [((1, 256, 1024), 'float32')]


def kernel(**inputs):
    import numpy as _np
    import concourse.bacc as _bacc
    from concourse import mybir as _mybir
    from concourse.bass_utils import run_bass_kernel_spmd as _run

    nc = _bacc.Bacc("TRN2", target_bir_lowering=False, num_devices=1)
    arrays, args = {}, []
    for name in _INS:
        a = _np.ascontiguousarray(inputs[name])
        arrays[f"in_{name}_dram"] = a
        args.append(nc.dram_tensor(f"in_{name}_dram", a.shape, _mybir.dt.from_np(a.dtype), kind="ExternalInput").ap())
    for i, (shape, dtype) in enumerate(_OUTS):
        dt = _mybir.dt.from_np(_np.dtype(dtype))
        args.append(nc.dram_tensor(f"out_{i}_dram", shape, dt, kind="ExternalOutput").ap())
    build(nc, *args)
    r = _run(nc, [arrays], core_ids=[0])
    got = tuple(r.results[0][f"out_{i}_dram"] for i in range(len(_OUTS)))
    return got[0]
```
